# Optimizing a Trainium2 kernel written in Bass

```python
import math
import jax, jax.numpy as jnp
from jax import lax
import numpy as np

D_MODEL = 2048
BATCH = 1
SEQ = 256
DEPTH = 2

CHUNK = 64
N_MIXERS = 3
NORM_EPS = 1e-6
NEG = -1e30

D_FF = -(-8 * D_MODEL // (3 * 256)) * 256

CONV_WIDTH = 31

MLA_HEADS = D_MODEL // 128
Q_LORA_RANK = 512
KV_LORA_RANK = 512
QK_NOPE_DIM = 128
QK_ROPE_DIM = 64
V_HEAD_DIM = 128
MLA_ROPE_THETA = 10000.0
Q_BLOCK = 128

SWA_HEAD_DIM = 64
SWA_HEADS = D_MODEL // SWA_HEAD_DIM
SWA_KV_HEADS = SWA_HEADS // 8
WINDOW = 128
WINDOW_CHUNKS = WINDOW // CHUNK
SWA_ROPE_THETA = 150000.0

N_CONV_LAYERS = len(range(0, DEPTH, N_MIXERS))
N_MLA_LAYERS = len(range(1, DEPTH, N_MIXERS))
N_SWA_LAYERS = len(range(2, DEPTH, N_MIXERS))

kernel_name = 'hybrid_chunk_causal_conv_mla_swa_encoder'

def rmsnorm(x, g):
    xf = x.astype(jnp.float32)
    y = xf * lax.rsqrt(jnp.mean(xf * xf, axis=-1, keepdims=True) + NORM_EPS)
    return (y * g.astype(jnp.float32)).astype(x.dtype)

def layernorm(x, g, b):
    xf = x.astype(jnp.float32)
    mu = jnp.mean(xf, axis=-1, keepdims=True)
    xc = xf - mu
    var = jnp.mean(xc * xc, axis=-1, keepdims=True)
    y = xc * lax.rsqrt(var + NORM_EPS) * g.astype(jnp.float32) + b.astype(jnp.float32)
    return y.astype(x.dtype)

def rope_angles(positions, dim, theta):
    inv_freq = 1.0 / (theta ** (jnp.arange(0, dim, 2, dtype=jnp.float32) / dim))
    ang = positions.astype(jnp.float32)[..., None] * inv_freq
    return jnp.cos(ang), jnp.sin(ang)

def apply_rope(x, cos, sin):
    xf = x.astype(jnp.float32)
    x1, x2 = jnp.split(xf, 2, axis=-1)
    c = cos[:, :, None, :]
    s = sin[:, :, None, :]
    return jnp.concatenate([x1 * c - x2 * s, x2 * c + x1 * s], axis=-1).astype(x.dtype)

def swiglu(h, w_gate, w_up, w_down):
    return (jax.nn.silu(h @ w_gate) * (h @ w_up)) @ w_down

def conv_module(h, w_pw1, b_pw1, w_dw, b_dw, ln_g, ln_b, w_pw2, b_pw2):
    u = h @ w_pw1 + b_pw1
    a, gate = jnp.split(u, 2, axis=-1)
    v = a * jax.nn.sigmoid(gate)
    v = lax.conv_general_dilated(
        v, w_dw[:, None, :].astype(v.dtype),
        window_strides=(1,),
        padding=[(CONV_WIDTH - 1, 0)],
        dimension_numbers=('NWC', 'WIO', 'NWC'),
        feature_group_count=D_MODEL) + b_dw
    v = jax.nn.silu(layernorm(v, ln_g, ln_b))
    return v @ w_pw2 + b_pw2

def mla(h, cos, sin, w_dq, q_norm_g, w_uq, w_dkv, kv_norm_g, w_ukv, w_o):
    B, S, _ = h.shape
    H = MLA_HEADS
    cq = rmsnorm(h @ w_dq, q_norm_g)
    q = (cq @ w_uq).reshape(B, S, H, QK_NOPE_DIM + QK_ROPE_DIM)
    q_nope = q[..., :QK_NOPE_DIM]
    q_rope = apply_rope(q[..., QK_NOPE_DIM:], cos, sin)
    ckv_full = h @ w_dkv
    ckv = rmsnorm(ckv_full[..., :KV_LORA_RANK], kv_norm_g)
    k_rope = apply_rope(ckv_full[:, :, None, KV_LORA_RANK:], cos, sin)[:, :, 0]
    kv = (ckv @ w_ukv).reshape(B, S, H, QK_NOPE_DIM + V_HEAD_DIM)
    k_nope = kv[..., :QK_NOPE_DIM]
    v = kv[..., QK_NOPE_DIM:]
    scale = (QK_NOPE_DIM + QK_ROPE_DIM) ** -0.5
    outs = []
    for qb in range(S // Q_BLOCK):
        q0 = qb * Q_BLOCK
        kend = q0 + Q_BLOCK
        s = (jnp.einsum('bqhd,bkhd->bhqk', q_nope[:, q0:kend], k_nope[:, :kend])
             + jnp.einsum('bqhr,bkr->bhqk', q_rope[:, q0:kend], k_rope[:, :kend]))
        s = s.astype(jnp.float32) * scale
        q_chunk = (q0 + jnp.arange(Q_BLOCK)) // CHUNK
        k_chunk = jnp.arange(kend) // CHUNK
        mask = k_chunk[None, :] <= q_chunk[:, None]
        s = jnp.where(mask[None, None], s, NEG)
        p = jax.nn.softmax(s, axis=-1).astype(v.dtype)
        outs.append(jnp.einsum('bhqk,bkhd->bqhd', p, v[:, :kend]))
    o = jnp.concatenate(outs, axis=1).reshape(B, S, H * V_HEAD_DIM)
    return o @ w_o

def swa_sink_attention(h, cos, sin, w_qkv, b_qkv, sinks, w_o, b_o):
    B, S, _ = h.shape
    Hq, Hk, Dh = SWA_HEADS, SWA_KV_HEADS, SWA_HEAD_DIM
    G = Hq // Hk
    nC = S // CHUNK
    WC = WINDOW_CHUNKS
    qkv = h @ w_qkv + b_qkv
    q = qkv[..., :Hq * Dh].reshape(B, S, Hq, Dh)
    k = qkv[..., Hq * Dh:(Hq + Hk) * Dh].reshape(B, S, Hk, Dh)
    v = qkv[..., (Hq + Hk) * Dh:].reshape(B, S, Hk, Dh)
    q = apply_rope(q, cos, sin)
    k = apply_rope(k, cos, sin)
    qc = q.reshape(B, nC, CHUNK, Hk, G, Dh)

    def band(t):
        tc = t.reshape(B, nC, CHUNK, Hk, Dh)
        tp = jnp.pad(tc, ((0, 0), (WC - 1, 0), (0, 0), (0, 0), (0, 0)))
        return jnp.concatenate([tp[:, j:j + nC] for j in range(WC)], axis=2)

    kb, vb = band(k), band(v)
    s = jnp.einsum('bcqkgd,bcwkd->bckgqw', qc, kb).astype(jnp.float32) * (Dh ** -0.5)
    key_chunk = jnp.arange(nC)[:, None] - (WC - 1) + jnp.arange(WINDOW)[None, :] // CHUNK
    valid = key_chunk >= 0
    s = jnp.where(valid[None, :, None, None, None, :], s, NEG)
    sink = sinks.astype(jnp.float32).reshape(1, 1, Hk, G, 1, 1)
    m = jnp.maximum(jnp.max(s, axis=-1, keepdims=True), sink)
    e = jnp.exp(s - m)
    p = e / (jnp.sum(e, axis=-1, keepdims=True) + jnp.exp(sink - m))
    o = jnp.einsum('bckgqw,bcwkd->bcqkgd', p.astype(vb.dtype), vb).reshape(B, S, Hq * Dh)
    return o @ w_o + b_o

def setup_inputs(seed: int = 0) -> dict:
    key = jax.random.key(seed)
    ks = jax.random.split(key, 40)
    f32 = jnp.float32
    D = D_MODEL

    def dense(k, shape, fan_in):
        return jax.random.normal(k, shape, f32) * (fan_in ** -0.5)

    def gain(k, shape):
        return 1.0 + 0.02 * jax.random.normal(k, shape, f32)

    def bias(k, shape):
        return 0.01 * jax.random.normal(k, shape, f32)

    x = jax.random.normal(ks[0], (BATCH, SEQ, D), f32)
    offset = jax.random.randint(ks[1], (BATCH, 1), 0, 1024, dtype=jnp.int32) * CHUNK
    positions = (offset + jnp.arange(SEQ, dtype=jnp.int32)[None, :]).astype(jnp.int32)

    nA, nB, nC_ = N_CONV_LAYERS, N_MLA_LAYERS, N_SWA_LAYERS
    mla_q_dim = MLA_HEADS * (QK_NOPE_DIM + QK_ROPE_DIM)
    mla_kv_dim = MLA_HEADS * (QK_NOPE_DIM + V_HEAD_DIM)
    swa_qkv_dim = (SWA_HEADS + 2 * SWA_KV_HEADS) * SWA_HEAD_DIM
    return {
        'x': x,
        'positions': positions,
        'attn_norm_g': gain(ks[2], (DEPTH, D)),
        'ffn_norm_g': gain(ks[3], (DEPTH, D)),
        'final_norm_g': gain(ks[4], (D,)),
        'conv_w_pw1': dense(ks[5], (nA, D, 2 * D), D),
        'conv_b_pw1': bias(ks[6], (nA, 2 * D)),
        'conv_w_dw': dense(ks[7], (nA, CONV_WIDTH, D), CONV_WIDTH),
        'conv_b_dw': bias(ks[8], (nA, D)),
        'conv_ln_g': gain(ks[9], (nA, D)),
        'conv_ln_b': bias(ks[10], (nA, D)),
        'conv_w_pw2': dense(ks[11], (nA, D, D), D),
        'conv_b_pw2': bias(ks[12], (nA, D)),
        'mla_w_dq': dense(ks[13], (nB, D, Q_LORA_RANK), D),
        'mla_q_norm_g': gain(ks[14], (nB, Q_LORA_RANK)),
        'mla_w_uq': dense(ks[15], (nB, Q_LORA_RANK, mla_q_dim), Q_LORA_RANK),
        'mla_w_dkv': dense(ks[16], (nB, D, KV_LORA_RANK + QK_ROPE_DIM), D),
        'mla_kv_norm_g': gain(ks[17], (nB, KV_LORA_RANK)),
        'mla_w_ukv': dense(ks[18], (nB, KV_LORA_RANK, mla_kv_dim), KV_LORA_RANK),
        'mla_w_o': dense(ks[19], (nB, MLA_HEADS * V_HEAD_DIM, D), MLA_HEADS * V_HEAD_DIM),
        'swa_w_qkv': dense(ks[20], (nC_, D, swa_qkv_dim), D),
        'swa_b_qkv': bias(ks[21], (nC_, swa_qkv_dim)),
        'swa_sinks': 0.5 * jax.random.normal(ks[22], (nC_, SWA_HEADS), f32),
        'swa_w_o': dense(ks[23], (nC_, SWA_HEADS * SWA_HEAD_DIM, D), SWA_HEADS * SWA_HEAD_DIM),
        'swa_b_o': bias(ks[24], (nC_, D)),
        'ffn_w_gate': dense(ks[25], (DEPTH, D, D_FF), D),
        'ffn_w_up': dense(ks[26], (DEPTH, D, D_FF), D),
        'ffn_w_down': dense(ks[27], (DEPTH, D_FF, D), D_FF),
    }

def reference(x, positions, attn_norm_g, ffn_norm_g, final_norm_g,
              conv_w_pw1, conv_b_pw1, conv_w_dw, conv_b_dw, conv_ln_g, conv_ln_b,
              conv_w_pw2, conv_b_pw2,
              mla_w_dq, mla_q_norm_g, mla_w_uq, mla_w_dkv, mla_kv_norm_g, mla_w_ukv, mla_w_o,
              swa_w_qkv, swa_b_qkv, swa_sinks, swa_w_o, swa_b_o,
              ffn_w_gate, ffn_w_up, ffn_w_down):
    cos_m, sin_m = rope_angles(positions, QK_ROPE_DIM, MLA_ROPE_THETA)
    cos_s, sin_s = rope_angles(positions, SWA_HEAD_DIM, SWA_ROPE_THETA)
    h = x
    for i in range(DEPTH):
        kind = i % N_MIXERS
        j = i // N_MIXERS
        y = rmsnorm(h, attn_norm_g[i])
        if kind == 0:
            y = conv_module(y, conv_w_pw1[j], conv_b_pw1[j], conv_w_dw[j], conv_b_dw[j],
                            conv_ln_g[j], conv_ln_b[j], conv_w_pw2[j], conv_b_pw2[j])
        elif kind == 1:
            y = mla(y, cos_m, sin_m, mla_w_dq[j], mla_q_norm_g[j], mla_w_uq[j],
                    mla_w_dkv[j], mla_kv_norm_g[j], mla_w_ukv[j], mla_w_o[j])
        else:
            y = swa_sink_attention(y, cos_s, sin_s, swa_w_qkv[j], swa_b_qkv[j],
                                   swa_sinks[j], swa_w_o[j], swa_b_o[j])
        h = h + y
        h = h + swiglu(rmsnorm(h, ffn_norm_g[i]), ffn_w_gate[i], ffn_w_up[i], ffn_w_down[i])
    return rmsnorm(h, final_norm_g)


_drawn_inputs = setup_inputs


def setup_inputs(seed=0):
    import zlib

    import numpy as np

    out = dict(_drawn_inputs(seed))
    spreads = {}
    factors = {'attn_norm_g': 3.835,
     'ffn_norm_g': 3.068,
     'final_norm_g': 2.858,
     'conv_b_pw1': 7.467,
     'conv_b_dw': 3.758,
     'conv_ln_g': 3.602,
     'conv_ln_b': 8.0,
     'conv_b_pw2': 4.744,
     'mla_q_norm_g': 8.0,
     'mla_kv_norm_g': 8.0}
    for name, (base, spread) in spreads.items():
        noise = np.random.default_rng([zlib.crc32(name.encode()), seed]).standard_normal(out[name].shape)
        drawn = base * np.exp(spread * noise) if base else spread * noise
        out[name] = __import__('jax').numpy.asarray(drawn.astype(out[name].dtype))
    for name, factor in factors.items():
        out[name] = (out[name] * factor).astype(out[name].dtype)
    return out
```

```python
from contextlib import ExitStack

import numpy as np
import concourse.bass as bass
from concourse import mybir
from concourse.alu_op_type import AluOpType as ALU

F32 = mybir.dt.float32
F32R = mybir.dt.float32r
I32 = mybir.dt.int32
ACT = mybir.ActivationFunctionType
AX = mybir.AxisListType

P = 128
D = 2048
S = 256
TT = S // P
KT = D // P
DFF = 5632
CH = 512
GK = 4
KG = KT // GK
RING = 4
EPS = 1e-6

TAPS = 31
HALO = TAPS - 1
CC = D // CH
CM = CH // P

HEADS = 16
NOPE = 128
ROPE = 64
VD = 128
LORA = 512
LT = LORA // P
QH = NOPE + ROPE
KVH = NOPE + VD
PAIRS = HEADS // 2
SM_SCALE = float(QH) ** -0.5
NEG = -1e30
FC = DFF // CH

G_PW1 = 0
G_PW2 = G_PW1 + 2 * CC * KG
G_FFN0 = G_PW2 + CC * KG
G_DQ = G_FFN0 + 3 * FC * KG
G_DKV = G_DQ + KG
G_KR = G_DKV + KG
G_ATT = G_KR + 1
G_WO = G_ATT + 2 * PAIRS
G_FFN1 = G_WO + CC * KG
G_END = G_FFN1 + 3 * FC * KG
POOL_LO = G_FFN0 + 3

R_ATTN, R_FFN, R_LNG, R_LNB, R_BDW, R_QN, R_KVN = 0, 32, 64, 80, 96, 112, 116
R_ALL = 120

PI_DIGITS = 314159265358979323846264338327950288419716939937510582097494
TWO_PI = 2 * PI_DIGITS / 10 ** 59
TURN_BITS = 12
TURN_PIECES = 5


def turn_pieces():
    q = 10 ** 59 * 2 ** (TURN_BITS * TURN_PIECES) // (2 * PI_DIGITS)
    out = []
    for j in range(TURN_PIECES):
        shift = TURN_BITS * (TURN_PIECES - 1 - j)
        out.append(float(((q >> shift) & (2 ** TURN_BITS - 1)) * 2.0 ** (shift - TURN_BITS * TURN_PIECES)))
    return out


def encoder(nc, x, positions, attn_norm_g, ffn_norm_g, final_norm_g, conv_w_pw1, conv_b_pw1, conv_w_dw,
            conv_b_dw, conv_ln_g, conv_ln_b, conv_w_pw2, conv_b_pw2, mla_w_dq, mla_q_norm_g, mla_w_uq,
            mla_w_dkv, mla_kv_norm_g, mla_w_ukv, mla_w_o, ffn_w_gate, ffn_w_up, ffn_w_down, inv_freq, out):
    ctx = ExitStack()
    with ctx:
        def sb(name, shape, dt=F32):
            return ctx.enter_context(nc.sbuf_tensor(name, shape, dt))

        def sem(name):
            return ctx.enter_context(nc.semaphore(name))

        resid = sb("resid", [P, TT, D])
        ytmp = sb("ytmp", [P, TT, D])
        x_hi = sb("x_hi", [P, KT, S], F32R)
        x_lo = sb("x_lo", [P, KT, S], F32R)
        raw = sb("raw", [P, RING, GK * CH])
        w_hi = sb("w_hi", [P, RING, GK * CH], F32R)
        w_lo = sb("w_lo", [P, RING, GK * CH], F32R)
        a_hi = sb("a_hi", [P, 2, LT, S], F32R)
        a_lo = sb("a_lo", [P, 2, LT, S], F32R)
        row_bc = sb("row_bc", [P, D])
        scratch = sb("scratch", [P, 3584])
        ident = sb("ident", [P, P])
        tap_col = sb("tap_col", [P, TAPS, KT])
        vec_col = sb("vec_col", [P, R_ALL])
        bias1_col = sb("bias1_col", [P, 2 * KT])
        mask = sb("mask", [P, 3 * P])
        cos2 = sb("cos2", [P, TT, ROPE])
        sin2 = sb("sin2", [P, TT, ROPE])
        pos_i = sb("pos_i", [P, TT], I32)
        pos_f = sb("pos_f", [P, TT])
        stat = sb("stat", [P, 2])
        rstd = sb("rstd", [P, 2])
        newton = sb("newton", [P, 2])
        bn = sb("bn", [P, TT, CC, 6])
        mv = sb("mv", [P, TT, 2])
        shift = sb("shift", [P, TT])
        nmax = sb("nmax", [P, 4])
        esum = sb("esum", [P, 4])
        erec = sb("erec", [P, 4])
        ps = ctx.enter_context(nc.psum_tensor("ps", [P, 8, 512], F32))

        conv_out = ytmp[:, :, :].rearrange("p t (m s) -> p (t m) s", s=S)
        vec_row = ytmp[0:R_ALL, 0, 0:P]
        bias1_row = ytmp[0:2 * KT, 0, P:2 * P]
        tap_row = ytmp[0:4 * TAPS, 0, 2 * P:6 * P].rearrange("p (q c) -> p q c", q=4)
        o = 0
        ang, a_top, a_low, frac, turns = [scratch[:, 64 * TT * n:64 * TT * n + 32 * TT].rearrange(
            "p (t f) -> p t f", t=TT) for n in range(5)]
        whole = scratch[:, 640:640 + 32 * TT].rearrange("p (t f) -> p t f", t=TT)
        freq = scratch[:, 768:768 + 32]
        vbuf = scratch[:, 0:CM * (S + HALO)].rearrange("p (m s) -> p m s", m=CM)
        o = CM * (S + HALO)
        acc = scratch[:, o:o + CM * S].rearrange("p (m s) -> p m s", m=CM)
        glu_sig = scratch[:, o + CM * S:o + 2 * CM * S].rearrange("p (m s) -> p m s", m=CM)
        taps = scratch[:, o + 2 * CM * S:o + 2 * CM * S + TAPS * CM].rearrange("p (w m) -> p w m", m=CM)
        z_buf, z_sig, z_act = [scratch[:, 1024 * n:1024 * n + 1024].rearrange("p (b f) -> p b f", b=2)
                               for n in range(3)]
        ff_sig = scratch[:, 0:1024].rearrange("p (t f) -> p t f", t=TT)
        ff_h = scratch[:, 1024:2048].rearrange("p (t f) -> p t f", t=TT)
        qT = scratch[:, 0:512].rearrange("p (a s) -> p a s", a=2)
        kT = scratch[:, 512:1024].rearrange("p (a s) -> p a s", a=2)
        v_sb = scratch[:, 1024:1536].rearrange("p (t f) -> p t f", t=TT)
        q_rot = scratch[:, 1536:1792].rearrange("p (t f) -> p t f", t=TT)
        qrT = scratch[:, 1792:2048]
        prob = scratch[:, 2048:2816].rearrange("p (a f) -> p a f", a=2)
        pT = scratch[:, 2816:3584].rearrange("p (a f) -> p a f", a=2)
        krT = ytmp[:, 1, 1024:1280]
        k_rot = ytmp[:, 1, 1280:1536].rearrange("p (t f) -> p t f", t=TT)
        rope_a = ytmp[:, 0, 1024:1280]
        rope_b = ytmp[:, 0, 1280:1536]
        c_q = ytmp[:, :, 0:LORA]
        c_kv = ytmp[:, :, LORA:2 * LORA]

        def hi32(ap):
            return ap.bitcast(F32)

        x_in = sem("x_in")
        small_in = sem("small_in")
        bias2_in = sem("bias2_in")
        final_g_in = sem("final_g_in")
        raw_in = [sem(f"raw_in{n}") for n in range(RING)]
        hi_done = sem("hi_done")
        lo_pool = sem("lo_pool")
        lo_dve = sem("lo_dve")
        group_used = sem("group_used")
        consts = sem("consts")
        vec_t = sem("vec_t")
        vec_done = sem("vec_done")
        chain = sem("chain")
        turn_ready = sem("turn_ready")
        rope_ready = sem("rope_ready")
        sq_act = sem("sq_act")
        rstd_ready = sem("rstd_ready")
        y_act = sem("y_act")
        y_dve = sem("y_dve")
        x_tr = sem("x_tr")
        xhi_done = sem("xhi_done")
        xlo_done = sem("xlo_done")
        glu_sig_done = sem("glu_sig_done")
        glu_done = sem("glu_done")
        conv_step = sem("conv_step")
        conv_tr = sem("conv_tr")
        z_done = sem("z_done")
        z_sig_done = sem("z_sig_done")
        z_act_done = sem("z_act_done")
        out_added = sem("out_added")
        ff_sig_done = sem("ff_sig_done")
        ff_h_done = sem("ff_h_done")
        ff_tr = sem("ff_tr")
        ahi_done = sem("ahi_done")
        alo_done = sem("alo_done")
        lat_tr = sem("lat_tr")
        kr_rot_done = sem("kr_rot_done")
        kr_tr = sem("kr_tr")
        kr_done = sem("kr_done")
        q_rot_done = sem("q_rot_done")
        qr_tr = sem("qr_tr")
        qr_done = sem("qr_done")
        qk_done = sem("qk_done")
        v_done = sem("v_done")
        scored = sem("scored")
        max_done = sem("max_done")
        exp_done = sem("exp_done")
        prob_done = sem("prob_done")
        prob_tr = sem("prob_tr")
        pT_done = sem("pT_done")
        pv_done = sem("pv_done")
        stored = sem("stored")

        def val(n0, i=None, per=0):
            return n0 if i is None else i * per + n0

        def wait_lo(eng, g, i=None, per=0):
            if g < POOL_LO:
                eng.wait_ge(lo_pool, val(g + 1, i, per))
            else:
                eng.wait_ge(lo_dve, val(g - POOL_LO + 1, i, per))

        def norm_counts(n):
            return KT * n

        block = ctx.enter_context(nc.Block())

        @block.sync
        def _(sp):
            def load(src, g, i=None, per=0, cols=CH, tiles=GK):
                slot = g % RING
                if g >= RING:
                    wait_lo(sp, g - RING, i, per)
                sp.dma_start(raw[:, slot, 0:tiles * cols].rearrange("p (k n) -> p k n", k=tiles),
                             src).then_inc(raw_in[slot], 16)

            def tile_rows(w, rows, cols):
                return w.rearrange("(k p) n -> p k n", p=P)[:, rows, cols]

            x_t = x[0].rearrange("(t p) d -> p t d", p=P)
            for t in range(TT):
                sp.dma_start(resid[:, t, :], x_t[:, t, :]).then_inc(x_in, 16)

            w1 = conv_w_pw1[0]
            def pw1_loads(c, i=None):
                base = 0 if i is None else i * CH
                for part, off in ((0, D), (1, 0)):
                    for j in range(KG):
                        load(tile_rows(w1, slice(GK * j, GK * j + GK), bass.ds(base + off + CH * c, CH)),
                             G_PW1 + 2 * KG * c + KG * part + j, i, 2 * KG)
            pw1_loads(0)
            with sp.Fori(0, CC - 1) as i:
                pw1_loads(1, i)

            def square_loads(w, g0):
                with sp.Fori(0, CC) as i:
                    for j in range(KG):
                        load(tile_rows(w, slice(GK * j, GK * j + GK), bass.ds(i * CH, CH)), g0 + j, i, KG)
            square_loads(conv_w_pw2[0], G_PW2)

            def ffn_loads(l, g0):
                wg, wu, wd = ffn_w_gate[l], ffn_w_up[l], ffn_w_down[l]

                def up(g, c, i=None, per=0):
                    base = 0 if i is None else i * CH
                    for n, w in ((0, wg), (1, wu)):
                        for j in range(KG):
                            load(tile_rows(w, slice(GK * j, GK * j + GK), bass.ds(base + CH * c, CH)),
                                 g + KG * n + j, i, per)

                def down(g, c, i=None, per=0):
                    base = 0 if i is None else i * CH
                    for n in range(CC):
                        load(wd[bass.ds(base + CH * c, CH), CH * n:CH * n + CH].rearrange("(k p) n -> p k n", p=P),
                             g + n, i, per)
                up(g0, 0)
                with sp.Fori(0, FC - 1) as i:
                    up(g0 + 2 * KG, 1, i, 3 * KG)
                    down(g0 + 4 * KG, 0, i, 3 * KG)
                down(g0 + 3 * KG * FC - KG, FC - 1)
            ffn_loads(0, G_FFN0)

            for j in range(KG):
                load(tile_rows(mla_w_dq[0], slice(GK * j, GK * j + GK), slice(0, CH)), G_DQ + j)
            for j in range(KG):
                load(tile_rows(mla_w_dkv[0], slice(GK * j, GK * j + GK), slice(0, CH)), G_DKV + j)
            load(tile_rows(mla_w_dkv[0], slice(0, KT), slice(LORA, LORA + ROPE)), G_KR, cols=ROPE, tiles=KT)

            def pair_loads(g, h, i=None, per=0, step=0):
                base = 0 if i is None else i * step
                load(tile_rows(mla_w_uq[0], slice(0, LT), bass.ds(base * (2 * QH) + 2 * QH * h, 2 * QH)),
                     g, i, per, cols=2 * QH)
                load(tile_rows(mla_w_ukv[0], slice(0, LT), bass.ds(base * (2 * KVH) + 2 * KVH * h, 2 * KVH)),
                     g + 1, i, per)
            pair_loads(G_ATT, 0)
            with sp.Fori(0, (PAIRS - 2) // 2) as i:
                for u in range(2):
                    pair_loads(G_ATT + 2 + 2 * u, 1 + u, i, 4, 2)
            pair_loads(G_ATT + 2 * (PAIRS - 1), PAIRS - 1)
            square_loads(mla_w_o[0], G_WO)
            ffn_loads(1, G_FFN1)

            for t in range(TT):
                sp.wait_ge(y_dve, 6 + CC + t + 1)
                sp.dma_start(out[0].rearrange("(t p) d -> p t d", p=P)[:, t, :], ytmp[:, t, :]).then_inc(stored, 16)
            sp.wait_ge(stored, 16 * TT)

        @block.gpsimd
        def _(pool):
            pool.memset(ident[:, :], 0.0).then_inc(consts, 1)
            pool.wait_ge(consts, 1)
            pool.affine_select(out=ident[:, :], in_=ident[:, :], compare_op=ALU.not_equal, fill=1.0, base=0,
                               pattern=[[-1, P]], channel_multiplier=1).then_inc(consts, 1)
            pool.memset(mask[:, :], 0.0).then_inc(consts, 1)
            pool.wait_ge(consts, 3)
            pool.memset(mask[0:64, 64:128], NEG).then_inc(consts, 1)
            pool.memset(mask[0:64, 320:384], NEG).then_inc(consts, 1)

            def lo(g, i=None, per=0):
                pool.wait_ge(hi_done, val(g + 1, i, per))
                pool.tensor_tensor(w_lo[:, g % RING, :], raw[:, g % RING, :], hi32(w_hi[:, g % RING, :]),
                                   ALU.subtract).then_inc(lo_pool, 1)
            for g in range(RING):
                lo(g)
            pool.wait_ge(bias2_in, 16)
            pool.wait_ge(y_act, 1)
            pool.wait_ge(y_dve, 1)
            for t in range(TT):
                pool.tensor_tensor(resid[:, t, :], resid[:, t, :], row_bc[:, :], ALU.add).then_inc(out_added, 1)
            with pool.Fori(0, G_PW2 // RING) as i:
                for g in range(RING):
                    lo(RING + g, i, RING)
            for b in range(KT // 2):
                pool.wait_ge(xhi_done, norm_counts(1) + 2 * b + 2)
                pool.tensor_tensor(x_lo[:, 2 * b:2 * b + 2, :].rearrange("p k s -> p (k s)"), z_act[:, b % 2, :],
                                   hi32(x_hi[:, 2 * b:2 * b + 2, :]).rearrange("p k s -> p (k s)"),
                                   ALU.subtract).then_inc(xlo_done, 2)
            with pool.Fori(0, CC - 1) as i:
                for g in range(RING):
                    lo(G_PW2 + RING + g, i, RING)
            for g in range(G_FFN0, POOL_LO):
                lo(g)

        @block.scalar
        def _(act):
            def rows(v):
                return v.rearrange("(t p) -> t p", p=P)

            loads = [(vec_row[R_ATTN:R_ATTN + 32, :], attn_norm_g.rearrange("l (t p) -> (l t) p", p=P)),
                     (vec_row[R_FFN:R_FFN + 32, :], ffn_norm_g.rearrange("l (t p) -> (l t) p", p=P)),
                     (vec_row[R_LNG:R_LNG + KT, :], rows(conv_ln_g[0])), (vec_row[R_LNB:R_LNB + KT, :], rows(conv_ln_b[0])),
                     (vec_row[R_BDW:R_BDW + KT, :], rows(conv_b_dw[0])), (vec_row[R_QN:R_QN + LT, :], rows(mla_q_norm_g[0])),
                     (vec_row[R_KVN:R_KVN + LT, :], rows(mla_kv_norm_g[0])), (bias1_row, rows(conv_b_pw1[0])),
                     (tap_row, conv_w_dw[0].rearrange("w (t p) -> (w t) p", p=P).rearrange("(q r) p -> r q p", q=4)),
                     (freq, inv_freq[0:1, :].to_broadcast([P, ROPE // 2]))]
            for dst, src in loads:
                act.dma_start(dst, src).then_inc(small_in, 16)
            with nc.allow_non_contiguous_dma(reason="256 positions, one per partition"):
                act.dma_start(pos_i[:, :], positions[0].rearrange("(t p) -> p t", p=P)).then_inc(small_in, 16)
            act.dma_start(row_bc[:, :], conv_b_pw2[0:1, :].to_broadcast([P, D])).then_inc(bias2_in, 16)

            def hi(g, i=None, per=0):
                slot = g % RING
                act.wait_ge(raw_in[slot], val(16 * (g // RING + 1), i, 16 * per // RING))
                if g >= RING:
                    act.wait_ge(group_used, val(g - RING + 1, i, per))
                act.activation(w_hi[:, slot, :], raw[:, slot, :], ACT.Copy).then_inc(hi_done, 1)

            def norm(n, nth, gain):
                if nth == 0:
                    act.wait_ge(x_in, 16 * TT)
                    act.wait_ge(vec_done, 3)
                else:
                    act.wait_ge(out_added, ADDED[n])
                act.activation(ytmp[:, 0, :], resid[:, 0, :], ACT.Square, accum_out=stat[:, 0:1]).then_inc(sq_act, 1)
                act.wait_ge(rstd_ready, RSTD[n])
                act.activation(ytmp[:, 0, :], resid[:, 0, :], ACT.Copy, scale=rstd[:, 0:1]).then_inc(y_act, 1)
                for k in range(KT):
                    if k % 2 == 0:
                        act.wait_ge(x_tr, XT[n] + k // 2 + 1)
                    act.activation(x_hi[:, k, :], ps[:, k // 2, S * (k % 2):S * (k % 2) + S], ACT.Copy,
                                   scale=vec_col[:, gain + k:gain + k + 1]).then_inc(xhi_done, 1)

            for g in range(2):
                hi(g)
            norm(0, 0, R_ATTN)
            for g in range(2, 4):
                hi(g)
            def gate_sigmoid(c, i=None):
                for j in range(KG):
                    hi(G_PW1 + 2 * KG * c + 4 + j, i, 2 * KG)
                act.wait_ge(group_used, val(G_PW1 + 2 * KG * c + KG, i, 2 * KG))
                if i is not None:
                    act.wait_ge(glu_done, val(CM + 1, i, CM + 1))
                for m in range(CM):
                    col = CM * c + KT + m if i is None else i * CM + CM * c + KT + m
                    act.activation(glu_sig[:, m, :], ps[:, m // 2, S * (m % 2):S * (m % 2) + S], ACT.Sigmoid,
                                   bias=bias1_col[:, bass.ds(col, 1)]).then_inc(glu_sig_done, 1)
                for j in range(KG):
                    hi(G_PW1 + 2 * KG * c + 8 + j, i, 2 * KG)
            gate_sigmoid(0)
            with act.Fori(0, CC - 1) as i:
                gate_sigmoid(1, i)

            act.wait_ge(rstd_ready, 2)
            for c in range(CC):
                act.activation(ytmp[:, 0, CH * c:CH * c + CH], ps[:, TT * c, :], ACT.Identity,
                               bias=shift[:, 0:1], scale=rstd[:, 0:1]).then_inc(y_act, 1)
            for b in range(KT // 2):
                act.wait_ge(z_done, 2 * b + 2)
                act.activation(z_sig[:, b % 2, :], z_buf[:, b % 2, :], ACT.Sigmoid).then_inc(z_sig_done, 1)
                act.wait_ge(z_act_done, b + 1)
                act.activation(x_hi[:, 2 * b:2 * b + 2, :].rearrange("p k s -> p (k s)"), z_act[:, b % 2, :],
                               ACT.Copy).then_inc(xhi_done, 2)

            def square(g0, have4=False):
                if have4:
                    for j in range(3):
                        hi(g0 + 4 + j)
                    with act.Fori(0, CC - 1) as i:
                        for j in range(KG):
                            hi(g0 + 7 + j, i, KG)
                else:
                    with act.Fori(0, CC) as i:
                        for j in range(KG):
                            hi(g0 + 3 + j, i, KG)

            square(G_PW2, have4=True)

            def ffn(l, g0):
                hi(g0 + 3)

                def gate_sig(i=None):
                    for t in range(TT):
                        act.wait_ge(group_used, val(g0 + (KG if i is None else 3 * KG), i, 3 * KG))
                        act.activation(ff_sig[:, t, :], ps[:, t, :], ACT.Sigmoid).then_inc(ff_sig_done, 1)

                def hidden(c0, i=None):
                    for b in range(2):
                        act.wait_ge(ff_tr, val(2 * (FC * l + c0) + b + 1, i, 2))
                        act.activation(a_hi[:, 0, 2 * b:2 * b + 2, :].rearrange("p k s -> p (k s)"), ps[:, 4 + b, :],
                                       ACT.Copy).then_inc(ahi_done, 1)
                for j in range(4, 8):
                    hi(g0 + j)
                gate_sig()
                for j in range(8, 12):
                    hi(g0 + j)
                with act.Fori(0, FC - 1) as i:
                    for j in range(12, 15):
                        hi(g0 + j, i, 12)
                    hidden(0, i)
                    for t in range(TT):
                        act.wait_ge(group_used, val(g0 + 12, i, 12))
                        act.activation(ff_sig[:, t, :], ps[:, t, :], ACT.Sigmoid).then_inc(ff_sig_done, 1)
                    for j in range(15, 24):
                        hi(g0 + j, i, 12)
                hidden(FC - 1)
                for j in range(3):
                    if g0 + 3 * KG * FC + j < G_END:
                        hi(g0 + 3 * KG * FC + j)

            norm(2, 1, R_FFN)
            ffn(0, G_FFN0)

            norm(3, 2, R_ATTN + KT)
            for g in (3, 4, 5, 6):
                hi(G_DQ + g)

            def latent(which, bank, gain):
                dst = c_q if which == 0 else c_kv
                act.activation(dst[:, 0, :], ps[:, bank, :], ACT.Square, accum_out=stat[:, 0:1]).then_inc(sq_act, 1)
                act.wait_ge(rstd_ready, 5 + which)
                act.activation(dst[:, 0, :], ps[:, bank, :], ACT.Copy, scale=rstd[:, 0:1]).then_inc(y_act, 1)

            def latent_hi(which, bank, gain):
                for k in range(LT):
                    if k % 2 == 0:
                        act.wait_ge(lat_tr, 2 * which + k // 2 + 1)
                    act.activation(a_hi[:, which, k, :], ps[:, bank + k // 2, S * (k % 2):S * (k % 2) + S], ACT.Copy,
                                   scale=vec_col[:, gain + k:gain + k + 1]).then_inc(ahi_done, 1)
            act.wait_ge(group_used, G_DQ + KG)
            latent(0, 0, R_QN)
            for g in (7, 8, 9, 10):
                hi(G_DQ + g)
            act.wait_ge(turn_ready, 4)
            act.activation(cos2[:, :, :], cos2[:, :, :], ACT.Sin).then_inc(rope_ready, 1)
            act.activation(sin2[:, :, :], sin2[:, :, :], ACT.Sin).then_inc(rope_ready, 1)
            act.wait_ge(group_used, G_DKV + KG)
            latent(1, 2, R_KVN)
            latent_hi(0, 5, R_QN)
            hi(G_DQ + 11)
            latent_hi(1, 0, R_KVN)

            def pair_project(g, h, i=None):
                hi(g + 3, i, 4)
                act.wait_ge(group_used, val(g + 1, i, 4))
                act.activation(qT.rearrange("p a s -> p (a s)"), ps[:, 0, :], ACT.Copy).then_inc(qk_done, 1)
                hi(g + 4, i, 4)
                act.wait_ge(group_used, val(g + 2, i, 4))
                act.activation(kT.rearrange("p a s -> p (a s)"), ps[:, 2, :], ACT.Copy).then_inc(qk_done, 1)

            def pair_out(h, i=None):
                for a in range(2):
                    act.wait_ge(prob_tr, val(2 * h + a + 1, i, 4))
                    act.activation(pT[:, a, :], ps[:, 6 + a, 0:3 * P], ACT.Copy).then_inc(pT_done, 1)
                for a in range(2):
                    act.wait_ge(pv_done, val(2 * h + a + 1, i, 4))
                    dst = x_hi[:, 2 * h + a, :] if i is None else \
                        x_hi[:, bass.ds(i * 4 + 2 * h + a, 1), :].rearrange("p k s -> p (k s)")
                    act.activation(dst, ps[:, 6 + a, 0:S], ACT.Copy).then_inc(xhi_done, 1)

            def pair_exp(h, i=None):
                for a in range(2):
                    for q, (lo_, hi_) in enumerate(((0, P), (P, 3 * P))):
                        act.wait_ge(max_done, val(4 * h + 2 * a + q + 1, i, 8))
                        act.activation(prob[:, a, lo_:hi_], prob[:, a, lo_:hi_], ACT.Exp,
                                       bias=nmax[:, 2 * a + q:2 * a + q + 1],
                                       accum_out=esum[:, 2 * a + q:2 * a + q + 1]).then_inc(exp_done, 1)

            pair_project(G_ATT, 0)
            pair_exp(0)
            with act.Fori(0, (PAIRS - 2) // 2) as i:
                for u in range(2):
                    pair_project(G_ATT + 2 + 2 * u, 1 + u, i)
                    pair_out(u, i)
                    pair_exp(1 + u, i)
            pair_project(G_ATT + 2 * (PAIRS - 1), PAIRS - 1)
            pair_out(PAIRS - 2)
            pair_exp(PAIRS - 1)
            pair_out(PAIRS - 1)

            square(G_WO)
            norm(5, 3, R_FFN + KT)
            ffn(1, G_FFN1)

            act.wait_ge(out_added, TT)
            act.dma_start(row_bc[:, :], final_norm_g.rearrange("(a d) -> a d", a=1).to_broadcast([P, D])).then_inc(final_g_in, 16)
            act.wait_ge(out_added, ADDED[6])
            act.activation(ytmp[:, 0, :], resid[:, 0, :], ACT.Square, accum_out=stat[:, 0:1]).then_inc(sq_act, 1)

        @block.vector
        def _(dve):
            links = [0]

            def link(ins):
                links[0] += 1
                ins.then_inc(chain, 1)
                dve.wait_ge(chain, links[0])

            def lo(g, i=None, per=0):
                dve.wait_ge(hi_done, val(g + 1, i, per))
                dve.tensor_tensor(w_lo[:, g % RING, :], raw[:, g % RING, :], hi32(w_hi[:, g % RING, :]),
                                  ALU.subtract).then_inc(lo_dve, 1)

            def inv_sqrt():
                link(dve.tensor_scalar(newton[:, :].bitcast(I32), stat[:, :].bitcast(I32), 1, None, ALU.logical_shift_right))
                link(dve.tensor_scalar(rstd[:, :].bitcast(I32), newton[:, :].bitcast(I32), -1.0, float(0x5F3759DF),
                                       ALU.mult, ALU.add))
                for step in range(4):
                    link(dve.tensor_tensor(newton[:, :], rstd[:, :], rstd[:, :], ALU.mult))
                    link(dve.tensor_tensor(newton[:, :], newton[:, :], stat[:, :], ALU.mult))
                    link(dve.tensor_scalar(newton[:, :], newton[:, :], -0.5, 1.5, ALU.mult, ALU.add))
                    last = dve.tensor_tensor(rstd[:, :], rstd[:, :], newton[:, :], ALU.mult)
                    if step < 3:
                        link(last)
                return last

            def mean_square(n, width):
                dve.wait_ge(sq_act, n)
                link(dve.tensor_scalar(stat[:, :], stat[:, :], 1.0 / width, EPS, ALU.mult, ALU.add))

            def norm(n, nth, gain):
                if nth:
                    dve.wait_ge(out_added, ADDED[n])
                link(dve.tensor_tensor_reduce(out=ytmp[:, 1, :], in0=resid[:, 1, :], in1=resid[:, 1, :], scale=1.0,
                                              scalar=0.0, op0=ALU.mult, op1=ALU.add, accum_out=stat[:, 1:2]))
                mean_square(SQ[n], D)
                inv_sqrt().then_inc(rstd_ready, 1)
                dve.wait_ge(rstd_ready, RSTD[n])
                dve.tensor_scalar(ytmp[:, 1, :], resid[:, 1, :], rstd[:, 1:2], None, ALU.mult).then_inc(y_dve, 1)
                for k in range(KT):
                    if k % 2 == 0:
                        dve.wait_ge(xhi_done, norm_counts(n) + k + 2)
                    dve.scalar_tensor_tensor(x_lo[:, k, :], ps[:, k // 2, S * (k % 2):S * (k % 2) + S],
                                             vec_col[:, gain + k:gain + k + 1], hi32(x_hi[:, k, :]),
                                             ALU.mult, ALU.subtract).then_inc(xlo_done, 1)

            dve.wait_ge(vec_t, 1)
            dve.tensor_copy(vec_col[:, :], ps[:, 0, 0:R_ALL]).then_inc(vec_done, 1)
            dve.tensor_copy(bias1_col[:, :], ps[:, 0, P:P + 2 * KT]).then_inc(vec_done, 1)
            dve.tensor_copy(tap_col[:, :, :].rearrange("p w t -> p (w t)"), ps[:, 1, 0:TAPS * KT]).then_inc(vec_done, 1)

            dve.wait_ge(x_in, 16 * TT)
            dve.wait_ge(vec_done, 3)
            norm(0, 0, R_ATTN)

            link(dve.tensor_copy(pos_f[:, :], pos_i[:, :]))
            for t in range(TT):
                link(dve.tensor_scalar(ang[:, t, :], freq, pos_f[:, t:t + 1], None, ALU.mult))
            link(dve.tensor_scalar(a_top.bitcast(I32), ang.bitcast(I32), -4096, None, ALU.bitwise_and))
            link(dve.tensor_tensor(a_low, ang, a_top, ALU.subtract))
            link(dve.memset(turns, 0.0))
            for piece in reversed(turn_pieces()):
                for part in (a_low, a_top):
                    link(dve.tensor_scalar(whole.bitcast(I32), part, piece, None, ALU.mult))
                    link(dve.scalar_tensor_tensor(frac, part, piece, whole.bitcast(I32), ALU.mult, ALU.subtract))
                    link(dve.tensor_tensor(turns, turns, frac, ALU.add))
            magic = 1.5 * 2.0 ** 23
            for quarter, dst in ((0.25, cos2), (0.0, sin2)):
                link(dve.tensor_scalar(frac, turns, quarter, None, ALU.add))
                link(dve.tensor_scalar(whole, frac, magic, magic, ALU.add, ALU.subtract))
                link(dve.tensor_tensor(frac, frac, whole, ALU.subtract))
                link(dve.tensor_scalar(frac, frac, TWO_PI, None, ALU.mult))
                for half in range(2):
                    dve.tensor_scalar(dst[:, :, 32 * half:32 * half + 32], frac, 3.1415925, -3.1415925,
                                      ALU.min, ALU.max).then_inc(turn_ready, 1)
                dve.wait_ge(turn_ready, 2 if dst is cos2 else 4)
            dve.memset(vbuf[:, :, 0:HALO], 0.0).then_inc(conv_step, 1)

            with dve.Fori(0, CC) as c:
                dve.wait_ge(conv_step, val(1, c, CM * TAPS))
                dve.tensor_copy(taps, tap_col[:, :, bass.ds(c * CM, CM)]).then_inc(glu_done, 1)
                for m in range(CM):
                    if m == 0:
                        dve.wait_ge(group_used, val(G_PW1 + 2 * KG, c, 2 * KG))
                    dve.wait_ge(glu_sig_done, val(m + 1, c, CM))
                    dve.scalar_tensor_tensor(vbuf[:, m, HALO:], ps[:, 2 + m // 2, S * (m % 2):S * (m % 2) + S],
                                             bias1_col[:, bass.ds(c * CM + m, 1)], glu_sig[:, m, :],
                                             ALU.add, ALU.mult).then_inc(glu_done, 1)
                for w in range(TAPS):
                    for m in range(CM):
                        n = CM * w + m
                        if w == 0:
                            dve.wait_ge(glu_done, val(m + 2, c, CM + 1))
                            dve.tensor_scalar(acc[:, m, :], vbuf[:, m, 0:S], taps[:, 0, m:m + 1],
                                              vec_col[:, bass.ds(c * CM + R_BDW + m, 1)],
                                              ALU.mult, ALU.add).then_inc(conv_step, 1)
                            continue
                        dve.wait_ge(conv_step, val(n - CM + 2, c, CM * TAPS))
                        dst = acc[:, m, :] if w < TAPS - 1 else \
                            conv_out[:, bass.ds(c * CM + m, 1), :].rearrange("p k s -> p (k s)")
                        dve.scalar_tensor_tensor(dst, vbuf[:, m, w:w + S], taps[:, w, m:m + 1], acc[:, m, :],
                                                 ALU.mult, ALU.add).then_inc(conv_step, 1)

            for c in range(CC):
                for t in range(TT):
                    dve.wait_ge(conv_tr, TT * c + t + 1)
                    last = dve.bn_stats(bn[:, t, c, :], ps[:, TT * c + t, :])
            link(last)
            for t in range(TT):
                link(dve.bn_aggr(mv[:, t, :], bn[:, t, :, :].rearrange("p c s -> p (c s)")))
            link(dve.tensor_scalar(stat[:, :], mv[:, :, 1], EPS, None, ALU.add))
            link(inv_sqrt())
            dve.scalar_tensor_tensor(shift[:, :], mv[:, :, 0], -1.0, rstd[:, :], ALU.mult, ALU.mult).then_inc(rstd_ready, 1)
            for c in range(CC):
                dve.tensor_scalar(ytmp[:, 1, CH * c:CH * c + CH], ps[:, TT * c + 1, :], mv[:, 1, 0:1], rstd[:, 1:2],
                                  ALU.subtract, ALU.mult).then_inc(y_dve, 1)
            for b in range(KT // 2):
                dve.wait_ge(x_tr, XT[1] + b + 1)
                if b >= 2:
                    dve.wait_ge(z_act_done, b - 1)
                for kk in range(2):
                    k = 2 * b + kk
                    dve.tensor_scalar(z_buf[:, b % 2, S * kk:S * kk + S], ps[:, b, S * kk:S * kk + S],
                                      vec_col[:, R_LNG + k:R_LNG + k + 1], vec_col[:, R_LNB + k:R_LNB + k + 1],
                                      ALU.mult, ALU.add).then_inc(z_done, 1)
                dve.wait_ge(z_sig_done, b + 1)
                if b >= 2:
                    dve.wait_ge(xlo_done, norm_counts(1) + 2 * b - 2)
                dve.tensor_tensor(z_act[:, b % 2, :], z_buf[:, b % 2, :], z_sig[:, b % 2, :],
                                  ALU.mult).then_inc(z_act_done, 1)

            def square(g0, split=True):
                with dve.Fori(0, CC // 2) as i:
                    for n in range(2):
                        for j in range(KG if split else 0):
                            lo(g0 + 3 + KG * n + j, i, 2 * KG)
                        for t in range(TT):
                            dve.wait_ge(group_used, val(g0 + KG * n + KG, i, 2 * KG))
                            cols = bass.ds(i * (2 * CH) + CH * n, CH)
                            dve.tensor_tensor(resid[:, t, cols], resid[:, t, cols], ps[:, 2 * n + t, :],
                                              ALU.add).then_inc(out_added, 1)

            dve.wait_ge(out_added, TT)
            square(G_PW2, split=False)

            def ffn(l, g0, added):
                def hidden(c0, i=None):
                    for b in range(2):
                        dve.wait_ge(ahi_done, val(AHI[l] + 2 * c0 + b + 1, i, 2))
                        dve.tensor_tensor(a_lo[:, 0, 2 * b:2 * b + 2, :].rearrange("p k s -> p (k s)"), ps[:, 4 + b, :],
                                          hi32(a_hi[:, 0, 2 * b:2 * b + 2, :]).rearrange("p k s -> p (k s)"),
                                          ALU.subtract).then_inc(alo_done, 1)

                def gate_mul(c0, i=None):
                    for t in range(TT):
                        dve.wait_ge(ff_sig_done, val(2 * (FC * l + c0) + t + 1, i, 2))
                        dve.tensor_tensor(ff_h[:, t, :], ps[:, t, :], ff_sig[:, t, :], ALU.mult).then_inc(ff_h_done, 1)

                def up_mul(c0, used, i=None):
                    for t in range(TT):
                        dve.wait_ge(group_used, val(used, i, 12))
                        dve.wait_ge(ff_h_done, val(4 * (FC * l + c0) + t + 1, i, 4))
                        dve.tensor_tensor(ff_h[:, t, :], ff_h[:, t, :], ps[:, 2 + t, :], ALU.mult).then_inc(ff_h_done, 1)

                def add(n, used, i=None):
                    for t in range(TT):
                        dve.wait_ge(group_used, val(used, i, 12))
                        cols = slice(CH * n, CH * n + CH)
                        dve.tensor_tensor(resid[:, t, cols], resid[:, t, cols], ps[:, 4 + (2 * n + t) % 4, :],
                                          ALU.add).then_inc(out_added, 1)
                lo(g0 + 3)
                for j in range(4, 8):
                    lo(g0 + j)
                gate_mul(0)
                for j in range(8, 11):
                    lo(g0 + j)
                up_mul(0, g0 + 8)
                lo(g0 + 11)
                with dve.Fori(0, FC - 1) as i:
                    for j in range(12, 15):
                        lo(g0 + j, i, 12)
                    hidden(0, i)
                    gate_mul(1, i)
                    for j in range(15, 19):
                        lo(g0 + j, i, 12)
                    up_mul(1, g0 + 16, i)
                    lo(g0 + 19, i, 12)
                    for n in range(CC):
                        lo(g0 + 20 + n, i, 12)
                        add(n, g0 + 17 + n, i)
                hidden(FC - 1)
                end = g0 + 3 * KG * FC
                for n in range(CC):
                    if n < 3 and end + n < G_END:
                        lo(end + n)
                    add(n, end - KG + n + 1)

            norm(2, 1, R_FFN)
            ffn(0, G_FFN0, 0)

            norm(3, 2, R_ATTN + KT)
            for g in (3, 4, 5, 6):
                lo(G_DQ + g)

            def latent(which, bank):
                dst = c_q if which == 0 else c_kv
                link(dve.tensor_copy(dst[:, 1, :], ps[:, bank + 1, :]))
                link(dve.tensor_tensor_reduce(out=rope_scr, in0=dst[:, 1, :], in1=dst[:, 1, :], scale=1.0,
                                              scalar=0.0, op0=ALU.mult, op1=ALU.add, accum_out=stat[:, 1:2]))
                mean_square(4 + which, LORA)
                inv_sqrt().then_inc(rstd_ready, 1)
                dve.wait_ge(rstd_ready, 5 + which)
                dve.tensor_scalar(dst[:, 1, :], dst[:, 1, :], rstd[:, 1:2], None, ALU.mult).then_inc(y_dve, 1)

            def latent_lo(which, bank, gain):
                for k in range(LT):
                    if k % 2 == 0:
                        dve.wait_ge(ahi_done, 2 * FC + LT * which + k + 2)
                    dve.scalar_tensor_tensor(a_lo[:, which, k, :], ps[:, bank + k // 2, S * (k % 2):S * (k % 2) + S],
                                             vec_col[:, gain + k:gain + k + 1], hi32(a_hi[:, which, k, :]),
                                             ALU.mult, ALU.subtract).then_inc(alo_done, 1)

            def rotate(src, dst, n, cos_bc, sin_bc):
                link(dve.tensor_tensor(rope_a4(n), src, cos_bc, ALU.mult))
                link(dve.tensor_tensor(rope_b4(n), src, sin_bc, ALU.mult))
                half = ROPE // 2
                link(dve.tensor_tensor(dst[..., 0:half], rope_a4(n)[..., 0:half], rope_b4(n)[..., half:ROPE], ALU.subtract))
                return dve.tensor_tensor(dst[..., half:ROPE], rope_a4(n)[..., half:ROPE], rope_b4(n)[..., 0:half], ALU.add)

            rope_scr = ytmp[:, 0, 1536:2048]

            def rope_a4(n):
                return rope_a[:, 0:TT * n * ROPE].rearrange("p (t h r) -> p t h r", t=TT, h=n)

            def rope_b4(n):
                return rope_b[:, 0:TT * n * ROPE].rearrange("p (t h r) -> p t h r", t=TT, h=n)

            def table(tab, n):
                return tab[:, :, :].rearrange("p t (h r) -> p t h r", h=1).to_broadcast([P, TT, n, ROPE])

            dve.wait_ge(group_used, G_DQ + KG)
            latent(0, 0)
            for g in (7, 8, 9, 10):
                lo(G_DQ + g)
            dve.wait_ge(group_used, G_DKV + KG)
            latent(1, 2)
            latent_lo(0, 5, R_QN)
            lo(G_DQ + 11)
            dve.wait_ge(rope_ready, 2)
            dve.wait_ge(group_used, G_KR + 1)
            kr4 = k_rot.rearrange("p t (h r) -> p t h r", h=2)
            link(rotate(ps[:, 4, 0:TT * ROPE].rearrange("p (t h r) -> p t h r", t=TT, h=1), kr4[:, :, 0:1, :], 1,
                        table(cos2, 1), table(sin2, 1)))
            dve.tensor_copy(kr4[:, :, 1:2, :], kr4[:, :, 0:1, :]).then_inc(kr_rot_done, 1)
            latent_lo(1, 0, R_KVN)
            dve.wait_ge(kr_tr, 1)
            dve.tensor_copy(krT, ps[:, 7, 0:S]).then_inc(kr_done, 1)

            rot_links = [0]

            def pair_project(g, h, i=None):
                lo(g + 3, i, 4)
                dve.wait_ge(group_used, val(g + 1, i, 4))
                src = ps[:, 1, 0:S].rearrange("p (t h r) -> p t h r", t=TT, h=2)
                a4, b4, d4 = rope_a4(2), rope_b4(2), q_rot.rearrange("p t (h r) -> p t h r", h=2)
                half = ROPE // 2
                dve.tensor_tensor(a4, src, table(cos2, 2), ALU.mult).then_inc(q_rot_done, 1)
                dve.tensor_tensor(b4, src, table(sin2, 2), ALU.mult).then_inc(q_rot_done, 1)
                dve.wait_ge(q_rot_done, val(4 * h + 2, i, 8))
                dve.tensor_tensor(d4[..., 0:half], a4[..., 0:half], b4[..., half:ROPE], ALU.subtract).then_inc(q_rot_done, 1)
                dve.tensor_tensor(d4[..., half:ROPE], a4[..., half:ROPE], b4[..., 0:half], ALU.add).then_inc(q_rot_done, 1)
                lo(g + 4, i, 4)

            def pair_out(h, i=None):
                for a in range(2):
                    dve.wait_ge(xhi_done, val(norm_counts(4) + 2 * h + a + 1, i, 4))
                    dst, high = (x_lo[:, 2 * h + a, :], x_hi[:, 2 * h + a, :]) if i is None else \
                        (x_lo[:, bass.ds(i * 4 + 2 * h + a, 1), :].rearrange("p k s -> p (k s)"),
                         x_hi[:, bass.ds(i * 4 + 2 * h + a, 1), :].rearrange("p k s -> p (k s)"))
                    dve.tensor_tensor(dst, ps[:, 6 + a, 0:S], hi32(high), ALU.subtract).then_inc(xlo_done, 1)

            def pair_keys(g, h, i=None):
                dve.wait_ge(group_used, val(g + 2, i, 4))
                dve.tensor_copy(v_sb.rearrange("p t f -> p (t f)"), ps[:, 3, :]).then_inc(v_done, 1)
                dve.wait_ge(qr_tr, val(h + 1, i, 2))
                dve.tensor_copy(qrT, ps[:, 1, S:2 * S]).then_inc(qr_done, 1)

            def pair_softmax(h, i=None):
                for a in range(2):
                    dve.wait_ge(scored, val(2 * h + a + 1, i, 4))
                    dve.scalar_tensor_tensor(prob[:, a, :], ps[:, 4 + a, 0:3 * P], SM_SCALE, mask[:, :],
                                             ALU.mult, ALU.add).then_inc(prob_done, 1)
                    for q, (lo_, hi_) in enumerate(((0, P), (P, 3 * P))):
                        dve.wait_ge(prob_done, val(7 * h + a + 1, i, 14))
                        dve.tensor_reduce(nmax[:, 2 * a + q:2 * a + q + 1], prob[:, a, lo_:hi_], AX.X, ALU.max,
                                          negate=True).then_inc(max_done, 1)
                dve.wait_ge(exp_done, val(4 * h + 4, i, 8))
                dve.reciprocal(erec[:, :], esum[:, :]).then_inc(prob_done, 1)
                dve.wait_ge(prob_done, val(7 * h + 3, i, 14))
                for a in range(2):
                    for q, (lo_, hi_) in enumerate(((0, P), (P, 3 * P))):
                        dve.tensor_scalar(prob[:, a, lo_:hi_], prob[:, a, lo_:hi_], erec[:, 2 * a + q:2 * a + q + 1],
                                          None, ALU.mult).then_inc(prob_done, 1)

            pair_project(G_ATT, 0)
            pair_keys(G_ATT, 0)
            pair_softmax(0)
            with dve.Fori(0, (PAIRS - 2) // 2) as i:
                for u in range(2):
                    g = G_ATT + 2 + 2 * u
                    pair_project(g, 1 + u, i)
                    pair_out(u, i)
                    pair_keys(g, 1 + u, i)
                    pair_softmax(1 + u, i)
            g = G_ATT + 2 * (PAIRS - 1)
            pair_project(g, PAIRS - 1)
            pair_out(PAIRS - 2)
            pair_keys(g, PAIRS - 1)
            pair_softmax(PAIRS - 1)
            pair_out(PAIRS - 1)

            square(G_WO)
            norm(5, 3, R_FFN + KT)
            ffn(1, G_FFN1, 0)

            dve.wait_ge(out_added, ADDED[6])
            link(dve.tensor_tensor_reduce(out=ytmp[:, 1, :], in0=resid[:, 1, :], in1=resid[:, 1, :], scale=1.0,
                                          scalar=0.0, op0=ALU.mult, op1=ALU.add, accum_out=stat[:, 1:2]))
            mean_square(7, D)
            link(inv_sqrt())
            dve.wait_ge(final_g_in, 16)
            for t in range(TT):
                dve.scalar_tensor_tensor(ytmp[:, t, :], resid[:, t, :], rstd[:, t:t + 1], row_bc[:, :],
                                         ALU.mult, ALU.mult).then_inc(y_dve, 1)

        @block.tensor
        def _(pe):
            def w_rows(tensor, slot, cols=CH):
                return tensor[:, slot, 0:(GK * CH // cols) * cols].rearrange("p (k n) -> p k n", n=cols)

            def product(dst, pairs, first, last, skip=False):
                for n, (lhsT, rhs) in enumerate(pairs):
                    ins = pe.matmul(dst, lhsT, rhs, start=first and n == 0, stop=last and n == len(pairs) - 1,
                                    skip_group_check=skip)
                return ins

            def three(a_h, a_l, b_h, b_l):
                return [(a_h, b_h), (a_h, b_l), (a_l, b_h)]

            def token_group(g, i, per, j, banks, xh, xl, kt0, n_groups, waits=None):
                wait_lo(pe, g, i, per)
                slot = g % RING
                wh, wl = w_rows(w_hi, slot), w_rows(w_lo, slot)
                for kk in range(GK):
                    for t in range(TT):
                        k = kt0 + kk
                        ins = product(ps[:, banks[t], :],
                                      three(xh[:, k, P * t:P * t + P], xl[:, k, P * t:P * t + P], wh[:, kk, :], wl[:, kk, :]),
                                      j == 0 and kk == 0, j == n_groups - 1 and kk == GK - 1)
                ins.then_inc(group_used, 1)

            def transposes(n):
                for b in range(KT // 2):
                    for kk in range(2):
                        for t in range(TT):
                            ins = pe.transpose(ps[:, b, S * kk + P * t:S * kk + P * t + P],
                                               ytmp[:, t, P * (2 * b + kk):P * (2 * b + kk) + P], ident[:, :])
                    ins.then_inc(x_tr, 1)

            pe.wait_ge(small_in, 16 * 11)
            pe.wait_ge(consts, 2)
            pe.transpose(ps[:, 0, 0:R_ALL], vec_row, ident[0:R_ALL, 0:R_ALL])
            pe.transpose(ps[:, 0, P:P + 2 * KT], bias1_row, ident[0:2 * KT, 0:2 * KT])
            for q in range(4):
                ins = pe.transpose(ps[:, 1, 4 * TAPS * q:4 * TAPS * q + 4 * TAPS], tap_row[:, q, :],
                                   ident[0:4 * TAPS, 0:4 * TAPS])
            ins.then_inc(vec_t, 1)

            pe.wait_ge(y_act, 1)
            pe.wait_ge(y_dve, 1)
            transposes(0)

            def channel_group(g, i, j, bank0, first):
                wait_lo(pe, g, i, 2 * KG)
                slot = g % RING
                wh, wl = w_rows(w_hi, slot), w_rows(w_lo, slot)
                if first:
                    pe.wait_ge(xlo_done, GK * (j + 1))
                for kk in range(GK):
                    k = GK * j + kk
                    for m in range(CM):
                        cols = slice(P * m, P * m + P)
                        ins = product(ps[:, bank0 + m // 2, S * (m % 2):S * (m % 2) + S],
                                      [(wh[:, kk, cols], x_hi[:, k, :]), (wh[:, kk, cols], x_lo[:, k, :]),
                                       (wl[:, kk, cols], x_hi[:, k, :])],
                                      j == 0 and kk == 0 and m % 2 == 0, j == KG - 1 and kk == GK - 1, skip=True)
                ins.then_inc(group_used, 1)

            def channel_chunk(c, i=None):
                for j in range(KG):
                    if i is not None and j == 0:
                        pe.wait_ge(glu_sig_done, val(CM, i, CM))
                    channel_group(G_PW1 + 2 * KG * c + j, i, j, 0, i is None)
                for j in range(KG):
                    if i is not None and j == 0:
                        pe.wait_ge(glu_done, val(CM + 1, i, CM + 1))
                    channel_group(G_PW1 + 2 * KG * c + KG + j, i, j, 2, False)
            channel_chunk(0)
            with pe.Fori(0, CC - 1) as i:
                channel_chunk(1, i)

            pe.wait_ge(glu_done, (CM + 1) * CC)
            for c in range(CC):
                pe.wait_ge(conv_step, CM * TAPS * (c + 1) + 1)
                for t in range(TT):
                    for m in range(CM):
                        ins = pe.transpose(ps[:, TT * c + t, P * m:P * m + P],
                                           conv_out[:, CM * c + m, P * t:P * t + P], ident[:, :])
                    ins.then_inc(conv_tr, 1)
            pe.wait_ge(y_act, 1 + CC)
            pe.wait_ge(y_dve, 1 + CC)
            transposes(1)

            def square(g0, x_count, added):
                with pe.Fori(0, CC // 2) as i:
                    for n in range(2):
                        for j in range(KG):
                            pe.wait_ge(xlo_done, x_count + GK * (j + 1))
                            if j == 0:
                                pe.wait_ge(out_added, val(added - 1 + n, i, 2 * TT))
                            token_group(g0 + KG * n + j, i, 2 * KG, j, (2 * n, 2 * n + 1), x_hi, x_lo, GK * j, KG)
            square(G_PW2, norm_counts(1), TT)

            def ffn(l, g0, x_count, added):
                def half(g, c0, i, part):
                    for j in range(KG):
                        if i is None and part == 0:
                            pe.wait_ge(xlo_done, x_count + GK * (j + 1))
                        token_group(g + j, i, 12, j, (2 * part, 2 * part + 1), x_hi, x_lo, GK * j, KG)

                def hidden(c0, i=None):
                    pe.wait_ge(ff_h_done, val(4 * (FC * l + c0) + 4, i, 4))
                    for b in range(2):
                        pe.wait_ge(out_added, val(added + TT * CC * (c0 - 1) + 5 + b, i, TT * CC))
                        for kk in range(2):
                            for t in range(TT):
                                m = 2 * b + kk
                                ins = pe.transpose(ps[:, 4 + b, S * kk + P * t:S * kk + P * t + P],
                                                   ff_h[:, t, P * m:P * m + P], ident[:, :])
                        ins.then_inc(ff_tr, 1)

                def down(g, c0, i=None):
                    pe.wait_ge(alo_done, val(AHI[l] + 2 * c0 + 2, i, 2))
                    for n in range(CC):
                        wait_lo(pe, g + n, i, 12)
                        slot = (g + n) % RING
                        wh, wl = w_rows(w_hi, slot), w_rows(w_lo, slot)
                        for t in range(TT):
                            block_no = 2 * n + t
                            if block_no >= 2:
                                pe.wait_ge(out_added, val(added + TT * CC * c0 + block_no - 3, i, TT * CC))
                            for kk in range(LT):
                                ins = product(ps[:, 4 + block_no % 4, :],
                                              three(a_hi[:, 0, kk, P * t:P * t + P], a_lo[:, 0, kk, P * t:P * t + P],
                                                    wh[:, kk, :], wl[:, kk, :]), kk == 0, kk == LT - 1)
                        ins.then_inc(group_used, 1)

                half(g0, 0, None, 0)
                half(g0 + KG, 0, None, 1)
                with pe.Fori(0, FC - 1) as i:
                    pe.wait_ge(ff_h_done, val(4 * FC * l + 4, i, 4))
                    half(g0 + 8, 0, i, 0)
                    hidden(0, i)
                    half(g0 + 12, 0, i, 1)
                    down(g0 + 16, 0, i)
                hidden(FC - 1)
                down(g0 + 3 * KG * FC - KG, FC - 1)

            pe.wait_ge(y_act, 2 + CC)
            pe.wait_ge(y_dve, 2 + CC)
            transposes(2)
            ffn(0, G_FFN0, norm_counts(2), ADDED[2])

            pe.wait_ge(y_act, 3 + CC)
            pe.wait_ge(y_dve, 3 + CC)
            transposes(3)
            for j in range(KG):
                pe.wait_ge(xlo_done, norm_counts(3) + GK * (j + 1))
                token_group(G_DQ + j, None, 0, j, (0, 1), x_hi, x_lo, GK * j, KG)
            for j in range(KG):
                token_group(G_DKV + j, None, 0, j, (2, 3), x_hi, x_lo, GK * j, KG)

            def latent_transposes(src, bank):
                for b in range(2):
                    for kk in range(2):
                        for t in range(TT):
                            k = 2 * b + kk
                            ins = pe.transpose(ps[:, bank + b, S * kk + P * t:S * kk + P * t + P],
                                               src[:, t, P * k:P * k + P], ident[:, :])
                    ins.then_inc(lat_tr, 1)
            pe.wait_ge(y_act, 4 + CC)
            pe.wait_ge(y_dve, 4 + CC)
            latent_transposes(c_q, 5)
            wait_lo(pe, G_KR)
            wh, wl = w_rows(w_hi, G_KR % RING, ROPE), w_rows(w_lo, G_KR % RING, ROPE)
            for t in range(TT):
                for k in range(KT):
                    ins = product(ps[:, 4, ROPE * t:ROPE * t + ROPE],
                                  three(x_hi[:, k, P * t:P * t + P], x_lo[:, k, P * t:P * t + P], wh[:, k, :], wl[:, k, :]),
                                  k == 0, k == KT - 1)
            ins.then_inc(group_used, 1)
            pe.wait_ge(y_act, 5 + CC)
            pe.wait_ge(y_dve, 5 + CC)
            latent_transposes(c_kv, 0)
            pe.wait_ge(kr_rot_done, 1)
            for t in range(TT):
                ins = pe.transpose(ps[:, 7, P * t:P * t + P], k_rot[:, t, :], ident[:, :])
            ins.then_inc(kr_tr, 1)

            def pair_project(g, h, i=None):
                if h == 0 and i is None:
                    pe.wait_ge(alo_done, 2 * FC + 2 * LT)
                wait_lo(pe, g, i, 4)
                wh, wl = w_rows(w_hi, g % RING, 2 * QH), w_rows(w_lo, g % RING, 2 * QH)
                for a in range(2):
                    for k in range(LT):
                        cols = slice(QH * a, QH * a + NOPE)
                        product(ps[:, 0, S * a:S * a + S],
                                [(wh[:, k, cols], a_hi[:, 0, k, :]), (wh[:, k, cols], a_lo[:, 0, k, :]),
                                 (wl[:, k, cols], a_hi[:, 0, k, :])], k == 0, k == LT - 1)
                for t in range(TT):
                    for k in range(LT):
                        def both(w):
                            return w[:, k, :].rearrange("p (a n) -> p a n", a=2)[:, :, NOPE:QH]
                        toks = slice(P * t, P * t + P)
                        ins = product(ps[:, 1, P * t:P * t + P].rearrange("p (a n) -> p a n", a=2),
                                      three(a_hi[:, 0, k, toks], a_lo[:, 0, k, toks], both(wh), both(wl)),
                                      k == 0, k == LT - 1)
                ins.then_inc(group_used, 1)
                g += 1
                wait_lo(pe, g, i, 4)
                wh, wl = w_rows(w_hi, g % RING), w_rows(w_lo, g % RING)
                for a in range(2):
                    for k in range(LT):
                        cols = slice(KVH * a, KVH * a + NOPE)
                        product(ps[:, 2, S * a:S * a + S],
                                [(wh[:, k, cols], a_hi[:, 1, k, :]), (wh[:, k, cols], a_lo[:, 1, k, :]),
                                 (wl[:, k, cols], a_hi[:, 1, k, :])], k == 0, k == LT - 1)
                if not (h == 0 and i is None):
                    pe.wait_ge(v_done, val(h, i, 2))
                for t in range(TT):
                    for k in range(LT):
                        def values(w):
                            return w[:, k, :].rearrange("p (a n) -> p a n", a=2)[:, :, NOPE:KVH]
                        toks = slice(P * t, P * t + P)
                        ins = product(ps[:, 3, S * t:S * t + S].rearrange("p (a n) -> p a n", a=2),
                                      three(a_hi[:, 1, k, toks], a_lo[:, 1, k, toks], values(wh), values(wl)),
                                      k == 0, k == LT - 1)
                ins.then_inc(group_used, 1)

            def pair_out(h, i=None):
                pe.wait_ge(prob_done, val(7 * h + 7, i, 14))
                for a in range(2):
                    if not (h == 0 and i is None):
                        base = norm_counts(4) + 2 * h - 2 + a + 1
                        pe.wait_ge(xlo_done, val(base, i, 4))
                    for s in range(3):
                        ins = pe.transpose(ps[:, 6 + a, P * s:P * s + P], prob[:, a, KEYS[s]], ident[:, :])
                    ins.then_inc(prob_tr, 1)
                for a in range(2):
                    pe.wait_ge(pT_done, val(2 * h + a + 1, i, 4))
                    pe.matmul(ps[:, 6 + a, 0:S], v_sb[:, 0, VD * a:VD * a + VD], pT[:, a, 0:S], start=True, stop=False)
                    pe.matmul(ps[:, 6 + a, P:S], v_sb[:, 1, VD * a:VD * a + VD], pT[:, a, S:S + P], start=False,
                              stop=True).then_inc(pv_done, 1)

            def pair_scores(h, i=None):
                pe.wait_ge(q_rot_done, val(4 * h + 4, i, 8))
                for t in range(TT):
                    ins = pe.transpose(ps[:, 1, S + P * t:S + P * t + P], q_rot[:, t, :], ident[:, :])
                ins.then_inc(qr_tr, 1)
                pe.wait_ge(qk_done, val(2 * h + 2, i, 4))
                pe.wait_ge(qr_done, val(h + 1, i, 2))
                if h == 0 and i is None:
                    pe.wait_ge(kr_done, 1)
                for a in range(2):
                    r = slice(ROPE * a, ROPE * a + ROPE)
                    for q, cols in enumerate((slice(0, P), slice(P, 3 * P))):
                        toks = slice(P * q, P * q + P)
                        keys = P * (q + 1)
                        pe.matmul(ps[:, 4 + a, cols], qT[:, a, toks], kT[:, a, 0:keys], start=True, stop=False)
                        ins = pe.matmul(ps[:, 4 + a, cols], qrT[r, toks], krT[r, 0:keys], start=False, stop=True)
                    ins.then_inc(scored, 1)

            KEYS = (slice(0, P), slice(P, 2 * P), slice(2 * P, 3 * P))
            pair_project(G_ATT, 0)
            pair_scores(0)
            with pe.Fori(0, (PAIRS - 2) // 2) as i:
                for u in range(2):
                    pair_project(G_ATT + 2 + 2 * u, 1 + u, i)
                    pair_out(u, i)
                    pair_scores(1 + u, i)
            pair_project(G_ATT + 2 * (PAIRS - 1), PAIRS - 1)
            pair_out(PAIRS - 2)
            pair_scores(PAIRS - 1)
            pair_out(PAIRS - 1)

            square(G_WO, norm_counts(4), ADDED[3])
            pe.wait_ge(y_act, 6 + CC)
            pe.wait_ge(y_dve, 6 + CC)
            transposes(5)
            ffn(1, G_FFN1, norm_counts(5), ADDED[5])


ADDED = {2: TT + TT * CC, 3: TT + TT * CC * (1 + FC), 5: TT + TT * CC * (2 + FC), 6: TT + TT * CC * (2 + 2 * FC)}
XT = {0: 0, 1: KT // 2, 2: KT, 3: 3 * KT // 2, 5: 2 * KT}
RSTD = {0: 1, 2: 3, 3: 4, 5: 7}
SQ = {0: 1, 2: 2, 3: 3, 5: 6}
AHI = {0: 0, 1: 2 * FC + 2 * LT}

_INS = ['x', 'positions', 'attn_norm_g', 'ffn_norm_g', 'final_norm_g', 'conv_w_pw1', 'conv_b_pw1', 'conv_w_dw',
        'conv_b_dw', 'conv_ln_g', 'conv_ln_b', 'conv_w_pw2', 'conv_b_pw2', 'mla_w_dq', 'mla_q_norm_g', 'mla_w_uq',
        'mla_w_dkv', 'mla_kv_norm_g', 'mla_w_ukv', 'mla_w_o', 'ffn_w_gate', 'ffn_w_up', 'ffn_w_down']


def kernel(**inputs):
    import concourse.bacc as _bacc
    from concourse.bass_utils import run_bass_kernel_spmd as _run

    nc = _bacc.Bacc("TRN2", target_bir_lowering=False, num_devices=1)
    arrays, args = {}, []
    named = [(name, np.ascontiguousarray(inputs[name])) for name in _INS]
    power = np.arange(0, ROPE, 2, dtype=np.float32) / np.float32(ROPE)
    freqs = np.float32(1) / (10000.0 ** power.astype(np.float64)).astype(np.float32)
    named.append(("inv_freq", freqs.reshape(1, ROPE // 2)))
    for name, a in named:
        arrays[f"in_{name}_dram"] = a
        args.append(nc.dram_tensor(f"in_{name}_dram", a.shape, mybir.dt.from_np(a.dtype), kind="ExternalInput").ap())
    args.append(nc.dram_tensor("out_0_dram", (1, S, D), F32, kind="ExternalOutput").ap())
    encoder(nc, *args)
    r = _run(nc, [arrays], core_ids=[0])
    return r.results[0]["out_0_dram"]
```

```python
from contextlib import ExitStack

import numpy as np
import concourse.bass as bass
from concourse import mybir
from concourse.alu_op_type import AluOpType as ALU

F32 = mybir.dt.float32
F32R = mybir.dt.float32r
I32 = mybir.dt.int32
ACT = mybir.ActivationFunctionType
AX = mybir.AxisListType

P = 128
D = 2048
S = 256
TT = S // P
KT = D // P
DFF = 5632
CH = 512
GK = 4
KG = KT // GK
RING = 4
LANDED = 32
EPS = 1e-6

TAPS = 31
HALO = TAPS - 1
CC = D // CH
CM = CH // P
HALVES = 2 * CC
PE_TAPS = 3
PE_TAPS_LAST = 13
DVE_STEPS = 2 * (TAPS - PE_TAPS)

HEADS = 16
NOPE = 128
ROPE = 64
VD = 128
LORA = 512
LT = LORA // P
QH = NOPE + ROPE
KVH = NOPE + VD
PAIRS = HEADS // 2
SM_SCALE = float(QH) ** -0.5
NEG = -1e30
FC = DFF // CH

G_PW1 = 0
G_PW2 = G_PW1 + 2 * CC * KG
G_FFN0 = G_PW2 + CC * KG
G_DQ = G_FFN0 + 3 * FC * KG
G_DKV = G_DQ + KG
G_KR = G_DKV + KG
G_ATT = G_KR + 1
G_WO = G_ATT + 2 * PAIRS
G_FFN1 = G_WO + CC * KG
G_END = G_FFN1 + 3 * FC * KG
POOL_LO = G_FFN0 + 3

R_ATTN, R_FFN, R_LNG, R_LNB, R_BDW, R_QN, R_KVN = 0, 32, 64, 80, 96, 112, 116
R_ALL = 120

PI_DIGITS = 314159265358979323846264338327950288419716939937510582097494
TWO_PI = 2 * PI_DIGITS / 10 ** 59
TURN_BITS = 12
TURN_PIECES = 5


def turn_pieces():
    q = 10 ** 59 * 2 ** (TURN_BITS * TURN_PIECES) // (2 * PI_DIGITS)
    out = []
    for j in range(TURN_PIECES):
        shift = TURN_BITS * (TURN_PIECES - 1 - j)
        out.append(float(((q >> shift) & (2 ** TURN_BITS - 1)) * 2.0 ** (shift - TURN_BITS * TURN_PIECES)))
    return out


def encoder(nc, x, positions, attn_norm_g, ffn_norm_g, final_norm_g, conv_w_pw1, conv_b_pw1, conv_w_dw,
            conv_b_dw, conv_ln_g, conv_ln_b, conv_w_pw2, conv_b_pw2, mla_w_dq, mla_q_norm_g, mla_w_uq,
            mla_w_dkv, mla_kv_norm_g, mla_w_ukv, mla_w_o, ffn_w_gate, ffn_w_up, ffn_w_down, inv_freq, out):
    ctx = ExitStack()
    with ctx:
        def sb(name, shape, dt=F32):
            return ctx.enter_context(nc.sbuf_tensor(name, shape, dt))

        def sem(name):
            return ctx.enter_context(nc.semaphore(name))

        resid = sb("resid", [P, TT, D])
        ytmp = sb("ytmp", [P, TT, D])
        x_hi = sb("x_hi", [P, KT, S], F32R)
        x_lo = sb("x_lo", [P, KT, S], F32R)
        raw = sb("raw", [P, RING, GK * CH])
        w_hi = sb("w_hi", [P, RING, GK * CH], F32R)
        w_lo = sb("w_lo", [P, RING, GK * CH], F32R)
        a_hi = sb("a_hi", [P, 2, LT, S], F32R)
        a_lo = sb("a_lo", [P, 2, LT, S], F32R)
        row_bc = sb("row_bc", [P, D])
        diag_more = sb("diag_more", [P, PE_TAPS_LAST - PE_TAPS - 2 * TT, P])
        scratch = sb("scratch", [P, 3584])
        ident = sb("ident", [P, P])
        tap_col = sb("tap_col", [P, TAPS, KT])
        vec_col = sb("vec_col", [P, R_ALL])
        bias1_col = sb("bias1_col", [P, 2 * KT])
        mask = sb("mask", [P, 3 * P])
        rlat = sb("rlat", [P, 2])
        rcomb = sb("rcomb", [P, 2])
        ssq = sb("ssq", [P, TT, CC])
        cos2 = sb("cos2", [P, TT, ROPE])
        sin2 = sb("sin2", [P, TT, ROPE])
        freq = sb("freq", [P, ROPE // 2])
        pos_i = sb("pos_i", [P, TT], I32)
        pos_f = sb("pos_f", [P, TT])
        stat = sb("stat", [P, 2])
        rstd = sb("rstd", [P, 2])
        newton = sb("newton", [P, 2])
        bn = sb("bn", [P, TT, HALVES, 6])
        mv = sb("mv", [P, TT, 2])
        shift = sb("shift", [P, TT])
        nmax = sb("nmax", [P, 4])
        esum = sb("esum", [P, 4])
        erec = sb("erec", [P, 4])
        ps = ctx.enter_context(nc.psum_tensor("ps", [P, 8, 512], F32))

        vec_row = scratch[0:R_ALL, 1024:1024 + P]
        bias1_row = scratch[0:2 * KT, 1024 + P:1024 + 2 * P]
        tap_row = scratch[0:4 * TAPS, 1024 + 2 * P:1024 + 6 * P].rearrange("p (q c) -> p q c", q=4)
        ang, a_top, a_low, frac, turns = [scratch[:, 64 * TT * n:64 * TT * n + 32 * TT].rearrange(
            "p (t f) -> p t f", t=TT) for n in range(5)]
        whole = scratch[:, 640:640 + 32 * TT].rearrange("p (t f) -> p t f", t=TT)
        vbuf = scratch[:, 0:CM * (S + HALO)].rearrange("p (m s) -> p m s", m=CM)
        o = CM * (S + HALO)
        acc = scratch[:, o:o + CM * S].rearrange("p (m s) -> p m s", m=CM)
        glu_sig = scratch[:, o + CM * S:o + 2 * CM * S].rearrange("p (m s) -> p m s", m=CM)
        taps = scratch[:, o + 2 * CM * S:o + 2 * CM * S + TAPS * CM].rearrange("p (w m) -> p w m", m=CM)
        diag = row_bc[:, 0:4 * PE_TAPS * P].rearrange("p (u w c) -> p u w c", u=4, c=P)
        early = [[diag_more[:, w, :] for w in range(PE_TAPS_LAST - PE_TAPS - 2 * TT)] +
                 [ytmp[:, t, D - P * n:D - P * n + P] for t in range(TT) for n in (1, 2)],
                 [row_bc[:, P * w:P * w + P] for w in range(2 * PE_TAPS, 2 * PE_TAPS + PE_TAPS_LAST - PE_TAPS)]]
        late = [[diag[:, mm, w, :] for w in range(PE_TAPS)] for mm in range(2)]
        diag_last = [early[mm] + late[mm] for mm in range(2)]
        order_last = [(mm, w) for mm in range(2) for w in range(PE_TAPS_LAST - PE_TAPS)] + \
                     [(mm, w) for mm in range(2) for w in range(PE_TAPS_LAST - PE_TAPS, PE_TAPS_LAST)]
        z_buf, z_sig, z_act = [scratch[:, 1024 * n:1024 * n + 1024].rearrange("p (b f) -> p b f", b=2)
                               for n in range(3)]
        ff_sig = scratch[:, 0:1024].rearrange("p (t f) -> p t f", t=TT)
        ff_h = scratch[:, 1024:2048].rearrange("p (t f) -> p t f", t=TT)
        qT = scratch[:, 0:512].rearrange("p (a s) -> p a s", a=2)
        kT = scratch[:, 512:1024].rearrange("p (a s) -> p a s", a=2)
        v_sb = scratch[:, 1024:1536].rearrange("p (t f) -> p t f", t=TT)
        q_rot = scratch[:, 1536:1792].rearrange("p (t f) -> p t f", t=TT)
        qrT = scratch[:, 1792:2048]
        prob = scratch[:, 2048:2816].rearrange("p (a f) -> p a f", a=2)
        pT = scratch[:, 2816:3584].rearrange("p (a f) -> p a f", a=2)
        krT = ytmp[:, 1, 1024:1280]
        k_rot = ytmp[:, 1, 1280:1536].rearrange("p (t f) -> p t f", t=TT)
        k_raw = ytmp[:, 1, 1536:1664].rearrange("p (t f) -> p t f", t=TT)
        rope_a = ytmp[:, 0, 1024:1280]
        rope_b = ytmp[:, 0, 1280:1536]
        c_q = ytmp[:, :, 0:LORA]
        c_kv = ytmp[:, :, LORA:2 * LORA]

        out_t = out[0].rearrange("(t p) d -> p t d", p=P)

        def hi32(ap):
            return ap.bitcast(F32)

        x_in = [sem(f"x_in{t}") for t in range(TT)]
        warm = sem("warm")
        small_in = sem("small_in")
        bias2_in = sem("bias2_in")
        final_g_in = sem("final_g_in")
        raw_in = [sem(f"raw_in{n}") for n in range(RING)]
        hi_done = sem("hi_done")
        lo_pool = sem("lo_pool")
        lo_dve = sem("lo_dve")
        group_used = sem("group_used")
        consts = sem("consts")
        vec_t = sem("vec_t")
        vec_done = sem("vec_done")
        chain = sem("chain")
        turn_ready = sem("turn_ready")
        rope_ready = sem("rope_ready")
        sq_act = sem("sq_act")
        rstd_ready = sem("rstd_ready")
        y_act = sem("y_act")
        y_dve = sem("y_dve")
        x_tr = sem("x_tr")
        xhi_done = sem("xhi_done")
        xlo_done = sem("xlo_done")
        glu_sig_done = sem("glu_sig_done")
        glu_done = sem("glu_done")
        conv_step = sem("conv_step")
        diag_done = sem("diag_done")
        row_done = sem("row_done")
        conv_tr = sem("conv_tr")
        z_done = sem("z_done")
        z_sig_done = sem("z_sig_done")
        z_act_done = sem("z_act_done")
        out_added = sem("out_added")
        ff_sig_done = sem("ff_sig_done")
        ff_h_done = sem("ff_h_done")
        ff_tr = sem("ff_tr")
        ahi_done = sem("ahi_done")
        alo_done = sem("alo_done")
        lat_tr = sem("lat_tr")
        kr_rot_done = sem("kr_rot_done")
        kr_tr = sem("kr_tr")
        kr_done = sem("kr_done")
        q_rot_done = sem("q_rot_done")
        qr_tr = sem("qr_tr")
        qr_done = sem("qr_done")
        qk_done = sem("qk_done")
        v_done = sem("v_done")
        scored = sem("scored")
        max_done = sem("max_done")
        exp_done = sem("exp_done")
        prob_done = sem("prob_done")
        prob_tr = sem("prob_tr")
        pT_done = sem("pT_done")
        pv_done = sem("pv_done")
        scaled_g = sem("scaled_g")
        rows_act = sem("rows_act")
        rows_dve = sem("rows_dve")
        stored = sem("stored")

        def val(n0, i=None, per=0):
            return n0 if i is None else i * per + n0

        def wait_lo(eng, g, i=None, per=0):
            if g < POOL_LO:
                eng.wait_ge(lo_pool, val(g + 1, i, per))
            else:
                eng.wait_ge(lo_dve, val(g - POOL_LO + 1, i, per))

        def norm_counts(n):
            return KT * n

        block = ctx.enter_context(nc.Block())

        @block.sync
        def _(sp):
            def load(src, g, i=None, per=0, cols=CH, tiles=GK):
                slot = g % RING
                if g >= RING:
                    wait_lo(sp, g - RING, i, per)
                sp.dma_start(raw[:, slot, 0:tiles * cols].rearrange("p (k n) -> p k n", k=tiles),
                             src).then_inc(raw_in[slot], LANDED)

            def tile_rows(w, rows, cols):
                return w.rearrange("(k p) n -> p k n", p=P)[:, rows, cols]

            x_t = x[0].rearrange("(t p) d -> p t d", p=P)
            for t in range(TT):
                sp.dma_start(resid[:, t, :], x_t[:, t, :]).then_inc(x_in[t], 16)

            w1 = conv_w_pw1[0].rearrange("(k p) (h n) -> p k h n", p=P, h=2)

            def pw1_loads(c, i=None):
                base = 0 if i is None else i * CH
                for u in range(2):
                    for j in range(KG):
                        g = G_PW1 + 2 * KG * c + KG * u + j
                        slot = g % RING
                        if g >= RING:
                            wait_lo(sp, g - RING, i, 2 * KG)
                        dst = raw[:, slot, :].rearrange("p (k h n) -> p k h n", k=GK, h=2)
                        for h in range(2):
                            if i is None and c == 0 and u == 0 and j == 1 and h == 0:
                                sp.wait_ge(small_in, 16 * 11)
                            sp.dma_start(dst[:, :, h, :],
                                         w1[:, GK * j:GK * j + GK, h, bass.ds(base + CH * c + CH // 2 * u, CH // 2)]
                                         ).then_inc(raw_in[slot], LANDED // 2)
            pw1_loads(0)
            with sp.Fori(0, CC - 1) as i:
                pw1_loads(1, i)

            def square_loads(w, g0):
                with sp.Fori(0, CC) as i:
                    for j in range(KG):
                        load(tile_rows(w, slice(GK * j, GK * j + GK), bass.ds(i * CH, CH)), g0 + j, i, KG)
            square_loads(conv_w_pw2[0], G_PW2)

            def ffn_loads(l, g0):
                wg, wu, wd = ffn_w_gate[l], ffn_w_up[l], ffn_w_down[l]

                def up(g, c, i=None, per=0):
                    base = 0 if i is None else i * CH
                    for n, w in ((0, wg), (1, wu)):
                        for j in range(KG):
                            load(tile_rows(w, slice(GK * j, GK * j + GK), bass.ds(base + CH * c, CH)),
                                 g + KG * n + j, i, per)

                def down(g, c, i=None, per=0):
                    base = 0 if i is None else i * CH
                    for n in range(CC):
                        load(wd[bass.ds(base + CH * c, CH), CH * n:CH * n + CH].rearrange("(k p) n -> p k n", p=P),
                             g + n, i, per)
                up(g0, 0)
                with sp.Fori(0, FC - 1) as i:
                    up(g0 + 2 * KG, 1, i, 3 * KG)
                    down(g0 + 4 * KG, 0, i, 3 * KG)
                down(g0 + 3 * KG * FC - KG, FC - 1)
            ffn_loads(0, G_FFN0)

            for j in range(KG):
                load(tile_rows(mla_w_dq[0], slice(GK * j, GK * j + GK), slice(0, CH)), G_DQ + j)
            for j in range(KG):
                load(tile_rows(mla_w_dkv[0], slice(GK * j, GK * j + GK), slice(0, CH)), G_DKV + j)
            load(tile_rows(mla_w_dkv[0], slice(0, KT), slice(LORA, LORA + ROPE)), G_KR, cols=ROPE, tiles=KT)

            def pair_loads(g, h, i=None, per=0, step=0):
                base = 0 if i is None else i * step
                load(tile_rows(mla_w_uq[0], slice(0, LT), bass.ds(base * (2 * QH) + 2 * QH * h, 2 * QH)),
                     g, i, per, cols=2 * QH)
                load(tile_rows(mla_w_ukv[0], slice(0, LT), bass.ds(base * (2 * KVH) + 2 * KVH * h, 2 * KVH)),
                     g + 1, i, per)
            pair_loads(G_ATT, 0)
            with sp.Fori(0, (PAIRS - 2) // 2) as i:
                for u in range(2):
                    pair_loads(G_ATT + 2 + 2 * u, 1 + u, i, 4, 2)
            pair_loads(G_ATT + 2 * (PAIRS - 1), PAIRS - 1)
            square_loads(mla_w_o[0], G_WO)
            ffn_loads(1, G_FFN1)

            for n in range(2):
                sp.wait_ge(rows_dve, n + 1)
                sp.dma_start(out_t[:, 1, 2 * CH * n:2 * CH * (n + 1)],
                             ytmp[:, 1, 2 * CH * n:2 * CH * (n + 1)]).then_inc(stored, 16)
            sp.wait_ge(stored, 16 * TT * 2)

        @block.gpsimd
        def _(pool):
            pool.memset(ident[:, :], 0.0).then_inc(consts, 1)
            pool.wait_ge(consts, 1)
            pool.affine_select(out=ident[:, :], in_=ident[:, :], compare_op=ALU.not_equal, fill=1.0, base=0,
                               pattern=[[-1, P]], channel_multiplier=1).then_inc(consts, 1)
            pool.memset(mask[:, :], 0.0).then_inc(consts, 1)
            pool.wait_ge(consts, 3)
            pool.memset(mask[0:64, 64:128], NEG).then_inc(consts, 1)
            pool.memset(mask[0:64, 320:384], NEG).then_inc(consts, 1)

            def lo(g, i=None, per=0):
                pool.wait_ge(hi_done, val(g + 1, i, per))
                pool.tensor_tensor(w_lo[:, g % RING, :], raw[:, g % RING, :], hi32(w_hi[:, g % RING, :]),
                                   ALU.subtract).then_inc(lo_pool, 1)
            for g in range(RING):
                lo(g)
            with pool.Fori(0, G_PW2 // RING) as i:
                for g in range(RING):
                    lo(RING + g, i, RING)
            for b in range(KT // 2):
                pool.wait_ge(xhi_done, norm_counts(1) + 2 * b + 2)
                pool.tensor_tensor(x_lo[:, 2 * b:2 * b + 2, :].rearrange("p k s -> p (k s)"), z_act[:, b % 2, :],
                                   hi32(x_hi[:, 2 * b:2 * b + 2, :]).rearrange("p k s -> p (k s)"),
                                   ALU.subtract).then_inc(xlo_done, 2)
            with pool.Fori(0, CC - 1) as i:
                for g in range(RING):
                    lo(G_PW2 + RING + g, i, RING)
            for g in range(G_FFN0, POOL_LO):
                lo(g)
            pool.wait_ge(final_g_in, 16)
            for n in range(CC):
                for t in range(TT):
                    pool.wait_ge(out_added, ADDED[5] + TT * CC * (FC - 1) + TT * n + t + 1)
                    pool.tensor_tensor(ytmp[:, t, CH * n:CH * n + CH], resid[:, t, CH * n:CH * n + CH],
                                       row_bc[:, CH * n:CH * n + CH], ALU.mult).then_inc(scaled_g, 1)

        @block.scalar
        def _(act):
            def rows(v):
                return v.rearrange("(t p) -> t p", p=P)

            loads = [(vec_row[R_ATTN:R_ATTN + 32, :], attn_norm_g.rearrange("l (t p) -> (l t) p", p=P)),
                     (vec_row[R_FFN:R_FFN + 32, :], ffn_norm_g.rearrange("l (t p) -> (l t) p", p=P)),
                     (vec_row[R_LNG:R_LNG + KT, :], rows(conv_ln_g[0])), (vec_row[R_LNB:R_LNB + KT, :], rows(conv_ln_b[0])),
                     (vec_row[R_BDW:R_BDW + KT, :], rows(conv_b_dw[0])), (vec_row[R_QN:R_QN + LT, :], rows(mla_q_norm_g[0])),
                     (vec_row[R_KVN:R_KVN + LT, :], rows(mla_kv_norm_g[0])), (bias1_row, rows(conv_b_pw1[0])),
                     (tap_row, conv_w_dw[0].rearrange("w (t p) -> (w t) p", p=P).rearrange("(q r) p -> r q p", q=4)),
                     (freq[:, :], inv_freq[0:1, :].to_broadcast([P, ROPE // 2]))]
            for dst, src in loads:
                act.dma_start(dst, src).then_inc(small_in, 16)
            with nc.allow_non_contiguous_dma(reason="256 positions, one per partition"):
                act.dma_start(pos_i[:, :], positions[0].rearrange("(t p) -> p t", p=P)).then_inc(small_in, 16)
            act.wait_ge(consts, 2)
            act.activation(esum[:, 0:1], ident[:, 0:1], ACT.Square).then_inc(warm, 1)
            act.wait_ge(warm, 1)

            def hi(g, i=None, per=0):
                slot = g % RING
                act.wait_ge(raw_in[slot], val(LANDED * (g // RING + 1), i, LANDED * per // RING))
                if g >= RING:
                    act.wait_ge(group_used, val(g - RING + 1, i, per))
                act.activation(w_hi[:, slot, :], raw[:, slot, :], ACT.Copy).then_inc(hi_done, 1)

            def first_norm(gain):
                act.wait_ge(x_in[0], 16)
                act.activation(ytmp[:, 0, :], resid[:, 0, :], ACT.Square, accum_out=stat[:, 0:1]).then_inc(sq_act, 1)
                act.dma_start(row_bc[:, :], conv_b_pw2[0:1, :].to_broadcast([P, D])).then_inc(bias2_in, 16)
                act.wait_ge(rstd_ready, 1)
                act.activation(ytmp[:, 0, :], resid[:, 0, :], ACT.Copy, scale=rstd[:, 0:1]).then_inc(y_act, 1)
                hi(0)
                act.wait_ge(vec_done, 1)
                for n in range(CC):
                    chunk_hi(0, n, gain)
                    if n == 0:
                        hi(1)

            def chunk_hi(norm, n, gain):
                for kk in range(GK):
                    k = GK * n + kk
                    if kk % 2 == 0:
                        act.wait_ge(x_tr, XT[norm] + k // 2 + 1)
                    act.activation(x_hi[:, k, :], ps[:, TBANK[norm][n] + kk // 2, S * (kk % 2):S * (kk % 2) + S],
                                   ACT.Copy, scale=vec_col[:, gain + k:gain + k + 1]).then_inc(xhi_done, 1)

            def norm(norm, gain, done=0):
                for n in range(done, CC):
                    chunk_hi(norm, n, gain)
                act.wait_ge(out_added, ADDED[norm])
                act.activation(ytmp[:, 0, :], resid[:, 0, :], ACT.Square, accum_out=stat[:, 0:1]).then_inc(sq_act, 1)

            first_norm(R_ATTN)
            hi(2)
            hi(3)
            act.wait_ge(vec_done, 3)

            def diagonals(s, i=None):
                for mm in range(2):
                    for w in range(PE_TAPS):
                        col = bass.ds((0 if i is None else i * CM) + 2 * s + mm, 1)
                        act.activation(diag[:, 2 * (s % 2) + mm, w, :], ident[:, :], ACT.Copy,
                                       scale=tap_col[:, w, col]).then_inc(diag_done, 1)

            def diagonals_last(which):
                for mm, w in which:
                    act.activation(diag_last[mm][w], ident[:, :], ACT.Copy,
                                   scale=tap_col[:, w, KT - 2 + mm:KT - 1 + mm]).then_inc(diag_done, 1)

            def rows_out(s, i=None):
                base = 0 if i is None else i * CH
                for t in range(TT):
                    act.wait_ge(conv_tr, val(TT * s + t + 1, i, 2 * TT))
                    act.activation(ytmp[:, t, bass.ds(base + CH // 2 * s, CH // 2)], ps[:, 4 + 2 * (s % 2) + t, 0:CH // 2],
                                   ACT.Copy).then_inc(row_done, 1)

            def conv_half(s, i=None):
                u = s % 2
                if s >= HALVES - 2:
                    n = PE_TAPS_LAST - PE_TAPS
                    diagonals_last(order_last[n * u:n * u + n])
                for j in range(KG):
                    hi(G_PW1 + KG * s + 4 + j, i, 2 * KG)
                act.wait_ge(group_used, val(G_PW1 + KG * s + KG, i, 2 * KG))
                if s >= 2:
                    act.wait_ge(glu_done, val((CM + 1) * (s // 2 - 1) + 2 * u + 3, i, CM + 1))
                for mm in range(2):
                    col = bass.ds((0 if i is None else i * CM) + KT + 2 * s + mm, 1)
                    act.activation(glu_sig[:, 2 * u + mm, :], ps[:, 2 * u + 1, S * mm:S * mm + S], ACT.Sigmoid,
                                   bias=bias1_col[:, col]).then_inc(glu_sig_done, 1)
                if s == 0:
                    act.wait_ge(out_added, TT)
                if s < HALVES - 1:
                    diagonals(s, i)
                if s > 0:
                    rows_out(s - 1, i)
            conv_half(0)
            conv_half(1)
            with act.Fori(0, CC - 2) as i:
                conv_half(2, i)
                conv_half(3, i)
            conv_half(HALVES - 2)
            conv_half(HALVES - 1)
            diagonals_last(order_last[2 * (PE_TAPS_LAST - PE_TAPS):])
            rows_out(HALVES - 1)

            act.wait_ge(rstd_ready, 2)
            for c in range(CC):
                act.activation(ytmp[:, 0, CH * c:CH * c + CH], ytmp[:, 0, CH * c:CH * c + CH], ACT.Identity,
                               bias=shift[:, 0:1], scale=rstd[:, 0:1]).then_inc(y_act, 1)

            def z_sigmoid(b):
                act.wait_ge(z_done, 2 * b + 2)
                act.activation(z_sig[:, b % 2, :], z_buf[:, b % 2, :], ACT.Sigmoid).then_inc(z_sig_done, 1)
            z_sigmoid(0)
            for b in range(KT // 2):
                if b < KT // 2 - 1:
                    z_sigmoid(b + 1)
                act.wait_ge(z_act_done, b + 1)
                act.activation(x_hi[:, 2 * b:2 * b + 2, :].rearrange("p k s -> p (k s)"), z_act[:, b % 2, :],
                               ACT.Copy).then_inc(xhi_done, 2)

            def square(g0, have4=False):
                if have4:
                    for j in range(3):
                        hi(g0 + 4 + j)
                    with act.Fori(0, CC - 1) as i:
                        for j in range(KG):
                            hi(g0 + 7 + j, i, KG)
                else:
                    with act.Fori(0, CC) as i:
                        for j in range(KG):
                            hi(g0 + 3 + j, i, KG)

            square(G_PW2, have4=True)

            def ffn(l, g0):
                hi(g0 + 3)

                def gate_sig(used, i=None):
                    for t in range(TT):
                        act.wait_ge(group_used, val(used, i, 12))
                        act.activation(ff_sig[:, t, :], ps[:, t, :], ACT.Sigmoid,
                                       scale=rstd[:, t:t + 1]).then_inc(ff_sig_done, 1)

                def hidden(c0, i=None):
                    for b in range(2):
                        act.wait_ge(ff_tr, val(2 * (FC * l + c0) + b + 1, i, 2))
                        act.activation(a_hi[:, 0, 2 * b:2 * b + 2, :].rearrange("p k s -> p (k s)"), ps[:, 4 + b, :],
                                       ACT.Copy).then_inc(ahi_done, 1)
                for j in range(4, 8):
                    hi(g0 + j)
                act.wait_ge(rstd_ready, RSTD[(2, 5)[l]])
                gate_sig(g0 + KG)
                for j in range(8, 11):
                    hi(g0 + j)
                with act.Fori(0, FC - 1) as i:
                    for j in range(11, 15):
                        hi(g0 + j, i, 12)
                    hidden(0, i)
                    gate_sig(g0 + 12, i)
                    for j in range(15, 23):
                        hi(g0 + j, i, 12)
                hidden(FC - 1)
                hi(g0 + 3 * KG * FC - 1)
                if l == 0:
                    end = g0 + 3 * KG * FC
                    hi(end)
                    hi(end + 1)
                    chunk_hi(3, 0, R_ATTN + KT)
                    hi(end + 2)
                    chunk_hi(3, 1, R_ATTN + KT)
                else:
                    for n in range(CC):
                        for t in range(TT):
                            act.wait_ge(out_added, ADDED[5] + TT * CC * (FC - 1) + TT * n + t + 1)
                            act.wait_ge(sq_act, SQ[5] + TT * n + t)
                            act.activation(ff_sig[:, t, :], resid[:, t, CH * n:CH * n + CH], ACT.Square,
                                           accum_out=ssq[:, t, n:n + 1]).then_inc(sq_act, 1)

            norm(2, R_FFN)
            ffn(0, G_FFN0)

            norm(3, R_ATTN + KT, done=2)
            for g in (3, 4, 5, 6):
                hi(G_DQ + g)

            def latent(which, bank, gain):
                dst = c_q if which == 0 else c_kv
                act.wait_ge(rstd_ready, RSTD[3])
                act.activation(dst[:, 0, :], ps[:, bank, :], ACT.Square, scale=rstd[:, 0:1],
                               accum_out=stat[:, 0:1]).then_inc(sq_act, 1)
                act.wait_ge(rstd_ready, 5 + which)
                act.activation(dst[:, 0, :], ps[:, bank, :], ACT.Copy, scale=rcomb[:, 0:1]).then_inc(y_act, 1)

            def latent_hi(which, bank, gain):
                for k in range(LT):
                    if k % 2 == 0:
                        act.wait_ge(lat_tr, 2 * which + k // 2 + 1)
                    act.activation(a_hi[:, which, k, :], ps[:, bank + k // 2, S * (k % 2):S * (k % 2) + S], ACT.Copy,
                                   scale=vec_col[:, gain + k:gain + k + 1]).then_inc(ahi_done, 1)
            act.wait_ge(group_used, G_DQ + KG)
            latent(0, 0, R_QN)
            for g in (7, 8, 9, 10):
                hi(G_DQ + g)
            act.wait_ge(turn_ready, 4)
            act.activation(cos2[:, :, :], cos2[:, :, :], ACT.Sin).then_inc(rope_ready, 1)
            act.activation(sin2[:, :, :], sin2[:, :, :], ACT.Sin).then_inc(rope_ready, 1)
            act.wait_ge(group_used, G_DKV + KG)
            latent(1, 2, R_KVN)
            latent_hi(0, 5, R_QN)
            hi(G_DQ + 11)
            latent_hi(1, 0, R_KVN)

            def pair_project(g, h, i=None):
                hi(g + 3, i, 4)
                act.wait_ge(group_used, val(g + 1, i, 4))
                act.activation(qT.rearrange("p a s -> p (a s)"), ps[:, 0, :], ACT.Copy).then_inc(qk_done, 1)
                hi(g + 4, i, 4)
                act.wait_ge(group_used, val(g + 2, i, 4))
                act.activation(kT.rearrange("p a s -> p (a s)"), ps[:, 2, :], ACT.Copy).then_inc(qk_done, 1)

            def pair_out(h, i=None):
                for a in range(2):
                    act.wait_ge(prob_tr, val(2 * h + a + 1, i, 4))
                    act.activation(pT[:, a, :], ps[:, 6 + a, 0:3 * P], ACT.Copy).then_inc(pT_done, 1)
                for a in range(2):
                    act.wait_ge(pv_done, val(2 * h + a + 1, i, 4))
                    dst = x_hi[:, 2 * h + a, :] if i is None else \
                        x_hi[:, bass.ds(i * 4 + 2 * h + a, 1), :].rearrange("p k s -> p (k s)")
                    act.activation(dst, ps[:, 6 + a, 0:S], ACT.Copy).then_inc(xhi_done, 1)

            def pair_exp(h, i=None):
                for a in range(2):
                    for q, (lo_, hi_) in enumerate(((0, P), (P, 3 * P))):
                        act.wait_ge(max_done, val(4 * h + 2 * a + q + 1, i, 8))
                        act.activation(prob[:, a, lo_:hi_], prob[:, a, lo_:hi_], ACT.Exp,
                                       bias=nmax[:, 2 * a + q:2 * a + q + 1],
                                       accum_out=esum[:, 2 * a + q:2 * a + q + 1]).then_inc(exp_done, 1)

            pair_project(G_ATT, 0)
            pair_exp(0)
            with act.Fori(0, (PAIRS - 2) // 2) as i:
                for u in range(2):
                    pair_project(G_ATT + 2 + 2 * u, 1 + u, i)
                    pair_out(u, i)
                    pair_exp(1 + u, i)
            pair_project(G_ATT + 2 * (PAIRS - 1), PAIRS - 1)
            pair_out(PAIRS - 2)
            pair_exp(PAIRS - 1)
            pair_out(PAIRS - 1)

            square(G_WO)
            act.wait_ge(out_added, TT)
            act.dma_start(row_bc[:, :], final_norm_g.rearrange("(a d) -> a d", a=1).to_broadcast([P, D])).then_inc(final_g_in, 16)
            norm(5, R_FFN + KT)
            ffn(1, G_FFN1)

            act.wait_ge(scaled_g, TT * CC)
            act.wait_ge(rstd_ready, 8)
            for n in range(2):
                act.activation(ytmp[:, 0, 2 * CH * n:2 * CH * (n + 1)], ytmp[:, 0, 2 * CH * n:2 * CH * (n + 1)], ACT.Copy,
                               scale=rstd[:, 0:1]).then_inc(rows_act, 1)
                act.wait_ge(rows_act, n + 1)
                act.dma_start(out_t[:, 0, 2 * CH * n:2 * CH * (n + 1)],
                              ytmp[:, 0, 2 * CH * n:2 * CH * (n + 1)]).then_inc(stored, 16)

        @block.vector
        def _(dve):
            links = [0]

            def link(ins):
                links[0] += 1
                ins.then_inc(chain, 1)
                dve.wait_ge(chain, links[0])

            def lo(g, i=None, per=0):
                dve.wait_ge(hi_done, val(g + 1, i, per))
                dve.tensor_tensor(w_lo[:, g % RING, :], raw[:, g % RING, :], hi32(w_hi[:, g % RING, :]),
                                  ALU.subtract).then_inc(lo_dve, 1)

            def inv_sqrt(root=rstd):
                link(dve.tensor_scalar(newton[:, :].bitcast(I32), stat[:, :].bitcast(I32), 1, None, ALU.logical_shift_right))
                link(dve.tensor_scalar(root[:, :].bitcast(I32), newton[:, :].bitcast(I32), -1.0, float(0x5F3759DF),
                                       ALU.mult, ALU.add))
                for step in range(3):
                    link(dve.scalar_tensor_tensor(newton[:, :], root[:, :], -0.5, root[:, :], ALU.mult, ALU.mult))
                    link(dve.tensor_tensor(newton[:, :], newton[:, :], stat[:, :], ALU.mult))
                    last = dve.scalar_tensor_tensor(root[:, :], newton[:, :], 1.5, root[:, :], ALU.add, ALU.mult)
                    if step < 2:
                        link(last)
                return last

            def mean_square(n, width):
                dve.wait_ge(sq_act, n)
                link(dve.tensor_scalar(stat[:, :], stat[:, :], 1.0 / width, EPS, ALU.mult, ALU.add))

            def chunk_lo(norm, n, gain):
                for kk in range(GK):
                    k = GK * n + kk
                    if kk % 2 == 0:
                        dve.wait_ge(xhi_done, norm_counts(norm) + k + 2)
                    dve.scalar_tensor_tensor(x_lo[:, k, :], ps[:, TBANK[norm][n] + kk // 2, S * (kk % 2):S * (kk % 2) + S],
                                             vec_col[:, gain + k:gain + k + 1], hi32(x_hi[:, k, :]),
                                             ALU.mult, ALU.subtract).then_inc(xlo_done, 1)

            def square_sum(norm):
                link(dve.tensor_tensor_reduce(out=ytmp[:, 1, :], in0=resid[:, 1, :], in1=resid[:, 1, :], scale=1.0,
                                              scalar=0.0, op0=ALU.mult, op1=ALU.add, accum_out=stat[:, 1:2]))
                mean_square(SQ[norm], D)
                inv_sqrt().then_inc(rstd_ready, 1)

            def first_norm(gain):
                square_sum(0)
                dve.wait_ge(rstd_ready, RSTD[0])
                dve.tensor_scalar(ytmp[:, 1, :], resid[:, 1, :], rstd[:, 1:2], None, ALU.mult).then_inc(y_dve, 1)
                dve.wait_ge(vec_t, 1)
                dve.tensor_copy(vec_col[:, :], ps[:, 6, 0:R_ALL]).then_inc(vec_done, 1)
                dve.tensor_copy(bias1_col[:, :], ps[:, 6, P:P + 2 * KT]).then_inc(vec_done, 1)
                dve.tensor_copy(tap_col[:, :, :].rearrange("p w t -> p (w t)"), ps[:, 7, 0:TAPS * KT]).then_inc(vec_done, 1)
                dve.wait_ge(vec_done, 3)
                for n in range(CC):
                    chunk_lo(0, n, gain)

            def norm(norm, gain, done=0):
                for n in range(done, CC):
                    chunk_lo(norm, n, gain)
                dve.wait_ge(out_added, ADDED[norm])
                square_sum(norm)

            dve.wait_ge(x_in[1], 16)
            first_norm(R_ATTN)

            dve.wait_ge(bias2_in, 16)
            dve.wait_ge(y_act, 1)
            dve.wait_ge(y_dve, 1)
            for t in range(TT):
                dve.tensor_tensor(resid[:, t, :], resid[:, t, :], row_bc[:, :], ALU.add).then_inc(out_added, 1)

            dve.memset(vbuf[:, :, 0:HALO], 0.0).then_inc(conv_step, 1)

            def conv_chunk(c, i=None):
                steps = 1 + 2 * DVE_STEPS * c
                tile0 = (0 if i is None else i * CM) + CM * c
                dve.wait_ge(conv_step, val(steps, i, 2 * DVE_STEPS))
                dve.tensor_copy(taps, tap_col[:, :, bass.ds(tile0, CM)]).then_inc(glu_done, 1)
                for u in range(2):
                    s = 2 * c + u
                    w0 = PE_TAPS if s < HALVES - 1 else PE_TAPS_LAST
                    dve.wait_ge(group_used, val(G_PW1 + KG * s + KG, i, 2 * KG))
                    if s >= 2:
                        dve.wait_ge(conv_tr, val(TT * (s - 1), i, 2 * TT))
                    for mm in range(2):
                        m = 2 * u + mm
                        dve.wait_ge(glu_sig_done, val(CM * c + m + 1, i, CM))
                        dve.scalar_tensor_tensor(vbuf[:, m, HALO:], ps[:, 2 * u, S * mm:S * mm + S],
                                                 bias1_col[:, bass.ds(tile0 + m, 1)], glu_sig[:, m, :],
                                                 ALU.add, ALU.mult).then_inc(glu_done, 1)
                    for w in range(w0, TAPS):
                        for mm in range(2):
                            m = 2 * u + mm
                            if w == w0:
                                dve.wait_ge(glu_done, val((CM + 1) * c + m + 2, i, CM + 1))
                                dve.tensor_scalar(acc[:, m, :], vbuf[:, m, w:w + S], taps[:, w, m:m + 1],
                                                  vec_col[:, bass.ds(tile0 + R_BDW + m, 1)],
                                                  ALU.mult, ALU.add).then_inc(conv_step, 1)
                                continue
                            dve.wait_ge(conv_step, val(steps + DVE_STEPS * u + 2 * (w - w0) + mm - 1, i,
                                                       2 * DVE_STEPS))
                            dve.scalar_tensor_tensor(acc[:, m, :], vbuf[:, m, w:w + S], taps[:, w, m:m + 1], acc[:, m, :],
                                                     ALU.mult, ALU.add).then_inc(conv_step, 1)
                    if s > 0:
                        row_stats(s - 1, i)

            def row_stats(s, i=None):
                half0 = (0 if i is None else i * 2) + s
                base = (0 if i is None else i * CH) + CH // 2 * s
                for t in range(TT):
                    dve.wait_ge(row_done, val(TT * s + t + 1, i, 2 * TT))
                    last = dve.bn_stats(bn[:, t, bass.ds(half0, 1), :].rearrange("p h s -> p (h s)"),
                                        ytmp[:, t, bass.ds(base, CH // 2)])
                return last
            conv_chunk(0)
            with dve.Fori(0, CC - 2) as i:
                conv_chunk(1, i)
            conv_chunk(CC - 1)

            link(row_stats(HALVES - 1))
            for t in range(TT):
                link(dve.bn_aggr(mv[:, t, :], bn[:, t, :, :].rearrange("p c s -> p (c s)")))
            link(dve.tensor_scalar(stat[:, :], mv[:, :, 1], EPS, None, ALU.add))
            link(inv_sqrt())
            dve.scalar_tensor_tensor(shift[:, :], mv[:, :, 0], -1.0, rstd[:, :], ALU.mult, ALU.mult).then_inc(rstd_ready, 1)
            for c in range(CC):
                dve.tensor_scalar(ytmp[:, 1, CH * c:CH * c + CH], ytmp[:, 1, CH * c:CH * c + CH], mv[:, 1, 0:1],
                                  rstd[:, 1:2], ALU.subtract, ALU.mult).then_inc(y_dve, 1)

            def gain_and_bias(b):
                dve.wait_ge(x_tr, XT[1] + b + 1)
                if b >= 2:
                    dve.wait_ge(z_act_done, b - 1)
                for kk in range(2):
                    k = 2 * b + kk
                    dve.tensor_scalar(z_buf[:, b % 2, S * kk:S * kk + S], ps[:, b, S * kk:S * kk + S],
                                      vec_col[:, R_LNG + k:R_LNG + k + 1], vec_col[:, R_LNB + k:R_LNB + k + 1],
                                      ALU.mult, ALU.add).then_inc(z_done, 1)
            gain_and_bias(0)
            for b in range(KT // 2):
                if b < KT // 2 - 1:
                    gain_and_bias(b + 1)
                dve.wait_ge(z_sig_done, b + 1)
                if b >= 2:
                    dve.wait_ge(xlo_done, norm_counts(1) + 2 * b - 2)
                dve.tensor_tensor(z_act[:, b % 2, :], z_buf[:, b % 2, :], z_sig[:, b % 2, :],
                                  ALU.mult).then_inc(z_act_done, 1)

            def square(g0, split=True):
                with dve.Fori(0, CC // 2) as i:
                    for n in range(2):
                        for j in range(KG if split else 0):
                            lo(g0 + 3 + KG * n + j, i, 2 * KG)
                        for t in range(TT):
                            dve.wait_ge(group_used, val(g0 + KG * n + KG, i, 2 * KG))
                            cols = bass.ds(i * (2 * CH) + CH * n, CH)
                            dve.tensor_tensor(resid[:, t, cols], resid[:, t, cols], ps[:, 2 * n + t, :],
                                              ALU.add).then_inc(out_added, 1)

            dve.wait_ge(out_added, TT)
            dve.wait_ge(xlo_done, norm_counts(1) + KT)
            link(dve.tensor_copy(pos_f[:, :], pos_i[:, :]))
            for t in range(TT):
                link(dve.tensor_scalar(ang[:, t, :], freq[:, :], pos_f[:, t:t + 1], None, ALU.mult))
            link(dve.tensor_scalar(a_top.bitcast(I32), ang.bitcast(I32), -4096, None, ALU.bitwise_and))
            link(dve.tensor_tensor(a_low, ang, a_top, ALU.subtract))
            link(dve.memset(turns, 0.0))
            for piece in reversed(turn_pieces()):
                for part in (a_low, a_top):
                    link(dve.tensor_scalar(whole.bitcast(I32), part, piece, None, ALU.mult))
                    link(dve.scalar_tensor_tensor(frac, part, piece, whole.bitcast(I32), ALU.mult, ALU.subtract))
                    link(dve.tensor_tensor(turns, turns, frac, ALU.add))
            magic = 1.5 * 2.0 ** 23
            for quarter, dst in ((0.25, cos2), (0.0, sin2)):
                link(dve.tensor_scalar(frac, turns, quarter, None, ALU.add))
                link(dve.tensor_scalar(whole, frac, magic, magic, ALU.add, ALU.subtract))
                link(dve.tensor_tensor(frac, frac, whole, ALU.subtract))
                link(dve.tensor_scalar(frac, frac, TWO_PI, None, ALU.mult))
                for half in range(2):
                    dve.tensor_scalar(dst[:, :, 32 * half:32 * half + 32], frac, 3.1415925, -3.1415925,
                                      ALU.min, ALU.max).then_inc(turn_ready, 1)
                dve.wait_ge(turn_ready, 2 if dst is cos2 else 4)

            square(G_PW2, split=False)

            def ffn(l, g0, added):
                def hidden(c0, i=None):
                    for b in range(2):
                        dve.wait_ge(ahi_done, val(AHI[l] + 2 * c0 + b + 1, i, 2))
                        dve.tensor_tensor(a_lo[:, 0, 2 * b:2 * b + 2, :].rearrange("p k s -> p (k s)"), ps[:, 4 + b, :],
                                          hi32(a_hi[:, 0, 2 * b:2 * b + 2, :]).rearrange("p k s -> p (k s)"),
                                          ALU.subtract).then_inc(alo_done, 1)

                def gate_mul(c0, i=None):
                    for t in range(TT):
                        dve.wait_ge(ff_sig_done, val(2 * (FC * l + c0) + t + 1, i, 2))
                        dve.scalar_tensor_tensor(ff_h[:, t, :], ps[:, t, :], rstd[:, t:t + 1], ff_sig[:, t, :],
                                                 ALU.mult, ALU.mult).then_inc(ff_h_done, 1)

                def up_mul(c0, used, i=None):
                    for t in range(TT):
                        dve.wait_ge(group_used, val(used, i, 12))
                        dve.wait_ge(ff_h_done, val(4 * (FC * l + c0) + t + 1, i, 4))
                        dve.scalar_tensor_tensor(ff_h[:, t, :], ps[:, 2 + t, :], rstd[:, t:t + 1], ff_h[:, t, :],
                                                 ALU.mult, ALU.mult).then_inc(ff_h_done, 1)

                def add(n, used, i=None):
                    for t in range(TT):
                        dve.wait_ge(group_used, val(used, i, 12))
                        cols = slice(CH * n, CH * n + CH)
                        dve.tensor_tensor(resid[:, t, cols], resid[:, t, cols], ps[:, 4 + (2 * n + t) % 4, :],
                                          ALU.add).then_inc(out_added, 1)
                lo(g0 + 3)
                for j in range(4, 8):
                    lo(g0 + j)
                gate_mul(0)
                for j in range(8, 11):
                    lo(g0 + j)
                up_mul(0, g0 + 8)
                with dve.Fori(0, FC - 1) as i:
                    for j in range(11, 15):
                        lo(g0 + j, i, 12)
                    hidden(0, i)
                    gate_mul(1, i)
                    for j in range(15, 19):
                        lo(g0 + j, i, 12)
                    up_mul(1, g0 + 16, i)
                    lo(g0 + 19, i, 12)
                    for n in range(CC):
                        if n < CC - 1:
                            lo(g0 + 20 + n, i, 12)
                        add(n, g0 + 17 + n, i)
                hidden(FC - 1)
                end = g0 + 3 * KG * FC
                lo(end - 1)
                for n in range(CC):
                    if l == 0 and n < 3:
                        lo(end + n)
                    if l == 0 and n == 3:
                        chunk_lo(3, 1, R_ATTN + KT)
                    add(n, end - KG + n + 1)
                    if l == 0 and n == 2:
                        chunk_lo(3, 0, R_ATTN + KT)

            norm(2, R_FFN)
            ffn(0, G_FFN0, 0)

            norm(3, R_ATTN + KT, done=2)
            for g in (3, 4, 5, 6):
                lo(G_DQ + g)

            def latent(which, bank):
                dst = c_q if which == 0 else c_kv
                link(dve.tensor_scalar(dst[:, 1, :], ps[:, bank + 1, :], rstd[:, 1:2], None, ALU.mult))
                link(dve.tensor_tensor_reduce(out=rope_scr, in0=dst[:, 1, :], in1=dst[:, 1, :], scale=1.0,
                                              scalar=0.0, op0=ALU.mult, op1=ALU.add, accum_out=stat[:, 1:2]))
                mean_square(4 + which, LORA)
                link(inv_sqrt(rlat))
                dve.tensor_tensor(rcomb[:, :], rlat[:, :], rstd[:, :], ALU.mult).then_inc(rstd_ready, 1)
                dve.tensor_scalar(dst[:, 1, :], dst[:, 1, :], rlat[:, 1:2], None, ALU.mult).then_inc(y_dve, 1)

            def latent_lo(which, bank, gain):
                for k in range(LT):
                    if k % 2 == 0:
                        dve.wait_ge(ahi_done, 2 * FC + LT * which + k + 2)
                    dve.scalar_tensor_tensor(a_lo[:, which, k, :], ps[:, bank + k // 2, S * (k % 2):S * (k % 2) + S],
                                             vec_col[:, gain + k:gain + k + 1], hi32(a_hi[:, which, k, :]),
                                             ALU.mult, ALU.subtract).then_inc(alo_done, 1)

            def rotate(src, dst, n, cos_bc, sin_bc):
                link(dve.tensor_tensor(rope_a4(n), src, cos_bc, ALU.mult))
                link(dve.tensor_tensor(rope_b4(n), src, sin_bc, ALU.mult))
                half = ROPE // 2
                link(dve.tensor_tensor(dst[..., 0:half], rope_a4(n)[..., 0:half], rope_b4(n)[..., half:ROPE], ALU.subtract))
                return dve.tensor_tensor(dst[..., half:ROPE], rope_a4(n)[..., half:ROPE], rope_b4(n)[..., 0:half], ALU.add)

            rope_scr = ytmp[:, 0, 1536:2048]

            def rope_a4(n):
                return rope_a[:, 0:TT * n * ROPE].rearrange("p (t h r) -> p t h r", t=TT, h=n)

            def rope_b4(n):
                return rope_b[:, 0:TT * n * ROPE].rearrange("p (t h r) -> p t h r", t=TT, h=n)

            def table(tab, n):
                return tab[:, :, :].rearrange("p t (h r) -> p t h r", h=1).to_broadcast([P, TT, n, ROPE])

            dve.wait_ge(group_used, G_DQ + KG)
            latent(0, 0)
            for g in (7, 8, 9, 10):
                lo(G_DQ + g)
            dve.wait_ge(group_used, G_DKV + KG)
            latent(1, 2)
            latent_lo(0, 5, R_QN)
            lo(G_DQ + 11)
            dve.wait_ge(rope_ready, 2)
            dve.wait_ge(group_used, G_KR + 1)
            kr4 = k_rot.rearrange("p t (h r) -> p t h r", h=2)
            for t in range(TT):
                link(dve.tensor_scalar(k_raw[:, t, :], ps[:, 4, ROPE * t:ROPE * t + ROPE], rstd[:, t:t + 1], None, ALU.mult))
            link(rotate(k_raw.rearrange("p t (h r) -> p t h r", h=1), kr4[:, :, 0:1, :], 1,
                        table(cos2, 1), table(sin2, 1)))
            dve.tensor_copy(kr4[:, :, 1:2, :], kr4[:, :, 0:1, :]).then_inc(kr_rot_done, 1)
            latent_lo(1, 0, R_KVN)
            dve.wait_ge(kr_tr, 1)
            dve.tensor_copy(krT, ps[:, 7, 0:S]).then_inc(kr_done, 1)

            rot_links = [0]

            def pair_project(g, h, i=None):
                lo(g + 3, i, 4)
                dve.wait_ge(group_used, val(g + 1, i, 4))
                src = ps[:, 1, 0:S].rearrange("p (t h r) -> p t h r", t=TT, h=2)
                a4, b4, d4 = rope_a4(2), rope_b4(2), q_rot.rearrange("p t (h r) -> p t h r", h=2)
                half = ROPE // 2
                dve.tensor_tensor(a4, src, table(cos2, 2), ALU.mult).then_inc(q_rot_done, 1)
                dve.tensor_tensor(b4, src, table(sin2, 2), ALU.mult).then_inc(q_rot_done, 1)
                dve.wait_ge(q_rot_done, val(4 * h + 2, i, 8))
                dve.tensor_tensor(d4[..., 0:half], a4[..., 0:half], b4[..., half:ROPE], ALU.subtract).then_inc(q_rot_done, 1)
                dve.tensor_tensor(d4[..., half:ROPE], a4[..., half:ROPE], b4[..., 0:half], ALU.add).then_inc(q_rot_done, 1)
                lo(g + 4, i, 4)
                pair_queries(h, i)

            def pair_out(h, i=None):
                for a in range(2):
                    dve.wait_ge(xhi_done, val(norm_counts(4) + 2 * h + a + 1, i, 4))
                    dst, high = (x_lo[:, 2 * h + a, :], x_hi[:, 2 * h + a, :]) if i is None else \
                        (x_lo[:, bass.ds(i * 4 + 2 * h + a, 1), :].rearrange("p k s -> p (k s)"),
                         x_hi[:, bass.ds(i * 4 + 2 * h + a, 1), :].rearrange("p k s -> p (k s)"))
                    dve.tensor_tensor(dst, ps[:, 6 + a, 0:S], hi32(high), ALU.subtract).then_inc(xlo_done, 1)

            def pair_keys(g, h, i=None):
                dve.wait_ge(group_used, val(g + 2, i, 4))
                dve.tensor_copy(v_sb.rearrange("p t f -> p (t f)"), ps[:, 3, :]).then_inc(v_done, 1)

            def pair_queries(h, i=None):
                dve.wait_ge(qr_tr, val(h + 1, i, 2))
                dve.tensor_copy(qrT, ps[:, 1, S:2 * S]).then_inc(qr_done, 1)

            def pair_softmax(h, i=None):
                for a in range(2):
                    dve.wait_ge(scored, val(2 * h + a + 1, i, 4))
                    dve.scalar_tensor_tensor(prob[:, a, :], ps[:, 4 + a, 0:3 * P], SM_SCALE, mask[:, :],
                                             ALU.mult, ALU.add).then_inc(prob_done, 1)
                    for q, (lo_, hi_) in enumerate(((0, P), (P, 3 * P))):
                        dve.wait_ge(prob_done, val(7 * h + a + 1, i, 14))
                        dve.tensor_reduce(nmax[:, 2 * a + q:2 * a + q + 1], prob[:, a, lo_:hi_], AX.X, ALU.max,
                                          negate=True).then_inc(max_done, 1)
                dve.wait_ge(exp_done, val(4 * h + 4, i, 8))
                dve.reciprocal(erec[:, :], esum[:, :]).then_inc(prob_done, 1)
                dve.wait_ge(prob_done, val(7 * h + 3, i, 14))
                for a in range(2):
                    for q, (lo_, hi_) in enumerate(((0, P), (P, 3 * P))):
                        dve.tensor_scalar(prob[:, a, lo_:hi_], prob[:, a, lo_:hi_], erec[:, 2 * a + q:2 * a + q + 1],
                                          None, ALU.mult).then_inc(prob_done, 1)

            pair_project(G_ATT, 0)
            pair_keys(G_ATT, 0)
            pair_softmax(0)
            with dve.Fori(0, (PAIRS - 2) // 2) as i:
                for u in range(2):
                    g = G_ATT + 2 + 2 * u
                    pair_project(g, 1 + u, i)
                    pair_out(u, i)
                    pair_keys(g, 1 + u, i)
                    pair_softmax(1 + u, i)
            g = G_ATT + 2 * (PAIRS - 1)
            pair_project(g, PAIRS - 1)
            pair_out(PAIRS - 2)
            pair_keys(g, PAIRS - 1)
            pair_softmax(PAIRS - 1)
            pair_out(PAIRS - 1)

            square(G_WO)
            norm(5, R_FFN + KT)
            ffn(1, G_FFN1, 0)

            dve.wait_ge(sq_act, SQ[5] + TT * CC)
            link(dve.tensor_reduce(stat[:, :], ssq[:, :, :], AX.X, ALU.add))
            link(dve.tensor_scalar(stat[:, :], stat[:, :], 1.0 / D, EPS, ALU.mult, ALU.add))
            inv_sqrt().then_inc(rstd_ready, 1)
            dve.wait_ge(rstd_ready, 8)
            dve.wait_ge(scaled_g, TT * CC)
            for n in range(2):
                dve.tensor_scalar(ytmp[:, 1, 2 * CH * n:2 * CH * (n + 1)], ytmp[:, 1, 2 * CH * n:2 * CH * (n + 1)],
                                  rstd[:, 1:2], None, ALU.mult).then_inc(rows_dve, 1)

        @block.tensor
        def _(pe):
            def w_rows(tensor, slot, cols=CH):
                return tensor[:, slot, 0:(GK * CH // cols) * cols].rearrange("p (k n) -> p k n", n=cols)

            def product(dst, pairs, first, last, skip=False):
                for n, (lhsT, rhs) in enumerate(pairs):
                    ins = pe.matmul(dst, lhsT, rhs, start=first and n == 0, stop=last and n == len(pairs) - 1,
                                    skip_group_check=skip)
                return ins

            def three(a_h, a_l, b_h, b_l):
                return [(a_h, b_h), (a_h, b_l), (a_l, b_h)]

            def token_group(g, i, per, j, banks, xh, xl, kt0, n_groups, x_count=None):
                wait_lo(pe, g, i, per)
                slot = g % RING
                wh, wl = w_rows(w_hi, slot), w_rows(w_lo, slot)
                for kk in range(GK):
                    if x_count is not None and kk % 2 == 0:
                        pe.wait_ge(xlo_done, x_count + kt0 + kk + 2)
                    for t in range(TT):
                        k = kt0 + kk
                        ins = product(ps[:, banks[t], :],
                                      three(xh[:, k, P * t:P * t + P], xl[:, k, P * t:P * t + P], wh[:, kk, :], wl[:, kk, :]),
                                      j == 0 and kk == 0, j == n_groups - 1 and kk == GK - 1)
                ins.then_inc(group_used, 1)

            def transposes(n, y_count=None):
                for b in range(KT // 2):
                    if n == 0 and b == 6:
                        pe.wait_ge(vec_done, 3)
                    if y_count is not None and b % 2 == 0:
                        pe.wait_ge(y_act, y_count + b // 2 + 1)
                        pe.wait_ge(y_dve, y_count + b // 2 + 1)
                    for kk in range(2):
                        for t in range(TT):
                            ins = pe.transpose(ps[:, b, S * kk + P * t:S * kk + P * t + P],
                                               ytmp[:, t, P * (2 * b + kk):P * (2 * b + kk) + P], ident[:, :])
                    ins.then_inc(x_tr, 1)

            def residual_transposes(norm, n, added):
                pe.wait_ge(out_added, added + TT * (n + 1))
                for b in range(2):
                    for kk in range(2):
                        for t in range(TT):
                            k = GK * n + 2 * b + kk
                            ins = pe.transpose(ps[:, TBANK[norm][n] + b, S * kk + P * t:S * kk + P * t + P],
                                               resid[:, t, P * k:P * k + P], ident[:, :])
                    ins.then_inc(x_tr, 1)

            pe.wait_ge(small_in, 16 * 11)
            pe.wait_ge(consts, 2)
            pe.transpose(ps[:, 6, 0:R_ALL], vec_row, ident[0:R_ALL, 0:R_ALL])
            pe.transpose(ps[:, 6, P:P + 2 * KT], bias1_row, ident[0:2 * KT, 0:2 * KT])
            for q in range(4):
                ins = pe.transpose(ps[:, 7, 4 * TAPS * q:4 * TAPS * q + 4 * TAPS], tap_row[:, q, :],
                                   ident[0:4 * TAPS, 0:4 * TAPS])
            ins.then_inc(vec_t, 1)

            pe.wait_ge(y_act, 1)
            pe.wait_ge(y_dve, 1)
            transposes(0)

            def channel_half(s, i=None):
                u = s % 2
                for j in range(KG):
                    g = G_PW1 + KG * s + j
                    wait_lo(pe, g, i, 2 * KG)
                    wh, wl = w_rows(w_hi, g % RING), w_rows(w_lo, g % RING)
                    if s == 0:
                        pe.wait_ge(xlo_done, GK * (j + 1))
                    if s >= 1 and j == 0:
                        if s == 1:
                            pe.wait_ge(xlo_done, GK * KG)
                        else:
                            pe.wait_ge(glu_done, val((CM + 1) * (s // 2 - 1) + 2 * u + 3, i, CM + 1))
                    for kk in range(GK):
                        k = GK * j + kk
                        for m in range(CM):
                            cols = slice(P * m, P * m + P)
                            ins = product(ps[:, 2 * u + m // 2, S * (m % 2):S * (m % 2) + S],
                                          [(wh[:, kk, cols], x_hi[:, k, :]), (wh[:, kk, cols], x_lo[:, k, :]),
                                           (wl[:, kk, cols], x_hi[:, k, :])],
                                          j == 0 and kk == 0 and m % 2 == 0, j == KG - 1 and kk == GK - 1, skip=True)
                    ins.then_inc(group_used, 1)

            def conv_rows(s, i=None):
                u = s % 2
                last = s == HALVES - 1
                pe.wait_ge(glu_done, val((CM + 1) * (s // 2) + 2 * u + 3, i, CM + 1))
                if s >= 2:
                    pe.wait_ge(row_done, val(TT * (s - 1), i, 2 * TT))
                for n, (mm, w) in enumerate(order_last if last else [(mm, w) for mm in range(2) for w in range(PE_TAPS)]):
                    made = 2 * PE_TAPS * s + n + 1 + (PE_TAPS_LAST - PE_TAPS if s == HALVES - 2 else 0)
                    pe.wait_ge(diag_done, val(made, i, 4 * PE_TAPS))
                    rhs = diag_last[mm][w] if last else diag[:, 2 * u + mm, w, :]
                    for t in range(TT):
                        product(ps[:, 4 + 2 * u + t, P * mm:P * mm + P],
                                [(vbuf[:, 2 * u + mm, w + P * t:w + P * t + P], rhs)], n == 0, False, skip=True)
                if last:
                    pe.wait_ge(conv_step, 1 + DVE_STEPS * s + 2 * (TAPS - PE_TAPS_LAST))
                else:
                    pe.wait_ge(conv_step, val(1 + DVE_STEPS * (s + 1), i, 2 * DVE_STEPS))
                for t in range(TT):
                    for mm in range(2):
                        ins = product(ps[:, 4 + 2 * u + t, P * mm:P * mm + P],
                                      [(acc[:, 2 * u + mm, P * t:P * t + P], ident[:, :])], False, True, skip=True)
                    ins.then_inc(conv_tr, 1)
            channel_half(0)
            channel_half(1)
            conv_rows(0)
            with pe.Fori(0, CC - 2) as i:
                channel_half(2, i)
                conv_rows(1, i)
                channel_half(3, i)
                conv_rows(2, i)
            channel_half(HALVES - 2)
            conv_rows(HALVES - 3)
            channel_half(HALVES - 1)
            conv_rows(HALVES - 2)
            conv_rows(HALVES - 1)

            pe.wait_ge(row_done, TT * HALVES)
            transposes(1, y_count=1)

            def square(g0, x_count, added):
                with pe.Fori(0, CC // 2) as i:
                    for n in range(2):
                        for j in range(KG):
                            if j == 0:
                                pe.wait_ge(out_added, val(added - 1 + n, i, 2 * TT))
                            token_group(g0 + KG * n + j, i, 2 * KG, j, (2 * n, 2 * n + 1), x_hi, x_lo, GK * j, KG,
                                        x_count=x_count)
            square(G_PW2, norm_counts(1), TT)

            def ffn(l, g0, x_count, added):
                def half(g, c0, i, part):
                    for j in range(KG):
                        if i is None and part == 0 and j == 1:
                            pe.wait_ge(xlo_done, x_count + GK)
                            residual_transposes((2, 5)[l], 3, added - TT * CC)
                        if i is None and part == 0:
                            pe.wait_ge(xlo_done, x_count + GK * (j + 1))
                        token_group(g + j, i, 12, j, (2 * part, 2 * part + 1), x_hi, x_lo, GK * j, KG)

                def hidden(c0, i=None):
                    pe.wait_ge(ff_h_done, val(4 * (FC * l + c0) + 4, i, 4))
                    for b in range(2):
                        pe.wait_ge(out_added, val(added + TT * CC * (c0 - 1) + 5 + b, i, TT * CC))
                        for kk in range(2):
                            for t in range(TT):
                                m = 2 * b + kk
                                ins = pe.transpose(ps[:, 4 + b, S * kk + P * t:S * kk + P * t + P],
                                                   ff_h[:, t, P * m:P * m + P], ident[:, :])
                        ins.then_inc(ff_tr, 1)

                def down(g, c0, i=None, after=None):
                    for n in range(CC):
                        wait_lo(pe, g + n, i, 12)
                        slot = (g + n) % RING
                        wh, wl = w_rows(w_hi, slot), w_rows(w_lo, slot)
                        for t in range(TT):
                            block_no = 2 * n + t
                            if block_no >= 2:
                                pe.wait_ge(out_added, val(added + TT * CC * c0 + block_no - 3, i, TT * CC))
                            for kk in range(LT):
                                if block_no == 0 and kk % 2 == 0:
                                    pe.wait_ge(alo_done, val(AHI[l] + 2 * c0 + kk // 2 + 1, i, 2))
                                ins = product(ps[:, 4 + block_no % 4, :],
                                              three(a_hi[:, 0, kk, P * t:P * t + P], a_lo[:, 0, kk, P * t:P * t + P],
                                                    wh[:, kk, :], wl[:, kk, :]), kk == 0, kk == LT - 1)
                        ins.then_inc(group_used, 1)
                        if after is not None:
                            after(n)

                half(g0, 0, None, 0)
                half(g0 + KG, 0, None, 1)
                with pe.Fori(0, FC - 1) as i:
                    pe.wait_ge(ff_h_done, val(4 * FC * l + 4, i, 4))
                    half(g0 + 8, 0, i, 0)
                    hidden(0, i)
                    half(g0 + 12, 0, i, 1)
                    down(g0 + 16, 0, i)
                hidden(FC - 1)

                def between(n):
                    if n >= 2:
                        if n == 3:
                            pe.wait_ge(xlo_done, norm_counts(3) + GK)
                        residual_transposes(3, n - 2, ADDED[3] - TT * CC)
                down(g0 + 3 * KG * FC - KG, FC - 1, after=between if l == 0 else None)

            def chunks_to_ffn(norm, added):
                residual_transposes(norm, 0, added)
                residual_transposes(norm, 1, added)
                pe.wait_ge(out_added, added + TT * CC)
                residual_transposes(norm, 2, added)
            chunks_to_ffn(2, TT)
            ffn(0, G_FFN0, norm_counts(2), ADDED[2])

            pe.wait_ge(xlo_done, norm_counts(3) + 2 * GK)
            residual_transposes(3, 2, ADDED[3] - TT * CC)
            for j in range(KG):
                if j == 1:
                    residual_transposes(3, 3, ADDED[3] - TT * CC)
                pe.wait_ge(xlo_done, norm_counts(3) + GK * (j + 1))
                token_group(G_DQ + j, None, 0, j, (0, 1), x_hi, x_lo, GK * j, KG)
            for j in range(KG):
                token_group(G_DKV + j, None, 0, j, (2, 3), x_hi, x_lo, GK * j, KG)

            def latent_transposes(src, bank):
                for b in range(2):
                    for kk in range(2):
                        for t in range(TT):
                            k = 2 * b + kk
                            ins = pe.transpose(ps[:, bank + b, S * kk + P * t:S * kk + P * t + P],
                                               src[:, t, P * k:P * k + P], ident[:, :])
                    ins.then_inc(lat_tr, 1)
            pe.wait_ge(y_act, 2 + CC)
            pe.wait_ge(y_dve, 2 + CC)
            latent_transposes(c_q, 5)
            wait_lo(pe, G_KR)
            wh, wl = w_rows(w_hi, G_KR % RING, ROPE), w_rows(w_lo, G_KR % RING, ROPE)
            for t in range(TT):
                for k in range(KT):
                    ins = product(ps[:, 4, ROPE * t:ROPE * t + ROPE],
                                  three(x_hi[:, k, P * t:P * t + P], x_lo[:, k, P * t:P * t + P], wh[:, k, :], wl[:, k, :]),
                                  k == 0, k == KT - 1)
            ins.then_inc(group_used, 1)
            pe.wait_ge(y_act, 3 + CC)
            pe.wait_ge(y_dve, 3 + CC)
            latent_transposes(c_kv, 0)
            pe.wait_ge(kr_rot_done, 1)
            for t in range(TT):
                ins = pe.transpose(ps[:, 7, P * t:P * t + P], k_rot[:, t, :], ident[:, :])
            ins.then_inc(kr_tr, 1)

            def pair_project(g, h, i=None):
                if h == 0 and i is None:
                    pe.wait_ge(alo_done, 2 * FC + 2 * LT)
                wait_lo(pe, g, i, 4)
                wh, wl = w_rows(w_hi, g % RING, 2 * QH), w_rows(w_lo, g % RING, 2 * QH)
                for a in range(2):
                    for k in range(LT):
                        cols = slice(QH * a, QH * a + NOPE)
                        product(ps[:, 0, S * a:S * a + S],
                                [(wh[:, k, cols], a_hi[:, 0, k, :]), (wh[:, k, cols], a_lo[:, 0, k, :]),
                                 (wl[:, k, cols], a_hi[:, 0, k, :])], k == 0, k == LT - 1)
                for t in range(TT):
                    for k in range(LT):
                        def both(w):
                            return w[:, k, :].rearrange("p (a n) -> p a n", a=2)[:, :, NOPE:QH]
                        toks = slice(P * t, P * t + P)
                        ins = product(ps[:, 1, P * t:P * t + P].rearrange("p (a n) -> p a n", a=2),
                                      three(a_hi[:, 0, k, toks], a_lo[:, 0, k, toks], both(wh), both(wl)),
                                      k == 0, k == LT - 1)
                ins.then_inc(group_used, 1)
                g += 1
                wait_lo(pe, g, i, 4)
                wh, wl = w_rows(w_hi, g % RING), w_rows(w_lo, g % RING)
                for a in range(2):
                    for k in range(LT):
                        cols = slice(KVH * a, KVH * a + NOPE)
                        product(ps[:, 2, S * a:S * a + S],
                                [(wh[:, k, cols], a_hi[:, 1, k, :]), (wh[:, k, cols], a_lo[:, 1, k, :]),
                                 (wl[:, k, cols], a_hi[:, 1, k, :])], k == 0, k == LT - 1)
                if not (h == 0 and i is None):
                    pe.wait_ge(v_done, val(h, i, 2))
                for t in range(TT):
                    for k in range(LT):
                        def values(w):
                            return w[:, k, :].rearrange("p (a n) -> p a n", a=2)[:, :, NOPE:KVH]
                        toks = slice(P * t, P * t + P)
                        ins = product(ps[:, 3, S * t:S * t + S].rearrange("p (a n) -> p a n", a=2),
                                      three(a_hi[:, 1, k, toks], a_lo[:, 1, k, toks], values(wh), values(wl)),
                                      k == 0, k == LT - 1)
                ins.then_inc(group_used, 1)

            def pair_out(h, i=None):
                pe.wait_ge(prob_done, val(7 * h + 7, i, 14))
                for a in range(2):
                    if not (h == 0 and i is None):
                        base = norm_counts(4) + 2 * h - 2 + a + 1
                        pe.wait_ge(xlo_done, val(base, i, 4))
                    for s in range(3):
                        ins = pe.transpose(ps[:, 6 + a, P * s:P * s + P], prob[:, a, KEYS[s]], ident[:, :])
                    ins.then_inc(prob_tr, 1)
                for a in range(2):
                    pe.wait_ge(pT_done, val(2 * h + a + 1, i, 4))
                    pe.matmul(ps[:, 6 + a, 0:S], v_sb[:, 0, VD * a:VD * a + VD], pT[:, a, 0:S], start=True, stop=False)
                    pe.matmul(ps[:, 6 + a, P:S], v_sb[:, 1, VD * a:VD * a + VD], pT[:, a, S:S + P], start=False,
                              stop=True).then_inc(pv_done, 1)

            def pair_queries(h, i=None):
                pe.wait_ge(q_rot_done, val(4 * h + 4, i, 8))
                for t in range(TT):
                    ins = pe.transpose(ps[:, 1, S + P * t:S + P * t + P], q_rot[:, t, :], ident[:, :])
                ins.then_inc(qr_tr, 1)

            def pair_scores(h, i=None):
                pe.wait_ge(qk_done, val(2 * h + 2, i, 4))
                pe.wait_ge(qr_done, val(h + 1, i, 2))
                if h == 0 and i is None:
                    pe.wait_ge(kr_done, 1)
                for a in range(2):
                    r = slice(ROPE * a, ROPE * a + ROPE)
                    for q, cols in enumerate((slice(0, P), slice(P, 3 * P))):
                        toks = slice(P * q, P * q + P)
                        keys = P * (q + 1)
                        pe.matmul(ps[:, 4 + a, cols], qT[:, a, toks], kT[:, a, 0:keys], start=True, stop=False)
                        ins = pe.matmul(ps[:, 4 + a, cols], qrT[r, toks], krT[r, 0:keys], start=False, stop=True)
                    ins.then_inc(scored, 1)

            KEYS = (slice(0, P), slice(P, 2 * P), slice(2 * P, 3 * P))
            pair_project(G_ATT, 0)
            pair_queries(0)
            pair_scores(0)
            with pe.Fori(0, (PAIRS - 2) // 2) as i:
                for u in range(2):
                    pair_project(G_ATT + 2 + 2 * u, 1 + u, i)
                    pair_queries(1 + u, i)
                    pair_out(u, i)
                    pair_scores(1 + u, i)
            pair_project(G_ATT + 2 * (PAIRS - 1), PAIRS - 1)
            pair_queries(PAIRS - 1)
            pair_out(PAIRS - 2)
            pair_scores(PAIRS - 1)
            pair_out(PAIRS - 1)

            square(G_WO, norm_counts(4), ADDED[3])
            chunks_to_ffn(5, ADDED[3])
            ffn(1, G_FFN1, norm_counts(5), ADDED[5])


ADDED = {2: TT + TT * CC, 3: TT + TT * CC * (1 + FC), 5: TT + TT * CC * (2 + FC), 6: TT + TT * CC * (2 + 2 * FC)}
XT = {0: 0, 1: KT // 2, 2: KT, 3: 3 * KT // 2, 5: 2 * KT}
TBANK = {0: (0, 2, 4, 6), 2: (4, 6, 2, 4), 3: (2, 2, 2, 4), 5: (4, 6, 2, 4)}
RSTD = {0: 1, 2: 3, 3: 4, 5: 7}
SQ = {0: 1, 2: 2, 3: 3, 5: 6}
AHI = {0: 0, 1: 2 * FC + 2 * LT}

_INS = ['x', 'positions', 'attn_norm_g', 'ffn_norm_g', 'final_norm_g', 'conv_w_pw1', 'conv_b_pw1', 'conv_w_dw',
        'conv_b_dw', 'conv_ln_g', 'conv_ln_b', 'conv_w_pw2', 'conv_b_pw2', 'mla_w_dq', 'mla_q_norm_g', 'mla_w_uq',
        'mla_w_dkv', 'mla_kv_norm_g', 'mla_w_ukv', 'mla_w_o', 'ffn_w_gate', 'ffn_w_up', 'ffn_w_down']


def kernel(**inputs):
    import concourse.bacc as _bacc
    from concourse.bass_utils import run_bass_kernel_spmd as _run

    nc = _bacc.Bacc("TRN2", target_bir_lowering=False, num_devices=1)
    arrays, args = {}, []
    named = [(name, np.ascontiguousarray(inputs[name])) for name in _INS]
    power = np.arange(0, ROPE, 2, dtype=np.float32) / np.float32(ROPE)
    freqs = np.float32(1) / (10000.0 ** power.astype(np.float64)).astype(np.float32)
    named.append(("inv_freq", freqs.reshape(1, ROPE // 2)))
    for name, a in named:
        arrays[f"in_{name}_dram"] = a
        args.append(nc.dram_tensor(f"in_{name}_dram", a.shape, mybir.dt.from_np(a.dtype), kind="ExternalInput").ap())
    args.append(nc.dram_tensor("out_0_dram", (1, S, D), F32, kind="ExternalOutput").ap())
    encoder(nc, *args)
    r = _run(nc, [arrays], core_ids=[0])
    return r.results[0]["out_0_dram"]
```

```python
from contextlib import ExitStack

import numpy as np
import concourse.bass as bass
from concourse import mybir
from concourse.alu_op_type import AluOpType as ALU

F32 = mybir.dt.float32
F32R = mybir.dt.float32r
I32 = mybir.dt.int32
ACT = mybir.ActivationFunctionType
AX = mybir.AxisListType

P = 128
D = 2048
S = 256
TT = S // P
KT = D // P
DFF = 5632
CH = 512
GK = 4
KG = KT // GK
RING = 4
LANDED = 64
EPS = 1e-6

TAPS = 31
HALO = TAPS - 1
CC = D // CH
CM = CH // P
HALVES = 2 * CC
PE_TAPS = 3
PE_TAPS_LAST = 13
DVE_STEPS = 2 * (TAPS - PE_TAPS)

HEADS = 16
NOPE = 128
ROPE = 64
VD = 128
LORA = 512
LT = LORA // P
QH = NOPE + ROPE
KVH = NOPE + VD
PAIRS = HEADS // 2
SM_SCALE = float(QH) ** -0.5
NEG = -1e30
FC = DFF // CH

G_PW1 = 0
G_PW2 = G_PW1 + 2 * CC * KG
G_FFN0 = G_PW2 + CC * KG
G_DQ = G_FFN0 + 3 * FC * KG
G_DKV = G_DQ + KG
G_KR = G_DKV + KG
G_ATT = G_KR + 1
G_WO = G_ATT + 2 * PAIRS
G_FFN1 = G_WO + CC * KG
G_END = G_FFN1 + 3 * FC * KG
POOL_LO = G_FFN0 + 3

R_ATTN, R_FFN, R_LNG, R_LNB, R_BDW, R_QN, R_KVN = 0, 32, 64, 80, 96, 112, 116
R_ALL = 120

PI_DIGITS = 314159265358979323846264338327950288419716939937510582097494
TWO_PI = 2 * PI_DIGITS / 10 ** 59
TURN_BITS = 12
TURN_PIECES = 5


def turn_pieces():
    q = 10 ** 59 * 2 ** (TURN_BITS * TURN_PIECES) // (2 * PI_DIGITS)
    out = []
    for j in range(TURN_PIECES):
        shift = TURN_BITS * (TURN_PIECES - 1 - j)
        out.append(float(((q >> shift) & (2 ** TURN_BITS - 1)) * 2.0 ** (shift - TURN_BITS * TURN_PIECES)))
    return out


def encoder(nc, x, positions, attn_norm_g, ffn_norm_g, final_norm_g, conv_w_pw1, conv_b_pw1, conv_w_dw,
            conv_b_dw, conv_ln_g, conv_ln_b, conv_w_pw2, conv_b_pw2, mla_w_dq, mla_q_norm_g, mla_w_uq,
            mla_w_dkv, mla_kv_norm_g, mla_w_ukv, mla_w_o, ffn_w_gate, ffn_w_up, ffn_w_down, inv_freq, out):
    ctx = ExitStack()
    with ctx:
        def sb(name, shape, dt=F32):
            return ctx.enter_context(nc.sbuf_tensor(name, shape, dt))

        def sem(name):
            return ctx.enter_context(nc.semaphore(name))

        resid = sb("resid", [P, TT, D])
        ytmp = sb("ytmp", [P, TT, D])
        x_hi = sb("x_hi", [P, KT, S], F32R)
        x_lo = sb("x_lo", [P, KT, S], F32R)
        raw = sb("raw", [P, RING, GK * CH])
        w_hi = sb("w_hi", [P, RING, GK * CH], F32R)
        w_lo = sb("w_lo", [P, RING, GK * CH], F32R)
        a_hi = sb("a_hi", [P, 2, LT, S], F32R)
        a_lo = sb("a_lo", [P, 2, LT, S], F32R)
        row_bc = sb("row_bc", [P, D])
        diag_more = sb("diag_more", [P, PE_TAPS_LAST - PE_TAPS - 2 * TT, P])
        scratch = sb("scratch", [P, 3584])
        ident = sb("ident", [P, P])
        tap_col = sb("tap_col", [P, TAPS, KT])
        vec_col = sb("vec_col", [P, R_ALL])
        bias1_col = sb("bias1_col", [P, 2 * KT])
        rlat = sb("rlat", [P, 2])
        rcomb = sb("rcomb", [P, 2])
        ssq = sb("ssq", [P, TT, CC])
        cosT = sb("cosT", [P, S])
        sinT = sb("sinT", [P, S])
        freq = sb("freq", [P, 1])
        stat = sb("stat", [P, 2])
        rstd = sb("rstd", [P, 2])
        newton = sb("newton", [P, 2])
        bn = sb("bn", [P, TT, HALVES, 6])
        mv = sb("mv", [P, TT, 2])
        shift = sb("shift", [P, TT])
        nmax = sb("nmax", [P, 4])
        esum = sb("esum", [P, 4])
        erec = sb("erec", [P, 4])
        ps = ctx.enter_context(nc.psum_tensor("ps", [P, 8, 512], F32))

        vec_row = scratch[0:R_ALL, 1024:1024 + P]
        bias1_row = scratch[0:2 * KT, 1024 + P:1024 + 2 * P]
        tap_row = scratch[0:4 * TAPS, 1024 + 2 * P:1024 + 6 * P].rearrange("p (q c) -> p q c", q=4)
        ang, a_top, a_low, frac, turns, whole, pos_f, pos_i = [scratch[:, S * n:S * n + S] for n in range(8)]
        vbuf = scratch[:, 0:CM * (S + HALO)].rearrange("p (m s) -> p m s", m=CM)
        o = CM * (S + HALO)
        acc = scratch[:, o:o + CM * S].rearrange("p (m s) -> p m s", m=CM)
        glu_sig = scratch[:, o + CM * S:o + 2 * CM * S].rearrange("p (m s) -> p m s", m=CM)
        taps = scratch[:, o + 2 * CM * S:o + 2 * CM * S + TAPS * CM].rearrange("p (w m) -> p w m", m=CM)
        diag = row_bc[:, 0:4 * PE_TAPS * P].rearrange("p (u w c) -> p u w c", u=4, c=P)
        early = [[diag_more[:, w, :] for w in range(PE_TAPS_LAST - PE_TAPS - 2 * TT)] +
                 [ytmp[:, t, D - P * n:D - P * n + P] for t in range(TT) for n in (1, 2)],
                 [row_bc[:, P * w:P * w + P] for w in range(2 * PE_TAPS, 2 * PE_TAPS + PE_TAPS_LAST - PE_TAPS)]]
        late = [[diag[:, mm, w, :] for w in range(PE_TAPS)] for mm in range(2)]
        diag_last = [early[mm] + late[mm] for mm in range(2)]
        order_last = [(mm, w) for mm in range(2) for w in range(PE_TAPS_LAST - PE_TAPS)] + \
                     [(mm, w) for mm in range(2) for w in range(PE_TAPS_LAST - PE_TAPS, PE_TAPS_LAST)]
        z_buf, z_sig, z_act = [scratch[:, 1024 * n:1024 * n + 1024].rearrange("p (b f) -> p b f", b=2)
                               for n in range(3)]
        ff_sig = scratch[:, 0:1024].rearrange("p (t f) -> p t f", t=TT)
        ff_h = scratch[:, 1024:2048].rearrange("p (t f) -> p t f", t=TT)
        qT = scratch[:, 0:512].rearrange("p (a s) -> p a s", a=2)
        kT = scratch[:, 512:1024].rearrange("p (a s) -> p a s", a=2)
        v_sb = scratch[:, 1024:1536].rearrange("p (t f) -> p t f", t=TT)
        q_raw = scratch[:, 1536:1792]
        qrT = scratch[:, 1792:2048]
        prob = scratch[:, 2048:2816].rearrange("p (a f) -> p a f", a=2)
        pT = scratch[:, 2816:3584].rearrange("p (a f) -> p a f", a=2)
        krT = ytmp[:, 1, 1024:1280]
        mask = ytmp[:, 1, 1280:1664]
        rope_a = ytmp[:, 0, 1024:1280]
        rope_b = ytmp[:, 0, 1280:1536]
        lat_junk = ytmp[:, 0, 1024:1536]
        swap = ytmp[:, 1, 1792:1920]
        twice = ytmp[0:ROPE, 0, 1536:1664]
        swap_twice = ytmp[0:ROPE, 0, 1664:1792]
        k_raw = ytmp[0:ROPE, 0, 1792:2048]
        rstd_rows = ytmp[:, 0, 1792:2048].rearrange("p (t c) -> p t c", t=TT)
        c_q = ytmp[:, :, 0:LORA]
        c_kv = ytmp[:, :, LORA:2 * LORA]

        out_t = out[0].rearrange("(t p) d -> p t d", p=P)

        def hi32(ap):
            return ap.bitcast(F32)

        x_in = [sem(f"x_in{t}") for t in range(TT)]
        warm = sem("warm")
        small_in = sem("small_in")
        bias2_in = sem("bias2_in")
        final_g_in = sem("final_g_in")
        raw_in = [sem(f"raw_in{n}") for n in range(RING)]
        hi_done = sem("hi_done")
        lo_pool = sem("lo_pool")
        lo_dve = sem("lo_dve")
        group_used = sem("group_used")
        consts = sem("consts")
        vec_t = sem("vec_t")
        vec_done = sem("vec_done")
        chain = sem("chain")
        turn_ready = sem("turn_ready")
        rope_ready = sem("rope_ready")
        sq_act = sem("sq_act")
        rstd_ready = sem("rstd_ready")
        y_act = sem("y_act")
        y_dve = sem("y_dve")
        x_tr = sem("x_tr")
        xhi_done = sem("xhi_done")
        xlo_done = sem("xlo_done")
        glu_sig_done = sem("glu_sig_done")
        glu_done = sem("glu_done")
        conv_step = sem("conv_step")
        diag_done = sem("diag_done")
        row_done = sem("row_done")
        conv_tr = sem("conv_tr")
        z_done = sem("z_done")
        z_sig_done = sem("z_sig_done")
        z_act_done = sem("z_act_done")
        out_added = sem("out_added")
        ff_sig_done = sem("ff_sig_done")
        ff_h_done = sem("ff_h_done")
        ff_tr = sem("ff_tr")
        ahi_done = sem("ahi_done")
        alo_done = sem("alo_done")
        lat_tr = sem("lat_tr")
        kr_raw_done = sem("kr_raw_done")
        kr_twice = sem("kr_twice")
        kr_done = sem("kr_done")
        pos_in = sem("pos_in")
        swaps = sem("swaps")
        q_raw_done = sem("q_raw_done")
        qr_swapped = sem("qr_swapped")
        qr_done = sem("qr_done")
        qk_done = sem("qk_done")
        v_done = sem("v_done")
        scored = sem("scored")
        max_done = sem("max_done")
        exp_done = sem("exp_done")
        prob_done = sem("prob_done")
        prob_tr = sem("prob_tr")
        pT_done = sem("pT_done")
        pv_done = sem("pv_done")
        scaled_g = sem("scaled_g")
        final_block = sem("final_block")
        rows_act = sem("rows_act")
        rows_dve = sem("rows_dve")
        stored = sem("stored")

        def val(n0, i=None, per=0):
            return n0 if i is None else i * per + n0

        def wait_lo(eng, g, i=None, per=0):
            if g < POOL_LO:
                eng.wait_ge(lo_pool, val(g + 1, i, per))
            else:
                eng.wait_ge(lo_dve, val(g - POOL_LO + 1, i, per))

        def norm_counts(n):
            return KT * n

        block = ctx.enter_context(nc.Block())

        @block.sync
        def _(sp):
            def load(src, g, i=None, per=0, cols=CH, tiles=GK):
                slot = g % RING
                if g >= RING:
                    wait_lo(sp, g - RING, i, per)
                sp.dma_start(raw[:, slot, 0:tiles * cols].rearrange("p (k n) -> p k n", k=tiles),
                             src).then_inc(raw_in[slot], LANDED)

            def tile_rows(w, rows, cols):
                return w.rearrange("(k p) n -> p k n", p=P)[:, rows, cols]

            x_t = x[0].rearrange("(t p) d -> p t d", p=P)
            for t in range(TT):
                sp.dma_start(resid[:, t, :], x_t[:, t, :]).then_inc(x_in[t], 16)

            w1 = conv_w_pw1[0].rearrange("(k p) (h n) -> p k h n", p=P, h=2)

            def pw1_loads(c, i=None):
                base = 0 if i is None else i * CH
                for u in range(2):
                    for j in range(KG):
                        g = G_PW1 + 2 * KG * c + KG * u + j
                        slot = g % RING
                        if g >= RING:
                            wait_lo(sp, g - RING, i, 2 * KG)
                        dst = raw[:, slot, :].rearrange("p (k h n) -> p k h n", k=GK, h=2)
                        for h in range(2):
                            if i is None and c == 0 and u == 0 and j == 1 and h == 0:
                                sp.wait_ge(small_in, 16 * 10)
                            sp.dma_start(dst[:, :, h, :],
                                         w1[:, GK * j:GK * j + GK, h, bass.ds(base + CH * c + CH // 2 * u, CH // 2)]
                                         ).then_inc(raw_in[slot], LANDED // 2)
            pw1_loads(0)
            with sp.Fori(0, CC - 1) as i:
                pw1_loads(1, i)

            def square_loads(w, g0):
                with sp.Fori(0, CC) as i:
                    for j in range(KG):
                        load(tile_rows(w, slice(GK * j, GK * j + GK), bass.ds(i * CH, CH)), g0 + j, i, KG)
            square_loads(conv_w_pw2[0], G_PW2)

            def ffn_loads(l, g0):
                wg, wu, wd = ffn_w_gate[l], ffn_w_up[l], ffn_w_down[l]

                def up(g, c, i=None, per=0):
                    base = 0 if i is None else i * CH
                    for n, w in ((0, wg), (1, wu)):
                        for j in range(KG):
                            load(tile_rows(w, slice(GK * j, GK * j + GK), bass.ds(base + CH * c, CH)),
                                 g + KG * n + j, i, per)

                def down(g, c, i=None, per=0):
                    base = 0 if i is None else i * CH
                    for n in range(CC):
                        load(wd[bass.ds(base + CH * c, CH), CH * n:CH * n + CH].rearrange("(k p) n -> p k n", p=P),
                             g + n, i, per)
                up(g0, 0)
                with sp.Fori(0, FC - 1) as i:
                    up(g0 + 2 * KG, 1, i, 3 * KG)
                    down(g0 + 4 * KG, 0, i, 3 * KG)
                down(g0 + 3 * KG * FC - KG, FC - 1)
            ffn_loads(0, G_FFN0)

            for j in range(KG):
                load(tile_rows(mla_w_dq[0], slice(GK * j, GK * j + GK), slice(0, CH)), G_DQ + j)
            for j in range(KG):
                load(tile_rows(mla_w_dkv[0], slice(GK * j, GK * j + GK), slice(0, CH)), G_DKV + j)
            load(tile_rows(mla_w_dkv[0], slice(0, KT), slice(LORA, LORA + ROPE)), G_KR, cols=ROPE, tiles=KT)

            def pair_loads(g, h, i=None, per=0, step=0):
                base = 0 if i is None else i * step
                slot = g % RING
                wait_lo(sp, g - RING, i, per)
                dst = raw[:, slot, 0:LT * 2 * QH].rearrange("p (k n) -> p k n", k=LT)
                for part, r0, r1 in ((slice(0, 2 * NOPE), 0, NOPE), (slice(2 * NOPE, 2 * QH), NOPE, QH)):
                    for a in range(2):
                        col = base * (2 * QH) + 2 * QH * h + QH * a + r0
                        n0 = part.start + (r1 - r0) * a
                        sp.dma_start(dst[:, :, n0:n0 + r1 - r0], tile_rows(mla_w_uq[0], slice(0, LT), bass.ds(col, r1 - r0))
                                     ).then_inc(raw_in[slot], LANDED // 4)
                load(tile_rows(mla_w_ukv[0], slice(0, LT), bass.ds(base * (2 * KVH) + 2 * KVH * h, 2 * KVH)),
                     g + 1, i, per)
            pair_loads(G_ATT, 0)
            with sp.Fori(0, (PAIRS - 2) // 2) as i:
                for u in range(2):
                    pair_loads(G_ATT + 2 + 2 * u, 1 + u, i, 4, 2)
            pair_loads(G_ATT + 2 * (PAIRS - 1), PAIRS - 1)
            square_loads(mla_w_o[0], G_WO)
            ffn_loads(1, G_FFN1)

            for t in range(TT):
                sp.wait_ge(rows_dve, t + 1)
                sp.dma_start(out_t[:, t, D // 2:], ytmp[:, t, D // 2:]).then_inc(stored, 16)
            sp.wait_ge(stored, 16 * 2 * TT)

        @block.gpsimd
        def _(pool):
            pool.memset(ident[:, :], 0.0).then_inc(consts, 1)
            pool.wait_ge(consts, 1)
            pool.affine_select(out=ident[:, :], in_=ident[:, :], compare_op=ALU.not_equal, fill=1.0, base=0,
                               pattern=[[-1, P]], channel_multiplier=1).then_inc(consts, 1)
            def lo(g, i=None, per=0):
                pool.wait_ge(hi_done, val(g + 1, i, per))
                pool.tensor_tensor(w_lo[:, g % RING, :], raw[:, g % RING, :], hi32(w_hi[:, g % RING, :]),
                                   ALU.subtract).then_inc(lo_pool, 1)
            for g in range(RING):
                lo(g)
            with pool.Fori(0, G_PW2 // RING) as i:
                for g in range(RING):
                    lo(RING + g, i, RING)
            for b in range(KT // 2):
                pool.wait_ge(xhi_done, norm_counts(1) + 2 * b + 2)
                pool.tensor_tensor(x_lo[:, 2 * b:2 * b + 2, :].rearrange("p k s -> p (k s)"), z_act[:, b % 2, :],
                                   hi32(x_hi[:, 2 * b:2 * b + 2, :]).rearrange("p k s -> p (k s)"),
                                   ALU.subtract).then_inc(xlo_done, 2)
            with pool.Fori(0, CC - 1) as i:
                for g in range(RING):
                    lo(G_PW2 + RING + g, i, RING)
            for g in range(G_FFN0, POOL_LO):
                lo(g)
            pool.wait_ge(rstd_ready, RSTD[3])
            half = ROPE // 2
            eye = ident[:, :].rearrange("p (h r) -> p h r", h=2)
            swap2 = swap.rearrange("p (h r) -> p h r", h=2)
            pool.tensor_scalar(swap2[:, :, 0:half], eye[:, :, half:ROPE], -1.0, None, ALU.mult).then_inc(swaps, 1)
            pool.tensor_copy(swap2[:, :, half:ROPE], eye[:, :, 0:half]).then_inc(swaps, 1)
            pool.wait_ge(swaps, 2)
            for n in range(2):
                pool.tensor_copy(twice[:, ROPE * n:ROPE * n + ROPE], ident[0:ROPE, 0:ROPE]).then_inc(swaps, 1)
                pool.tensor_copy(swap_twice[:, ROPE * n:ROPE * n + ROPE], swap[0:ROPE, 0:ROPE]).then_inc(swaps, 1)
            pool.memset(mask, 0.0).then_inc(swaps, 1)
            pool.wait_ge(swaps, 7)
            pool.memset(mask[0:64, 64:128], NEG).then_inc(swaps, 1)
            pool.memset(mask[0:64, 320:384], NEG).then_inc(swaps, 1)
            pool.wait_ge(final_g_in, 16)
            for idx, (n, t) in enumerate(FINAL):
                pool.wait_ge(out_added, ADDED[5] + TT * CC * (FC - 1) + idx + 1)
                pool.tensor_tensor(ytmp[:, t, CH * n:CH * n + CH], resid[:, t, CH * n:CH * n + CH],
                                   row_bc[:, CH * n:CH * n + CH], ALU.mult).then_inc(scaled_g, 1)

        @block.scalar
        def _(act):
            def rows(v):
                return v.rearrange("(t p) -> t p", p=P)

            loads = [(vec_row[R_ATTN:R_ATTN + 32, :], attn_norm_g.rearrange("l (t p) -> (l t) p", p=P)),
                     (vec_row[R_FFN:R_FFN + 32, :], ffn_norm_g.rearrange("l (t p) -> (l t) p", p=P)),
                     (vec_row[R_LNG:R_LNG + KT, :], rows(conv_ln_g[0])), (vec_row[R_LNB:R_LNB + KT, :], rows(conv_ln_b[0])),
                     (vec_row[R_BDW:R_BDW + KT, :], rows(conv_b_dw[0])), (vec_row[R_QN:R_QN + LT, :], rows(mla_q_norm_g[0])),
                     (vec_row[R_KVN:R_KVN + LT, :], rows(mla_kv_norm_g[0])), (bias1_row, rows(conv_b_pw1[0])),
                     (tap_row, conv_w_dw[0].rearrange("w (t p) -> (w t) p", p=P).rearrange("(q r) p -> r q p", q=4)),
                     (freq[:, :], inv_freq)]
            for dst, src in loads:
                act.dma_start(dst, src).then_inc(small_in, 16)
            act.wait_ge(consts, 2)
            act.activation(esum[:, 0:1], ident[:, 0:1], ACT.Square).then_inc(warm, 1)
            act.wait_ge(warm, 1)

            def hi(g, i=None, per=0):
                slot = g % RING
                act.wait_ge(raw_in[slot], val(LANDED * (g // RING + 1), i, LANDED * per // RING))
                if g >= RING:
                    act.wait_ge(group_used, val(g - RING + 1, i, per))
                act.activation(w_hi[:, slot, :], raw[:, slot, :], ACT.Copy).then_inc(hi_done, 1)

            def first_norm(gain):
                act.wait_ge(x_in[0], 16)
                act.activation(ytmp[:, 0, :], resid[:, 0, :], ACT.Square, accum_out=stat[:, 0:1]).then_inc(sq_act, 1)
                act.dma_start(row_bc[:, :], conv_b_pw2[0:1, :].to_broadcast([P, D])).then_inc(bias2_in, 16)
                act.wait_ge(rstd_ready, 1)
                act.activation(ytmp[:, 0, :], resid[:, 0, :], ACT.Copy, scale=rstd[:, 0:1]).then_inc(y_act, 1)
                hi(0)
                act.wait_ge(vec_done, 1)
                for n in range(CC):
                    chunk_hi(0, n, gain)
                    if n == 0:
                        hi(1)

            def chunk_hi(norm, n, gain):
                for kk in range(GK):
                    k = GK * n + kk
                    if kk % 2 == 0:
                        act.wait_ge(x_tr, XT[norm] + k // 2 + 1)
                    act.activation(x_hi[:, k, :], ps[:, TBANK[norm][n] + kk // 2, S * (kk % 2):S * (kk % 2) + S],
                                   ACT.Copy, scale=vec_col[:, gain + k:gain + k + 1]).then_inc(xhi_done, 1)

            def norm(norm, gain, done=0):
                for n in range(done, CC):
                    chunk_hi(norm, n, gain)
                act.wait_ge(out_added, ADDED[norm])
                act.activation(ytmp[:, 0, :], resid[:, 0, :], ACT.Square, accum_out=stat[:, 0:1]).then_inc(sq_act, 1)

            first_norm(R_ATTN)
            hi(2)
            hi(3)
            act.wait_ge(vec_done, 3)

            def diagonals(s, i=None):
                for mm in range(2):
                    for w in range(PE_TAPS):
                        col = bass.ds((0 if i is None else i * CM) + 2 * s + mm, 1)
                        act.activation(diag[:, 2 * (s % 2) + mm, w, :], ident[:, :], ACT.Copy,
                                       scale=tap_col[:, w, col]).then_inc(diag_done, 1)

            def diagonals_last(which):
                for mm, w in which:
                    act.activation(diag_last[mm][w], ident[:, :], ACT.Copy,
                                   scale=tap_col[:, w, KT - 2 + mm:KT - 1 + mm]).then_inc(diag_done, 1)

            def rows_out(s, i=None):
                base = 0 if i is None else i * CH
                for t in range(TT):
                    act.wait_ge(conv_tr, val(TT * s + t + 1, i, 2 * TT))
                    act.activation(ytmp[:, t, bass.ds(base + CH // 2 * s, CH // 2)], ps[:, 4 + 2 * (s % 2) + t, 0:CH // 2],
                                   ACT.Copy).then_inc(row_done, 1)

            def conv_half(s, i=None):
                u = s % 2
                if s >= HALVES - 2:
                    n = PE_TAPS_LAST - PE_TAPS
                    diagonals_last(order_last[n * u:n * u + n])
                for j in range(KG):
                    hi(G_PW1 + KG * s + 4 + j, i, 2 * KG)
                act.wait_ge(group_used, val(G_PW1 + KG * s + KG, i, 2 * KG))
                if s >= 2:
                    act.wait_ge(glu_done, val((CM + 1) * (s // 2 - 1) + 2 * u + 3, i, CM + 1))
                for mm in range(2):
                    col = bass.ds((0 if i is None else i * CM) + KT + 2 * s + mm, 1)
                    act.activation(glu_sig[:, 2 * u + mm, :], ps[:, 2 * u + 1, S * mm:S * mm + S], ACT.Sigmoid,
                                   bias=bias1_col[:, col]).then_inc(glu_sig_done, 1)
                if s == 0:
                    act.wait_ge(out_added, TT)
                if s < HALVES - 1:
                    diagonals(s, i)
                if s > 0:
                    rows_out(s - 1, i)
            conv_half(0)
            conv_half(1)
            with act.Fori(0, CC - 2) as i:
                conv_half(2, i)
                conv_half(3, i)
            conv_half(HALVES - 2)
            conv_half(HALVES - 1)
            diagonals_last(order_last[2 * (PE_TAPS_LAST - PE_TAPS):])
            rows_out(HALVES - 1)

            act.wait_ge(rstd_ready, 2)
            for c in range(CC):
                act.activation(ytmp[:, 0, CH * c:CH * c + CH], ytmp[:, 0, CH * c:CH * c + CH], ACT.Identity,
                               bias=shift[:, 0:1], scale=rstd[:, 0:1]).then_inc(y_act, 1)

            def z_sigmoid(b):
                act.wait_ge(z_done, 2 * b + 2)
                act.activation(z_sig[:, b % 2, :], z_buf[:, b % 2, :], ACT.Sigmoid).then_inc(z_sig_done, 1)
            z_sigmoid(0)
            for b in range(KT // 2):
                if b < KT // 2 - 1:
                    z_sigmoid(b + 1)
                act.wait_ge(z_act_done, b + 1)
                act.activation(x_hi[:, 2 * b:2 * b + 2, :].rearrange("p k s -> p (k s)"), z_act[:, b % 2, :],
                               ACT.Copy).then_inc(xhi_done, 2)

            def square(g0, have4=False):
                if have4:
                    for j in range(3):
                        hi(g0 + 4 + j)
                    with act.Fori(0, CC - 1) as i:
                        for j in range(KG):
                            hi(g0 + 7 + j, i, KG)
                else:
                    with act.Fori(0, CC) as i:
                        for j in range(KG):
                            hi(g0 + 3 + j, i, KG)

            act.wait_ge(xlo_done, norm_counts(1) + KT)
            act.dma_start(pos_i.bitcast(I32), positions[0:1, :].to_broadcast([P, S])).then_inc(pos_in, 16)
            square(G_PW2, have4=True)

            def ffn(l, g0):
                hi(g0 + 3)

                def gate_sig(used, i=None):
                    for t in range(TT):
                        act.wait_ge(group_used, val(used, i, 12))
                        act.activation(ff_sig[:, t, :], ps[:, t, :], ACT.Sigmoid,
                                       scale=rstd[:, t:t + 1]).then_inc(ff_sig_done, 1)

                def hidden(c0, i=None):
                    for b in range(2):
                        act.wait_ge(ff_tr, val(2 * (FC * l + c0) + b + 1, i, 2))
                        act.activation(a_hi[:, 0, 2 * b:2 * b + 2, :].rearrange("p k s -> p (k s)"), ps[:, 4 + b, :],
                                       ACT.Copy).then_inc(ahi_done, 1)
                for j in range(4, 8):
                    hi(g0 + j)
                act.wait_ge(rstd_ready, RSTD[(2, 5)[l]])
                gate_sig(g0 + KG)
                for j in range(8, 11):
                    hi(g0 + j)
                with act.Fori(0, FC - 1) as i:
                    for j in range(11, 15):
                        hi(g0 + j, i, 12)
                    hidden(0, i)
                    gate_sig(g0 + 12, i)
                    for j in range(15, 23):
                        hi(g0 + j, i, 12)
                hidden(FC - 1)
                hi(g0 + 3 * KG * FC - 1)
                if l == 0:
                    end = g0 + 3 * KG * FC
                    hi(end)
                    chunk_hi(3, 0, R_ATTN + KT)
                    hi(end + 1)
                    chunk_hi(3, 1, R_ATTN + KT)
                    hi(end + 2)

            norm(2, R_FFN)
            ffn(0, G_FFN0)

            norm(3, R_ATTN + KT, done=2)
            for g in (3, 4, 5, 6):
                hi(G_DQ + g)

            def latent(which, bank, gain):
                dst = c_q if which == 0 else c_kv
                act.wait_ge(rstd_ready, RSTD[3])
                act.activation(dst[:, 0, :], ps[:, bank, :], ACT.Square, scale=rstd[:, 0:1],
                               accum_out=stat[:, 0:1]).then_inc(sq_act, 1)
                act.wait_ge(rstd_ready, 5 + which)
                act.activation(dst[:, 0, :], ps[:, bank, :], ACT.Copy, scale=rcomb[:, 0:1]).then_inc(y_act, 1)

            def latent_hi(which, bank, gain):
                for k in range(LT):
                    if k % 2 == 0:
                        act.wait_ge(lat_tr, 2 * which + k // 2 + 1)
                    act.activation(a_hi[:, which, k, :], ps[:, bank + k // 2, S * (k % 2):S * (k % 2) + S], ACT.Copy,
                                   scale=vec_col[:, gain + k:gain + k + 1]).then_inc(ahi_done, 1)
            act.wait_ge(group_used, G_DQ + KG)
            latent(0, 0, R_QN)
            for g in (7, 8, 9, 10):
                hi(G_DQ + g)
            act.wait_ge(turn_ready, 2)
            act.activation(cosT[:, :], cosT[:, :], ACT.Sin).then_inc(rope_ready, 1)
            act.activation(sinT[:, :], sinT[:, :], ACT.Sin).then_inc(rope_ready, 1)
            act.wait_ge(group_used, G_DKV + KG)
            latent(1, 2, R_KVN)
            latent_hi(0, 5, R_QN)
            latent_hi(1, 2, R_KVN)
            hi(G_DQ + 11)

            def pair_project(g, h, i=None):
                hi(g + 3, i, 4)
                act.wait_ge(group_used, val(g + 1, i, 4))
                act.activation(qT.rearrange("p a s -> p (a s)"), ps[:, 0, :], ACT.Copy).then_inc(qk_done, 1)
                hi(g + 4, i, 4)
                act.wait_ge(group_used, val(g + 2, i, 4))
                act.activation(kT.rearrange("p a s -> p (a s)"), ps[:, 2, :], ACT.Copy).then_inc(qk_done, 1)

            def pair_out(h, i=None):
                for a in range(2):
                    act.wait_ge(prob_tr, val(2 * h + a + 1, i, 4))
                    act.activation(pT[:, a, :], ps[:, 6 + a, 0:3 * P], ACT.Copy).then_inc(pT_done, 1)
                for a in range(2):
                    act.wait_ge(pv_done, val(2 * h + a + 1, i, 4))
                    dst = x_hi[:, 2 * h + a, :] if i is None else \
                        x_hi[:, bass.ds(i * 4 + 2 * h + a, 1), :].rearrange("p k s -> p (k s)")
                    act.activation(dst, ps[:, 6 + a, 0:S], ACT.Copy).then_inc(xhi_done, 1)

            def pair_exp(h, i=None):
                for a in range(2):
                    for q, (lo_, hi_) in enumerate(((0, P), (P, 3 * P))):
                        act.wait_ge(max_done, val(4 * h + 2 * a + q + 1, i, 8))
                        act.activation(prob[:, a, lo_:hi_], prob[:, a, lo_:hi_], ACT.Exp,
                                       bias=nmax[:, 2 * a + q:2 * a + q + 1],
                                       accum_out=esum[:, 2 * a + q:2 * a + q + 1]).then_inc(exp_done, 1)

            pair_project(G_ATT, 0)
            pair_exp(0)
            with act.Fori(0, (PAIRS - 2) // 2) as i:
                for u in range(2):
                    pair_project(G_ATT + 2 + 2 * u, 1 + u, i)
                    pair_out(u, i)
                    pair_exp(1 + u, i)
            pair_project(G_ATT + 2 * (PAIRS - 1), PAIRS - 1)
            pair_out(PAIRS - 2)
            pair_exp(PAIRS - 1)
            pair_out(PAIRS - 1)

            square(G_WO)
            act.wait_ge(out_added, TT)
            act.dma_start(row_bc[:, :], final_norm_g.rearrange("(a d) -> a d", a=1).to_broadcast([P, D])).then_inc(final_g_in, 16)
            norm(5, R_FFN + KT)
            ffn(1, G_FFN1)

            for idx, (n, t) in enumerate(FINAL):
                act.wait_ge(out_added, ADDED[5] + TT * CC * (FC - 1) + idx + 1)
                act.wait_ge(sq_act, SQ[5] + idx)
                act.activation(ff_sig[:, t, :], resid[:, t, CH * n:CH * n + CH], ACT.Square,
                               accum_out=ssq[:, t, n:n + 1]).then_inc(sq_act, 1)
                if (n, t) in TILE_END:
                    act.wait_ge(scaled_g, idx + 1)
                    act.wait_ge(rstd_ready, RSTD[6] + t)
                    act.activation(ytmp[:, t, 0:D // 2], ytmp[:, t, 0:D // 2], ACT.Copy,
                                   scale=rstd[:, t:t + 1]).then_inc(rows_act, 1)
                    act.wait_ge(rows_act, t + 1)
                    act.dma_start(out_t[:, t, 0:D // 2], ytmp[:, t, 0:D // 2]).then_inc(stored, 16)

        @block.vector
        def _(dve):
            links = [0]

            def link(ins):
                links[0] += 1
                ins.then_inc(chain, 1)
                dve.wait_ge(chain, links[0])

            def lo(g, i=None, per=0):
                dve.wait_ge(hi_done, val(g + 1, i, per))
                dve.tensor_tensor(w_lo[:, g % RING, :], raw[:, g % RING, :], hi32(w_hi[:, g % RING, :]),
                                  ALU.subtract).then_inc(lo_dve, 1)

            def inv_sqrt(root=rstd, c=slice(0, TT)):
                link(dve.tensor_scalar(newton[:, c].bitcast(I32), stat[:, c].bitcast(I32), 1, None, ALU.logical_shift_right))
                link(dve.tensor_scalar(root[:, c].bitcast(I32), newton[:, c].bitcast(I32), -1.0, float(0x5F3759DF),
                                       ALU.mult, ALU.add))
                for step in range(3):
                    link(dve.scalar_tensor_tensor(newton[:, c], root[:, c], -0.5, root[:, c], ALU.mult, ALU.mult))
                    link(dve.tensor_tensor(newton[:, c], newton[:, c], stat[:, c], ALU.mult))
                    last = dve.scalar_tensor_tensor(root[:, c], newton[:, c], 1.5, root[:, c], ALU.add, ALU.mult)
                    if step < 2:
                        link(last)
                return last

            def mean_square(n, width):
                dve.wait_ge(sq_act, n)
                link(dve.tensor_scalar(stat[:, :], stat[:, :], 1.0 / width, EPS, ALU.mult, ALU.add))

            def chunk_lo(norm, n, gain):
                for kk in range(GK):
                    k = GK * n + kk
                    if kk % 2 == 0:
                        dve.wait_ge(xhi_done, norm_counts(norm) + k + 2)
                    dve.scalar_tensor_tensor(x_lo[:, k, :], ps[:, TBANK[norm][n] + kk // 2, S * (kk % 2):S * (kk % 2) + S],
                                             vec_col[:, gain + k:gain + k + 1], hi32(x_hi[:, k, :]),
                                             ALU.mult, ALU.subtract).then_inc(xlo_done, 1)

            def square_sum(norm):
                link(dve.tensor_tensor_reduce(out=ytmp[:, 1, :], in0=resid[:, 1, :], in1=resid[:, 1, :], scale=1.0,
                                              scalar=0.0, op0=ALU.mult, op1=ALU.add, accum_out=stat[:, 1:2]))
                mean_square(SQ[norm], D)
                inv_sqrt().then_inc(rstd_ready, 1)

            def first_norm(gain):
                square_sum(0)
                dve.wait_ge(rstd_ready, RSTD[0])
                dve.tensor_scalar(ytmp[:, 1, :], resid[:, 1, :], rstd[:, 1:2], None, ALU.mult).then_inc(y_dve, 1)
                dve.wait_ge(vec_t, 1)
                dve.tensor_copy(vec_col[:, :], ps[:, 6, 0:R_ALL]).then_inc(vec_done, 1)
                dve.tensor_copy(bias1_col[:, :], ps[:, 6, P:P + 2 * KT]).then_inc(vec_done, 1)
                dve.tensor_copy(tap_col[:, :, :].rearrange("p w t -> p (w t)"), ps[:, 7, 0:TAPS * KT]).then_inc(vec_done, 1)
                dve.wait_ge(vec_done, 3)
                for n in range(CC):
                    chunk_lo(0, n, gain)

            def norm(norm, gain, done=0):
                for n in range(done, CC):
                    chunk_lo(norm, n, gain)
                dve.wait_ge(out_added, ADDED[norm])
                square_sum(norm)

            dve.wait_ge(x_in[1], 16)
            first_norm(R_ATTN)

            dve.wait_ge(bias2_in, 16)
            dve.wait_ge(y_act, 1)
            dve.wait_ge(y_dve, 1)
            for t in range(TT):
                dve.tensor_tensor(resid[:, t, :], resid[:, t, :], row_bc[:, :], ALU.add).then_inc(out_added, 1)

            dve.memset(vbuf[:, :, 0:HALO], 0.0).then_inc(conv_step, 1)

            def conv_chunk(c, i=None):
                steps = 1 + 2 * DVE_STEPS * c
                tile0 = (0 if i is None else i * CM) + CM * c
                dve.wait_ge(conv_step, val(steps, i, 2 * DVE_STEPS))
                dve.tensor_copy(taps, tap_col[:, :, bass.ds(tile0, CM)]).then_inc(glu_done, 1)
                for u in range(2):
                    s = 2 * c + u
                    w0 = PE_TAPS if s < HALVES - 1 else PE_TAPS_LAST
                    dve.wait_ge(group_used, val(G_PW1 + KG * s + KG, i, 2 * KG))
                    if s >= 2:
                        dve.wait_ge(conv_tr, val(TT * (s - 1), i, 2 * TT))
                    for mm in range(2):
                        m = 2 * u + mm
                        dve.wait_ge(glu_sig_done, val(CM * c + m + 1, i, CM))
                        dve.scalar_tensor_tensor(vbuf[:, m, HALO:], ps[:, 2 * u, S * mm:S * mm + S],
                                                 bias1_col[:, bass.ds(tile0 + m, 1)], glu_sig[:, m, :],
                                                 ALU.add, ALU.mult).then_inc(glu_done, 1)
                    for w in range(w0, TAPS):
                        for mm in range(2):
                            m = 2 * u + mm
                            if w == w0:
                                dve.wait_ge(glu_done, val((CM + 1) * c + m + 2, i, CM + 1))
                                dve.tensor_scalar(acc[:, m, :], vbuf[:, m, w:w + S], taps[:, w, m:m + 1],
                                                  vec_col[:, bass.ds(tile0 + R_BDW + m, 1)],
                                                  ALU.mult, ALU.add).then_inc(conv_step, 1)
                                continue
                            dve.wait_ge(conv_step, val(steps + DVE_STEPS * u + 2 * (w - w0) + mm - 1, i,
                                                       2 * DVE_STEPS))
                            dve.scalar_tensor_tensor(acc[:, m, :], vbuf[:, m, w:w + S], taps[:, w, m:m + 1], acc[:, m, :],
                                                     ALU.mult, ALU.add).then_inc(conv_step, 1)
                    if s > 0:
                        row_stats(s - 1, i)

            def row_stats(s, i=None):
                half0 = (0 if i is None else i * 2) + s
                base = (0 if i is None else i * CH) + CH // 2 * s
                for t in range(TT):
                    dve.wait_ge(row_done, val(TT * s + t + 1, i, 2 * TT))
                    last = dve.bn_stats(bn[:, t, bass.ds(half0, 1), :].rearrange("p h s -> p (h s)"),
                                        ytmp[:, t, bass.ds(base, CH // 2)])
                return last
            conv_chunk(0)
            with dve.Fori(0, CC - 2) as i:
                conv_chunk(1, i)
            conv_chunk(CC - 1)

            link(row_stats(HALVES - 1))
            for t in range(TT):
                link(dve.bn_aggr(mv[:, t, :], bn[:, t, :, :].rearrange("p c s -> p (c s)")))
            link(dve.tensor_scalar(stat[:, :], mv[:, :, 1], EPS, None, ALU.add))
            link(inv_sqrt())
            dve.scalar_tensor_tensor(shift[:, :], mv[:, :, 0], -1.0, rstd[:, :], ALU.mult, ALU.mult).then_inc(rstd_ready, 1)
            for c in range(CC):
                dve.tensor_scalar(ytmp[:, 1, CH * c:CH * c + CH], ytmp[:, 1, CH * c:CH * c + CH], mv[:, 1, 0:1],
                                  rstd[:, 1:2], ALU.subtract, ALU.mult).then_inc(y_dve, 1)

            def gain_and_bias(b):
                dve.wait_ge(x_tr, XT[1] + b + 1)
                if b >= 2:
                    dve.wait_ge(z_act_done, b - 1)
                for kk in range(2):
                    k = 2 * b + kk
                    dve.tensor_scalar(z_buf[:, b % 2, S * kk:S * kk + S], ps[:, b, S * kk:S * kk + S],
                                      vec_col[:, R_LNG + k:R_LNG + k + 1], vec_col[:, R_LNB + k:R_LNB + k + 1],
                                      ALU.mult, ALU.add).then_inc(z_done, 1)
            gain_and_bias(0)
            for b in range(KT // 2):
                if b < KT // 2 - 1:
                    gain_and_bias(b + 1)
                dve.wait_ge(z_sig_done, b + 1)
                if b >= 2:
                    dve.wait_ge(xlo_done, norm_counts(1) + 2 * b - 2)
                dve.tensor_tensor(z_act[:, b % 2, :], z_buf[:, b % 2, :], z_sig[:, b % 2, :],
                                  ALU.mult).then_inc(z_act_done, 1)

            def square(g0, split=True):
                with dve.Fori(0, CC // 2) as i:
                    for n in range(2):
                        for j in range(KG if split else 0):
                            lo(g0 + 3 + KG * n + j, i, 2 * KG)
                        for t in range(TT):
                            dve.wait_ge(group_used, val(g0 + KG * n + KG, i, 2 * KG))
                            cols = bass.ds(i * (2 * CH) + CH * n, CH)
                            dve.tensor_tensor(resid[:, t, cols], resid[:, t, cols], ps[:, 2 * n + t, :],
                                              ALU.add).then_inc(out_added, 1)

            dve.wait_ge(out_added, TT)
            dve.wait_ge(xlo_done, norm_counts(1) + KT)
            dve.wait_ge(pos_in, 16)
            link(dve.tensor_copy(pos_f, pos_i.bitcast(I32)))
            link(dve.tensor_scalar(ang, pos_f, freq[:, 0:1], None, ALU.mult))
            link(dve.tensor_scalar(a_top.bitcast(I32), ang.bitcast(I32), -4096, None, ALU.bitwise_and))
            link(dve.tensor_tensor(a_low, ang, a_top, ALU.subtract))
            link(dve.memset(turns, 0.0))
            for piece in reversed(turn_pieces()):
                for part in (a_low, a_top):
                    link(dve.tensor_scalar(whole.bitcast(I32), part, piece, None, ALU.mult))
                    link(dve.scalar_tensor_tensor(frac, part, piece, whole.bitcast(I32), ALU.mult, ALU.subtract))
                    link(dve.tensor_tensor(turns, turns, frac, ALU.add))
            magic = 1.5 * 2.0 ** 23
            for quarter, dst in ((0.25, cosT), (0.0, sinT)):
                link(dve.tensor_scalar(frac, turns, quarter, None, ALU.add))
                link(dve.tensor_scalar(whole, frac, magic, magic, ALU.add, ALU.subtract))
                link(dve.tensor_tensor(frac, frac, whole, ALU.subtract))
                link(dve.tensor_scalar(frac, frac, TWO_PI, None, ALU.mult))
                dve.tensor_scalar(dst[:, :], frac, 3.1415925, -3.1415925, ALU.min, ALU.max).then_inc(turn_ready, 1)
                dve.wait_ge(turn_ready, 1 if dst is cosT else 2)

            square(G_PW2, split=False)

            def final_rows_and_norm():
                for idx, (n, t) in enumerate(FINAL):
                    dve.wait_ge(final_block, idx + 1)
                    cols = slice(CH * n, CH * n + CH)
                    dve.tensor_tensor(resid[:, t, cols], resid[:, t, cols], ps[:, 4 + (2 * n + t) % 4, :],
                                      ALU.add).then_inc(out_added, 1)
                    if (n, t) in TILE_END:
                        dve.wait_ge(sq_act, SQ[5] + idx + 1)
                        link(dve.tensor_reduce(stat[:, t:t + 1], ssq[:, t, :], AX.X, ALU.add))
                        link(dve.tensor_scalar(stat[:, t:t + 1], stat[:, t:t + 1], 1.0 / D, EPS, ALU.mult, ALU.add))
                        inv_sqrt(c=slice(t, t + 1)).then_inc(rstd_ready, 1)
                        dve.wait_ge(rstd_ready, RSTD[6] + t)
                        dve.wait_ge(scaled_g, idx + 1)
                        dve.tensor_scalar(ytmp[:, t, D // 2:], ytmp[:, t, D // 2:], rstd[:, t:t + 1], None,
                                          ALU.mult).then_inc(rows_dve, 1)

            def ffn(l, g0, added):
                def hidden(c0, i=None):
                    for b in range(2):
                        dve.wait_ge(ahi_done, val(AHI[l] + 2 * c0 + b + 1, i, 2))
                        dve.tensor_tensor(a_lo[:, 0, 2 * b:2 * b + 2, :].rearrange("p k s -> p (k s)"), ps[:, 4 + b, :],
                                          hi32(a_hi[:, 0, 2 * b:2 * b + 2, :]).rearrange("p k s -> p (k s)"),
                                          ALU.subtract).then_inc(alo_done, 1)

                def gate_mul(c0, i=None):
                    for t in range(TT):
                        dve.wait_ge(ff_sig_done, val(2 * (FC * l + c0) + t + 1, i, 2))
                        dve.scalar_tensor_tensor(ff_h[:, t, :], ps[:, t, :], rstd[:, t:t + 1], ff_sig[:, t, :],
                                                 ALU.mult, ALU.mult).then_inc(ff_h_done, 1)

                def up_mul(c0, used, i=None):
                    for t in range(TT):
                        dve.wait_ge(group_used, val(used, i, 12))
                        dve.wait_ge(ff_h_done, val(4 * (FC * l + c0) + t + 1, i, 4))
                        dve.scalar_tensor_tensor(ff_h[:, t, :], ps[:, 2 + t, :], rstd[:, t:t + 1], ff_h[:, t, :],
                                                 ALU.mult, ALU.mult).then_inc(ff_h_done, 1)

                def add(n, used, i=None):
                    for t in range(TT):
                        dve.wait_ge(group_used, val(used, i, 12))
                        cols = slice(CH * n, CH * n + CH)
                        dve.tensor_tensor(resid[:, t, cols], resid[:, t, cols], ps[:, 4 + (2 * n + t) % 4, :],
                                          ALU.add).then_inc(out_added, 1)
                lo(g0 + 3)
                for j in range(4, 8):
                    lo(g0 + j)
                gate_mul(0)
                for j in range(8, 11):
                    lo(g0 + j)
                up_mul(0, g0 + 8)
                with dve.Fori(0, FC - 1) as i:
                    for j in range(11, 15):
                        lo(g0 + j, i, 12)
                    hidden(0, i)
                    gate_mul(1, i)
                    for j in range(15, 19):
                        lo(g0 + j, i, 12)
                    up_mul(1, g0 + 16, i)
                    lo(g0 + 19, i, 12)
                    for n in range(CC):
                        if n < CC - 1:
                            lo(g0 + 20 + n, i, 12)
                        add(n, g0 + 17 + n, i)
                hidden(FC - 1)
                end = g0 + 3 * KG * FC
                lo(end - 1)
                if l == 0:
                    for n in range(CC):
                        add(n, end - KG + n + 1)
                        if n in (1, 2):
                            chunk_lo(3, n - 1, R_ATTN + KT)
                        if n != 2:
                            lo(end + n - n // 3)
                else:
                    final_rows_and_norm()

            norm(2, R_FFN)
            ffn(0, G_FFN0, 0)

            norm(3, R_ATTN + KT, done=2)
            for g in (3, 4, 5, 6):
                lo(G_DQ + g)

            def latent(which, bank):
                dst = c_q if which == 0 else c_kv
                link(dve.tensor_scalar(dst[:, 1, :], ps[:, bank + 1, :], rstd[:, 1:2], None, ALU.mult))
                link(dve.tensor_tensor_reduce(out=lat_junk, in0=dst[:, 1, :], in1=dst[:, 1, :], scale=1.0,
                                              scalar=0.0, op0=ALU.mult, op1=ALU.add, accum_out=stat[:, 1:2]))
                mean_square(4 + which, LORA)
                link(inv_sqrt(rlat))
                dve.tensor_tensor(rcomb[:, :], rlat[:, :], rstd[:, :], ALU.mult).then_inc(rstd_ready, 1)
                dve.tensor_scalar(dst[:, 1, :], dst[:, 1, :], rlat[:, 1:2], None, ALU.mult).then_inc(y_dve, 1)

            def latent_lo(which, bank, gain):
                for k in range(LT):
                    if k % 2 == 0:
                        dve.wait_ge(ahi_done, 2 * FC + LT * which + k + 2)
                    dve.scalar_tensor_tensor(a_lo[:, which, k, :], ps[:, bank + k // 2, S * (k % 2):S * (k % 2) + S],
                                             vec_col[:, gain + k:gain + k + 1], hi32(a_hi[:, which, k, :]),
                                             ALU.mult, ALU.subtract).then_inc(alo_done, 1)

            dve.wait_ge(rstd_ready, RSTD[3])
            dve.tensor_copy(rstd_rows, rstd[:, :].rearrange("p (t c) -> p t c", c=1).to_broadcast([P, TT, P])
                            ).then_inc(kr_raw_done, 1)
            dve.wait_ge(group_used, G_DQ + KG)
            latent(0, 0)
            for g in (7, 8, 9, 10):
                lo(G_DQ + g)
            dve.wait_ge(group_used, G_DKV + KG)
            latent(1, 2)
            latent_lo(0, 5, R_QN)
            dve.wait_ge(kr_twice, 1)
            link(dve.tensor_copy(rope_b, ps[:, 7, 0:S]))
            dve.wait_ge(group_used, G_KR + 1)
            dve.tensor_tensor(k_raw, ps[0:ROPE, 4, 0:S], rope_b[0:ROPE, :], ALU.mult).then_inc(kr_raw_done, 1)
            latent_lo(1, 2, R_KVN)
            dve.wait_ge(kr_twice, 2)
            dve.wait_ge(rope_ready, 2)
            dve.wait_ge(kr_raw_done, 2)
            dve.wait_ge(swaps, 9)
            link(dve.tensor_tensor(rope_a, ps[:, 7, 0:S], cosT[:, :], ALU.mult))
            link(dve.tensor_tensor(rope_b, ps[:, 7, S:2 * S], sinT[:, :], ALU.mult))
            dve.tensor_tensor(krT, rope_a, rope_b, ALU.add).then_inc(kr_done, 1)
            lo(G_DQ + 11)

            def pair_project(g, h, i=None):
                lo(g + 3, i, 4)
                dve.wait_ge(group_used, val(g + 1, i, 4))
                dve.tensor_copy(q_raw, ps[:, 1, 0:S]).then_inc(q_raw_done, 1)
                dve.wait_ge(q_raw_done, val(3 * h + 1, i, 6))
                dve.tensor_tensor(rope_a, q_raw, cosT[:, :], ALU.mult).then_inc(q_raw_done, 1)
                lo(g + 4, i, 4)
                pair_queries(h, i)

            def pair_out(h, i=None):
                for a in range(2):
                    dve.wait_ge(xhi_done, val(norm_counts(4) + 2 * h + a + 1, i, 4))
                    dst, high = (x_lo[:, 2 * h + a, :], x_hi[:, 2 * h + a, :]) if i is None else \
                        (x_lo[:, bass.ds(i * 4 + 2 * h + a, 1), :].rearrange("p k s -> p (k s)"),
                         x_hi[:, bass.ds(i * 4 + 2 * h + a, 1), :].rearrange("p k s -> p (k s)"))
                    dve.tensor_tensor(dst, ps[:, 6 + a, 0:S], hi32(high), ALU.subtract).then_inc(xlo_done, 1)

            def pair_keys(g, h, i=None):
                dve.wait_ge(group_used, val(g + 2, i, 4))
                dve.tensor_copy(v_sb.rearrange("p t f -> p (t f)"), ps[:, 3, :]).then_inc(v_done, 1)

            def pair_queries(h, i=None):
                dve.wait_ge(qr_swapped, val(h + 1, i, 2))
                dve.tensor_tensor(rope_b, ps[:, 1, S:2 * S], sinT[:, :], ALU.mult).then_inc(q_raw_done, 1)
                dve.wait_ge(q_raw_done, val(3 * h + 3, i, 6))
                dve.tensor_tensor(qrT, rope_a, rope_b, ALU.add).then_inc(qr_done, 1)

            def pair_softmax(h, i=None):
                for a in range(2):
                    dve.wait_ge(scored, val(2 * h + a + 1, i, 4))
                    dve.scalar_tensor_tensor(prob[:, a, :], ps[:, 4 + a, 0:3 * P], SM_SCALE, mask,
                                             ALU.mult, ALU.add).then_inc(prob_done, 1)
                    for q, (lo_, hi_) in enumerate(((0, P), (P, 3 * P))):
                        dve.wait_ge(prob_done, val(7 * h + a + 1, i, 14))
                        dve.tensor_reduce(nmax[:, 2 * a + q:2 * a + q + 1], prob[:, a, lo_:hi_], AX.X, ALU.max,
                                          negate=True).then_inc(max_done, 1)
                dve.wait_ge(exp_done, val(4 * h + 4, i, 8))
                dve.reciprocal(erec[:, :], esum[:, :]).then_inc(prob_done, 1)
                dve.wait_ge(prob_done, val(7 * h + 3, i, 14))
                for a in range(2):
                    for q, (lo_, hi_) in enumerate(((0, P), (P, 3 * P))):
                        dve.tensor_scalar(prob[:, a, lo_:hi_], prob[:, a, lo_:hi_], erec[:, 2 * a + q:2 * a + q + 1],
                                          None, ALU.mult).then_inc(prob_done, 1)

            pair_project(G_ATT, 0)
            pair_keys(G_ATT, 0)
            pair_softmax(0)
            with dve.Fori(0, (PAIRS - 2) // 2) as i:
                for u in range(2):
                    g = G_ATT + 2 + 2 * u
                    pair_project(g, 1 + u, i)
                    pair_out(u, i)
                    pair_keys(g, 1 + u, i)
                    pair_softmax(1 + u, i)
            g = G_ATT + 2 * (PAIRS - 1)
            pair_project(g, PAIRS - 1)
            pair_out(PAIRS - 2)
            pair_keys(g, PAIRS - 1)
            pair_softmax(PAIRS - 1)
            pair_out(PAIRS - 1)

            square(G_WO)
            norm(5, R_FFN + KT)
            ffn(1, G_FFN1, 0)


        @block.tensor
        def _(pe):
            def w_rows(tensor, slot, cols=CH):
                return tensor[:, slot, 0:(GK * CH // cols) * cols].rearrange("p (k n) -> p k n", n=cols)

            def product(dst, pairs, first, last, skip=False):
                for n, (lhsT, rhs) in enumerate(pairs):
                    ins = pe.matmul(dst, lhsT, rhs, start=first and n == 0, stop=last and n == len(pairs) - 1,
                                    skip_group_check=skip)
                return ins

            def three(a_h, a_l, b_h, b_l):
                return [(a_h, b_h), (a_h, b_l), (a_l, b_h)]

            def token_group(g, i, per, j, banks, xh, xl, kt0, n_groups, x_count=None):
                wait_lo(pe, g, i, per)
                slot = g % RING
                wh, wl = w_rows(w_hi, slot), w_rows(w_lo, slot)
                for kk in range(GK):
                    if x_count is not None and kk % 2 == 0:
                        pe.wait_ge(xlo_done, x_count + kt0 + kk + 2)
                    for t in range(TT):
                        k = kt0 + kk
                        ins = product(ps[:, banks[t], :],
                                      three(xh[:, k, P * t:P * t + P], xl[:, k, P * t:P * t + P], wh[:, kk, :], wl[:, kk, :]),
                                      j == 0 and kk == 0, j == n_groups - 1 and kk == GK - 1)
                ins.then_inc(group_used, 1)

            def transposes(n, y_count=None):
                for b in range(KT // 2):
                    if n == 0 and b == 6:
                        pe.wait_ge(vec_done, 3)
                    if y_count is not None and b % 2 == 0:
                        pe.wait_ge(y_act, y_count + b // 2 + 1)
                        pe.wait_ge(y_dve, y_count + b // 2 + 1)
                    for kk in range(2):
                        for t in range(TT):
                            ins = pe.transpose(ps[:, b, S * kk + P * t:S * kk + P * t + P],
                                               ytmp[:, t, P * (2 * b + kk):P * (2 * b + kk) + P], ident[:, :])
                    ins.then_inc(x_tr, 1)

            def residual_transposes(norm, n, added):
                pe.wait_ge(out_added, added + TT * (n + 1))
                for b in range(2):
                    for kk in range(2):
                        for t in range(TT):
                            k = GK * n + 2 * b + kk
                            ins = pe.transpose(ps[:, TBANK[norm][n] + b, S * kk + P * t:S * kk + P * t + P],
                                               resid[:, t, P * k:P * k + P], ident[:, :])
                    ins.then_inc(x_tr, 1)

            pe.wait_ge(small_in, 16 * 10)
            pe.wait_ge(consts, 2)
            pe.transpose(ps[:, 6, 0:R_ALL], vec_row, ident[0:R_ALL, 0:R_ALL])
            pe.transpose(ps[:, 6, P:P + 2 * KT], bias1_row, ident[0:2 * KT, 0:2 * KT])
            for q in range(4):
                ins = pe.transpose(ps[:, 7, 4 * TAPS * q:4 * TAPS * q + 4 * TAPS], tap_row[:, q, :],
                                   ident[0:4 * TAPS, 0:4 * TAPS])
            ins.then_inc(vec_t, 1)

            pe.wait_ge(y_act, 1)
            pe.wait_ge(y_dve, 1)
            transposes(0)

            def channel_half(s, i=None):
                u = s % 2
                for j in range(KG):
                    g = G_PW1 + KG * s + j
                    wait_lo(pe, g, i, 2 * KG)
                    wh, wl = w_rows(w_hi, g % RING), w_rows(w_lo, g % RING)
                    if s == 0:
                        pe.wait_ge(xlo_done, GK * (j + 1))
                    if s >= 1 and j == 0:
                        if s == 1:
                            pe.wait_ge(xlo_done, GK * KG)
                        else:
                            pe.wait_ge(glu_done, val((CM + 1) * (s // 2 - 1) + 2 * u + 3, i, CM + 1))
                    for kk in range(GK):
                        k = GK * j + kk
                        for m in range(CM):
                            cols = slice(P * m, P * m + P)
                            ins = product(ps[:, 2 * u + m // 2, S * (m % 2):S * (m % 2) + S],
                                          [(wh[:, kk, cols], x_hi[:, k, :]), (wh[:, kk, cols], x_lo[:, k, :]),
                                           (wl[:, kk, cols], x_hi[:, k, :])],
                                          j == 0 and kk == 0 and m % 2 == 0, j == KG - 1 and kk == GK - 1, skip=True)
                    ins.then_inc(group_used, 1)

            def conv_rows(s, i=None):
                u = s % 2
                last = s == HALVES - 1
                pe.wait_ge(glu_done, val((CM + 1) * (s // 2) + 2 * u + 3, i, CM + 1))
                if s >= 2:
                    pe.wait_ge(row_done, val(TT * (s - 1), i, 2 * TT))
                for n, (mm, w) in enumerate(order_last if last else [(mm, w) for mm in range(2) for w in range(PE_TAPS)]):
                    made = 2 * PE_TAPS * s + n + 1 + (PE_TAPS_LAST - PE_TAPS if s == HALVES - 2 else 0)
                    pe.wait_ge(diag_done, val(made, i, 4 * PE_TAPS))
                    rhs = diag_last[mm][w] if last else diag[:, 2 * u + mm, w, :]
                    for t in range(TT):
                        product(ps[:, 4 + 2 * u + t, P * mm:P * mm + P],
                                [(vbuf[:, 2 * u + mm, w + P * t:w + P * t + P], rhs)], n == 0, False, skip=True)
                if last:
                    pe.wait_ge(conv_step, 1 + DVE_STEPS * s + 2 * (TAPS - PE_TAPS_LAST))
                else:
                    pe.wait_ge(conv_step, val(1 + DVE_STEPS * (s + 1), i, 2 * DVE_STEPS))
                for t in range(TT):
                    for mm in range(2):
                        ins = product(ps[:, 4 + 2 * u + t, P * mm:P * mm + P],
                                      [(acc[:, 2 * u + mm, P * t:P * t + P], ident[:, :])], False, True, skip=True)
                    ins.then_inc(conv_tr, 1)
            channel_half(0)
            channel_half(1)
            conv_rows(0)
            with pe.Fori(0, CC - 2) as i:
                channel_half(2, i)
                conv_rows(1, i)
                channel_half(3, i)
                conv_rows(2, i)
            channel_half(HALVES - 2)
            conv_rows(HALVES - 3)
            channel_half(HALVES - 1)
            conv_rows(HALVES - 2)
            conv_rows(HALVES - 1)

            pe.wait_ge(row_done, TT * HALVES)
            transposes(1, y_count=1)

            def square(g0, x_count, added):
                with pe.Fori(0, CC // 2) as i:
                    for n in range(2):
                        for j in range(KG):
                            if j == 0:
                                pe.wait_ge(out_added, val(added - 1 + n, i, 2 * TT))
                            token_group(g0 + KG * n + j, i, 2 * KG, j, (2 * n, 2 * n + 1), x_hi, x_lo, GK * j, KG,
                                        x_count=x_count)
            square(G_PW2, norm_counts(1), TT)

            def ffn(l, g0, x_count, added):
                def half(g, c0, i, part):
                    for j in range(KG):
                        if i is None and part == 0 and j == 1:
                            pe.wait_ge(xlo_done, x_count + GK)
                            residual_transposes((2, 5)[l], 3, added - TT * CC)
                        if i is None and part == 0:
                            pe.wait_ge(xlo_done, x_count + GK * (j + 1))
                        token_group(g + j, i, 12, j, (2 * part, 2 * part + 1), x_hi, x_lo, GK * j, KG)

                def hidden(c0, i=None):
                    pe.wait_ge(ff_h_done, val(4 * (FC * l + c0) + 4, i, 4))
                    for b in range(2):
                        pe.wait_ge(out_added, val(added + TT * CC * (c0 - 1) + 5 + b, i, TT * CC))
                        for kk in range(2):
                            for t in range(TT):
                                m = 2 * b + kk
                                ins = pe.transpose(ps[:, 4 + b, S * kk + P * t:S * kk + P * t + P],
                                                   ff_h[:, t, P * m:P * m + P], ident[:, :])
                        ins.then_inc(ff_tr, 1)

                def down(g, c0, i=None, after=None):
                    for n in range(CC):
                        wait_lo(pe, g + n, i, 12)
                        slot = (g + n) % RING
                        wh, wl = w_rows(w_hi, slot), w_rows(w_lo, slot)
                        for t in range(TT):
                            block_no = 2 * n + t
                            if block_no >= 2:
                                pe.wait_ge(out_added, val(added + TT * CC * c0 + block_no - 3, i, TT * CC))
                            for kk in range(LT):
                                if block_no == 0 and kk % 2 == 0:
                                    pe.wait_ge(alo_done, val(AHI[l] + 2 * c0 + kk // 2 + 1, i, 2))
                                ins = product(ps[:, 4 + block_no % 4, :],
                                              three(a_hi[:, 0, kk, P * t:P * t + P], a_lo[:, 0, kk, P * t:P * t + P],
                                                    wh[:, kk, :], wl[:, kk, :]), kk == 0, kk == LT - 1)
                        ins.then_inc(group_used, 1)
                        if after is not None:
                            after(n)

                def down_last(g, added):
                    for idx, (n, t) in enumerate(FINAL):
                        wait_lo(pe, g + n)
                        if idx < 2:
                            pe.wait_ge(alo_done, AHI[l] + 2 * FC)
                        elif idx < 4:
                            pe.wait_ge(out_added, added + idx - 3)
                        else:
                            pe.wait_ge(out_added, added + FINAL.index((n - 2, t)) + 1)
                        wh, wl = w_rows(w_hi, (g + n) % RING), w_rows(w_lo, (g + n) % RING)
                        for kk in range(LT):
                            ins = product(ps[:, 4 + (2 * n + t) % 4, :],
                                          three(a_hi[:, 0, kk, P * t:P * t + P], a_lo[:, 0, kk, P * t:P * t + P],
                                                wh[:, kk, :], wl[:, kk, :]), kk == 0, kk == LT - 1)
                        ins.then_inc(final_block, 1)

                half(g0, 0, None, 0)
                half(g0 + KG, 0, None, 1)
                with pe.Fori(0, FC - 1) as i:
                    pe.wait_ge(ff_h_done, val(4 * FC * l + 4, i, 4))
                    half(g0 + 8, 0, i, 0)
                    hidden(0, i)
                    half(g0 + 12, 0, i, 1)
                    down(g0 + 16, 0, i)
                hidden(FC - 1)

                def between(n):
                    if n == 3:
                        pe.wait_ge(xlo_done, norm_counts(3) + GK)
                    if n >= 1:
                        residual_transposes(3, n - 1, ADDED[3] - TT * CC)
                if l == 0:
                    down(g0 + 3 * KG * FC - KG, FC - 1, after=between)
                else:
                    down_last(g0 + 3 * KG * FC - KG, added + TT * CC * (FC - 1))

            def chunks_to_ffn(norm, added):
                residual_transposes(norm, 0, added)
                residual_transposes(norm, 1, added)
                pe.wait_ge(out_added, added + TT * CC)
                residual_transposes(norm, 2, added)
            chunks_to_ffn(2, TT)
            ffn(0, G_FFN0, norm_counts(2), ADDED[2])

            pe.wait_ge(xlo_done, norm_counts(3) + 2 * GK)
            for j in range(KG):
                if j == 1:
                    residual_transposes(3, 3, ADDED[3] - TT * CC)
                pe.wait_ge(xlo_done, norm_counts(3) + GK * (j + 1))
                token_group(G_DQ + j, None, 0, j, (0, 1), x_hi, x_lo, GK * j, KG)
            for j in range(KG):
                token_group(G_DKV + j, None, 0, j, (2, 3), x_hi, x_lo, GK * j, KG)

            def latent_transposes(src, bank):
                for b in range(2):
                    for kk in range(2):
                        for t in range(TT):
                            k = 2 * b + kk
                            ins = pe.transpose(ps[:, bank + b, S * kk + P * t:S * kk + P * t + P],
                                               src[:, t, P * k:P * k + P], ident[:, :])
                    ins.then_inc(lat_tr, 1)
            pe.wait_ge(y_act, 2 + CC)
            pe.wait_ge(y_dve, 2 + CC)
            latent_transposes(c_q, 5)
            pe.wait_ge(kr_raw_done, 1)
            for t in range(TT):
                ins = pe.matmul(ps[:, 7, P * t:P * t + P], rstd_rows[:, t, :], ident[:, :], start=True, stop=True)
            ins.then_inc(kr_twice, 1)
            wait_lo(pe, G_KR)
            wh, wl = w_rows(w_hi, G_KR % RING, ROPE), w_rows(w_lo, G_KR % RING, ROPE)
            for k in range(KT):
                ins = product(ps[0:ROPE, 4, 0:S], [(wh[:, k, :], x_hi[:, k, :]), (wh[:, k, :], x_lo[:, k, :]),
                                                   (wl[:, k, :], x_hi[:, k, :])], k == 0, k == KT - 1)
            ins.then_inc(group_used, 1)
            pe.wait_ge(y_act, 3 + CC)
            pe.wait_ge(y_dve, 3 + CC)
            latent_transposes(c_kv, 2)
            def pair_project(g, h, i=None):
                if h == 0 and i is None:
                    pe.wait_ge(alo_done, 2 * FC + LT)
                wait_lo(pe, g, i, 4)
                wh, wl = w_rows(w_hi, g % RING, 2 * QH), w_rows(w_lo, g % RING, 2 * QH)
                for a in range(2):
                    for k in range(LT):
                        cols = slice(NOPE * a, NOPE * a + NOPE)
                        product(ps[:, 0, S * a:S * a + S],
                                [(wh[:, k, cols], a_hi[:, 0, k, :]), (wh[:, k, cols], a_lo[:, 0, k, :]),
                                 (wl[:, k, cols], a_hi[:, 0, k, :])], k == 0, k == LT - 1)
                for k in range(LT):
                    cols = slice(2 * NOPE, 2 * QH)
                    ins = product(ps[:, 1, 0:S], [(wh[:, k, cols], a_hi[:, 0, k, :]), (wh[:, k, cols], a_lo[:, 0, k, :]),
                                                  (wl[:, k, cols], a_hi[:, 0, k, :])], k == 0, k == LT - 1)
                ins.then_inc(group_used, 1)
                g += 1
                if h == 0 and i is None:
                    pe.wait_ge(kr_raw_done, 2)
                    pe.wait_ge(swaps, 6)
                    pe.matmul(ps[:, 7, 0:S], twice, k_raw, start=True, stop=True)
                    pe.matmul(ps[:, 7, S:2 * S], swap_twice, k_raw, start=True, stop=True).then_inc(kr_twice, 1)
                    pe.wait_ge(alo_done, 2 * FC + 2 * LT)
                wait_lo(pe, g, i, 4)
                wh, wl = w_rows(w_hi, g % RING), w_rows(w_lo, g % RING)
                for a in range(2):
                    for k in range(LT):
                        cols = slice(KVH * a, KVH * a + NOPE)
                        product(ps[:, 2, S * a:S * a + S],
                                [(wh[:, k, cols], a_hi[:, 1, k, :]), (wh[:, k, cols], a_lo[:, 1, k, :]),
                                 (wl[:, k, cols], a_hi[:, 1, k, :])], k == 0, k == LT - 1)
                if not (h == 0 and i is None):
                    pe.wait_ge(v_done, val(h, i, 2))
                for t in range(TT):
                    for k in range(LT):
                        def values(w):
                            return w[:, k, :].rearrange("p (a n) -> p a n", a=2)[:, :, NOPE:KVH]
                        toks = slice(P * t, P * t + P)
                        ins = product(ps[:, 3, S * t:S * t + S].rearrange("p (a n) -> p a n", a=2),
                                      three(a_hi[:, 1, k, toks], a_lo[:, 1, k, toks], values(wh), values(wl)),
                                      k == 0, k == LT - 1)
                ins.then_inc(group_used, 1)

            def pair_out(h, i=None):
                pe.wait_ge(prob_done, val(7 * h + 7, i, 14))
                for a in range(2):
                    if not (h == 0 and i is None):
                        base = norm_counts(4) + 2 * h - 2 + a + 1
                        pe.wait_ge(xlo_done, val(base, i, 4))
                    for s in range(3):
                        ins = pe.transpose(ps[:, 6 + a, P * s:P * s + P], prob[:, a, KEYS[s]], ident[:, :])
                    ins.then_inc(prob_tr, 1)
                for a in range(2):
                    pe.wait_ge(pT_done, val(2 * h + a + 1, i, 4))
                    pe.matmul(ps[:, 6 + a, 0:S], v_sb[:, 0, VD * a:VD * a + VD], pT[:, a, 0:S], start=True, stop=False)
                    pe.matmul(ps[:, 6 + a, P:S], v_sb[:, 1, VD * a:VD * a + VD], pT[:, a, S:S + P], start=False,
                              stop=True).then_inc(pv_done, 1)

            def pair_queries(h, i=None):
                pe.wait_ge(q_raw_done, val(3 * h + 1, i, 6))
                pe.matmul(ps[:, 1, S:2 * S], swap, q_raw, start=True, stop=True).then_inc(qr_swapped, 1)

            def pair_scores(h, i=None):
                pe.wait_ge(qk_done, val(2 * h + 2, i, 4))
                pe.wait_ge(qr_done, val(h + 1, i, 2))
                if h == 0 and i is None:
                    pe.wait_ge(kr_done, 1)
                for a in range(2):
                    r = slice(ROPE * a, ROPE * a + ROPE)
                    for q, cols in enumerate((slice(0, P), slice(P, 3 * P))):
                        toks = slice(P * q, P * q + P)
                        keys = P * (q + 1)
                        pe.matmul(ps[:, 4 + a, cols], qT[:, a, toks], kT[:, a, 0:keys], start=True, stop=False)
                        ins = pe.matmul(ps[:, 4 + a, cols], qrT[r, toks], krT[r, 0:keys], start=False, stop=True)
                    ins.then_inc(scored, 1)

            KEYS = (slice(0, P), slice(P, 2 * P), slice(2 * P, 3 * P))
            pair_project(G_ATT, 0)
            pair_queries(0)
            pair_scores(0)
            with pe.Fori(0, (PAIRS - 2) // 2) as i:
                for u in range(2):
                    pair_project(G_ATT + 2 + 2 * u, 1 + u, i)
                    pair_queries(1 + u, i)
                    pair_out(u, i)
                    pair_scores(1 + u, i)
            pair_project(G_ATT + 2 * (PAIRS - 1), PAIRS - 1)
            pair_queries(PAIRS - 1)
            pair_out(PAIRS - 2)
            pair_scores(PAIRS - 1)
            pair_out(PAIRS - 1)

            square(G_WO, norm_counts(4), ADDED[3])
            chunks_to_ffn(5, ADDED[3])
            ffn(1, G_FFN1, norm_counts(5), ADDED[5])


ADDED = {2: TT + TT * CC, 3: TT + TT * CC * (1 + FC), 5: TT + TT * CC * (2 + FC), 6: TT + TT * CC * (2 + 2 * FC)}
XT = {0: 0, 1: KT // 2, 2: KT, 3: 3 * KT // 2, 5: 2 * KT}
TBANK = {0: (0, 2, 4, 6), 2: (4, 6, 2, 4), 3: (2, 0, 2, 4), 5: (4, 6, 2, 4)}
RSTD = {0: 1, 2: 3, 3: 4, 5: 7, 6: 8}
SQ = {0: 1, 2: 2, 3: 3, 5: 6}
AHI = {0: 0, 1: 2 * FC + 2 * LT}

TILE_END = ((CC - 1, 0), (CC - 1, 1))
FINAL = [(0, 0), (0, 1), (1, 0), (1, 1), (2, 0), (3, 0), (2, 1), (3, 1)]

_INS = ['x', 'positions', 'attn_norm_g', 'ffn_norm_g', 'final_norm_g', 'conv_w_pw1', 'conv_b_pw1', 'conv_w_dw',
        'conv_b_dw', 'conv_ln_g', 'conv_ln_b', 'conv_w_pw2', 'conv_b_pw2', 'mla_w_dq', 'mla_q_norm_g', 'mla_w_uq',
        'mla_w_dkv', 'mla_kv_norm_g', 'mla_w_ukv', 'mla_w_o', 'ffn_w_gate', 'ffn_w_up', 'ffn_w_down']


def kernel(**inputs):
    import concourse.bacc as _bacc
    from concourse.bass_utils import run_bass_kernel_spmd as _run

    nc = _bacc.Bacc("TRN2", target_bir_lowering=False, num_devices=1)
    arrays, args = {}, []
    named = [(name, np.ascontiguousarray(inputs[name])) for name in _INS]
    power = np.arange(0, ROPE, 2, dtype=np.float32) / np.float32(ROPE)
    freqs = np.float32(1) / (10000.0 ** power.astype(np.float64)).astype(np.float32)
    named.append(("inv_freq", np.tile(freqs, P // len(freqs)).reshape(P, 1)))
    for name, a in named:
        arrays[f"in_{name}_dram"] = a
        args.append(nc.dram_tensor(f"in_{name}_dram", a.shape, mybir.dt.from_np(a.dtype), kind="ExternalInput").ap())
    args.append(nc.dram_tensor("out_0_dram", (1, S, D), F32, kind="ExternalOutput").ap())
    encoder(nc, *args)
    r = _run(nc, [arrays], core_ids=[0])
    return r.results[0]["out_0_dram"]
```
